# Optimizing a Trainium2 kernel written in Bass

```python
import math
import jax, jax.numpy as jnp
from jax import lax
import numpy as np

D_MODEL = 1024
BATCH = 1
SEQ = 256
DEPTH = 2

CTX_LEN = 256
GRID_W = 64
N_BRANCH = 3
BRANCH_WIDTH = D_MODEL // 2
GDN_HEADS = 4
GDN_DK = 128
GDN_DV = 128
GDN_CHUNK = 64
SCONV_WIDTH = BRANCH_WIDTH
ATT_HEADS = 8
ATT_KV_HEADS = 2
ATT_GROUP = ATT_HEADS // ATT_KV_HEADS
ATT_HD = 64
ATT_BLOCK = 128
ROPE_THETA = 10000.0
ROPE_AXIS_PAIRS = ATT_HD // 4
PEER_HEADS = 8
PEER_DK = 128
PEER_NKEYS = 128
PEER_EXPERTS = PEER_NKEYS * PEER_NKEYS
PEER_TOPK = 16
PEER_CHUNK = 128
NORM_EPS = 1e-6
PROJ_SIZES = (
    2 * GDN_HEADS * GDN_DK + GDN_HEADS * GDN_DV,
    GDN_HEADS * GDN_DV,
    4 * GDN_HEADS,
    3 * SCONV_WIDTH,
    ATT_HEADS * ATT_HD,
    2 * ATT_KV_HEADS * ATT_HD,
    N_BRANCH * D_MODEL,
)
D_IN = sum(PROJ_SIZES)

kernel_name = 'hybrid_diffusion_block'

def _rmsnorm(x, w):
    xf = x.astype(jnp.float32)
    y = xf * lax.rsqrt(jnp.mean(xf * xf, axis=-1, keepdims=True) + NORM_EPS)
    return (y * w.astype(jnp.float32)).astype(x.dtype)

def _l2norm(x):
    return x * lax.rsqrt(jnp.sum(x * x, axis=-1, keepdims=True) + NORM_EPS)

def _dwconv3(x, w):
    return lax.conv_general_dilated(
        x, w[:, None, :].astype(x.dtype), window_strides=(1,), padding=((1, 1),),
        dimension_numbers=('NWC', 'WIO', 'NWC'), feature_group_count=x.shape[-1])

def _split_proj(p):
    out, start = [], 0
    for size in PROJ_SIZES:
        out.append(p[..., start:start + size])
        start += size
    return out

def _gdn_prep(qkv, ab, conv_w, a_log, dt_bias):
    b, t, _ = qkv.shape
    qkv = jax.nn.silu(_dwconv3(qkv, conv_w)).astype(jnp.float32)
    q = qkv[..., :GDN_HEADS * GDN_DK].reshape(b, t, GDN_HEADS, GDN_DK)
    k = qkv[..., GDN_HEADS * GDN_DK:2 * GDN_HEADS * GDN_DK].reshape(b, t, GDN_HEADS, GDN_DK)
    v = qkv[..., 2 * GDN_HEADS * GDN_DK:].reshape(b, t, GDN_HEADS, GDN_DV)
    q = _l2norm(q) * (GDN_DK ** -0.5)
    k = _l2norm(k)
    ab = ab.astype(jnp.float32).reshape(b, t, 2, 2, GDN_HEADS)
    g = -jnp.exp(a_log.astype(jnp.float32)) * jax.nn.softplus(ab[:, :, 0] + dt_bias.astype(jnp.float32))
    beta = jax.nn.sigmoid(ab[:, :, 1])
    to_bh = lambda z: jnp.transpose(z, (0, 2, 1, 3))
    to_dbh = lambda z: jnp.transpose(z, (2, 0, 3, 1))
    return to_bh(q), to_bh(k), to_bh(v), to_dbh(g), to_dbh(beta)

def _chunk_gated_delta(q, k, v, beta, g, s0, emit):
    b, h, t, dk = q.shape
    dv = v.shape[-1]
    n = t // GDN_CHUNK
    q = q.reshape(b, h, n, GDN_CHUNK, dk)
    k = k.reshape(b, h, n, GDN_CHUNK, dk)
    v = v.reshape(b, h, n, GDN_CHUNK, dv)
    beta = beta.reshape(b, h, n, GDN_CHUNK)
    gc = jnp.cumsum(g.reshape(b, h, n, GDN_CHUNK), axis=-1)
    pos = jnp.arange(GDN_CHUNK)
    incl = pos[:, None] >= pos[None, :]
    strict = pos[:, None] > pos[None, :]
    diff = gc[..., :, None] - gc[..., None, :]
    ldec = jnp.where(incl, jnp.exp(jnp.where(incl, diff, 0.0)), 0.0)
    kb = k * beta[..., None]
    a = jnp.where(strict, jnp.einsum('bhnid,bhnjd->bhnij', kb, k) * ldec, 0.0)
    rhs = jnp.concatenate([v * beta[..., None], kb * jnp.exp(gc)[..., None]], axis=-1)
    sol = lax.linalg.triangular_solve(a + jnp.eye(GDN_CHUNK, dtype=a.dtype), rhs,
                                      left_side=True, lower=True, unit_diagonal=True)
    g_last = gc[..., -1]
    k_dec = k * jnp.exp(g_last[..., None] - gc)[..., None]
    xs = [sol[..., :dv], sol[..., dv:], k_dec, g_last]
    if emit:
        qk = jnp.einsum('bhnid,bhnjd->bhnij', q, k) * ldec
        xs = xs + [qk, q * jnp.exp(gc)[..., None]]
    xs = tuple(jnp.moveaxis(z, 2, 0) for z in xs)

    def step(s, inp):
        u_n, w_n, kd_n, gl_n = inp[:4]
        v_new = u_n - jnp.einsum('bhik,bhkv->bhiv', w_n, s)
        s_next = s * jnp.exp(gl_n)[..., None, None] + jnp.einsum('bhik,bhiv->bhkv', kd_n, v_new)
        if not emit:
            return s_next, None
        qk_n, qd_n = inp[4:]
        o_n = jnp.einsum('bhik,bhkv->bhiv', qd_n, s) + jnp.einsum('bhij,bhjv->bhiv', qk_n, v_new)
        return s_next, o_n

    s_fin, o = lax.scan(step, s0, xs)
    if not emit:
        return None, s_fin
    return jnp.moveaxis(o, 0, 2).reshape(b, h, t, dv), s_fin

def _gated_out(o, z, norm_w):
    b, h, t, dv = o.shape
    o = jnp.transpose(o, (0, 2, 1, 3))
    o = o * lax.rsqrt(jnp.mean(o * o, axis=-1, keepdims=True) + NORM_EPS) * norm_w.astype(jnp.float32)
    zg = jax.nn.silu(z.astype(jnp.float32)).reshape(b, t, h, dv)
    return (o * zg).reshape(b, t, h * dv).astype(z.dtype)

def _gdn_branch(qkv_l, z_l, ab_l, qkv_c, z_c, ab_c, conv_w, a_log, dt_bias, norm_w, emit_ctx):
    ql, kl, vl, gl, bl = _gdn_prep(qkv_l, ab_l, conv_w, a_log, dt_bias)
    qc, kc, vc, gcx, bc = _gdn_prep(qkv_c, ab_c, conv_w, a_log, dt_bias)
    s0 = jnp.zeros((ql.shape[0], GDN_HEADS, GDN_DK, GDN_DV), jnp.float32)
    rev = lambda z: jnp.flip(z, axis=2)
    oc_f, sc_f = _chunk_gated_delta(qc, kc, vc, bc[0], gcx[0], s0, emit_ctx)
    ol_f, _ = _chunk_gated_delta(ql, kl, vl, bl[0], gl[0], sc_f, True)
    oc_b, sc_b = _chunk_gated_delta(rev(qc), rev(kc), rev(vc), rev(bc[1]), rev(gcx[1]), s0, emit_ctx)
    ol_b, _ = _chunk_gated_delta(rev(ql), rev(kl), rev(vl), rev(bl[1]), rev(gl[1]), sc_b, True)
    o_l = _gated_out(ol_f + rev(ol_b), z_l, norm_w)
    if not emit_ctx:
        return o_l, None
    return o_l, _gated_out(oc_f + rev(oc_b), z_c, norm_w)

def _shortconv_branch(p, conv_w):
    bg, cg, xin = jnp.split(p, 3, axis=-1)
    return bg * _dwconv3(cg * xin, conv_w)

def _axial_rope(x, row, col):
    freqs = ROPE_THETA ** (-jnp.arange(ROPE_AXIS_PAIRS, dtype=jnp.float32) / ROPE_AXIS_PAIRS)
    ang = jnp.stack([row[:, None] * freqs, col[:, None] * freqs], axis=1)
    shape = (1, x.shape[1]) + (1,) * (x.ndim - 3) + (2, ROPE_AXIS_PAIRS)
    cos = jnp.cos(ang).reshape(shape).astype(x.dtype)
    sin = jnp.sin(ang).reshape(shape).astype(x.dtype)
    xr = x.reshape(x.shape[:-1] + (2, 2, ROPE_AXIS_PAIRS))
    x1, x2 = xr[..., 0, :], xr[..., 1, :]
    return jnp.stack([x1 * cos - x2 * sin, x2 * cos + x1 * sin], axis=-2).reshape(x.shape)

def _q_heads(q, w):
    b, n = q.shape[:2]
    return _rmsnorm(q.reshape(b, n, ATT_KV_HEADS, ATT_GROUP, ATT_HD), w)

def _kv_heads(kv, w):
    b, n = kv.shape[:2]
    k, v = jnp.split(kv, 2, axis=-1)
    k = _rmsnorm(k.reshape(b, n, ATT_KV_HEADS, ATT_HD), w)
    return k, v.reshape(b, n, ATT_KV_HEADS, ATT_HD)

def _attend(q, keys, vals):
    s = jnp.einsum('bqhgd,bkhd->bhgqk', q, keys).astype(jnp.float32) * (ATT_HD ** -0.5)
    p = jax.nn.softmax(s, axis=-1).astype(vals.dtype)
    return jnp.einsum('bhgqk,bkhd->bqhgd', p, vals)

def _attention_branch(q_l, kv_l, q_c, kv_c, q_norm_w, k_norm_w, row, col, emit_ctx):
    b, t, _ = q_l.shape
    ql = _axial_rope(_q_heads(q_l, q_norm_w), row, col)
    kl, vl = _kv_heads(kv_l, k_norm_w)
    kl = _axial_rope(kl, row, col)
    kc, vc = _kv_heads(kv_c, k_norm_w)
    keys = jnp.concatenate([kl, kc], axis=1)
    vals = jnp.concatenate([vl, vc], axis=1)
    nb = t // ATT_BLOCK
    qb = jnp.moveaxis(ql.reshape(b, nb, ATT_BLOCK, ATT_KV_HEADS, ATT_GROUP, ATT_HD), 1, 0)
    ol = lax.map(lambda qblk: _attend(qblk, keys, vals), qb)
    ol = jnp.moveaxis(ol, 0, 1).reshape(b, t, ATT_HEADS * ATT_HD)
    if not emit_ctx:
        return ol, None
    qc = _q_heads(q_c, q_norm_w)
    oc = _attend(qc, kc, vc).reshape(b, kv_c.shape[1], ATT_HEADS * ATT_HD)
    return ol, oc

def _merge(branches, gates, w_branch, w_out):
    b, t = branches.shape[:2]
    g = jax.nn.sigmoid(gates.reshape(b, t, N_BRANCH, D_MODEL))
    mixed = jnp.einsum('btnw,nwd,btnd->btd', branches, w_branch, g)
    return mixed @ w_out

def _token_mixers(u, uc, row, col, w_in, conv_a_w, a_log, dt_bias, gdn_norm_w, conv_b_w,
                  q_norm_w, k_norm_w, w_branch, w_out, emit_ctx):
    pl = _split_proj(u @ w_in)
    pc = _split_proj(uc @ w_in)
    oa_l, oa_c = _gdn_branch(pl[0], pl[1], pl[2], pc[0], pc[1], pc[2],
                             conv_a_w, a_log, dt_bias, gdn_norm_w, emit_ctx)
    ob_l = _shortconv_branch(pl[3], conv_b_w)
    oc_l, oc_c = _attention_branch(pl[4], pl[5], pc[4], pc[5], q_norm_w, k_norm_w, row, col, emit_ctx)
    y_l = _merge(jnp.stack([oa_l, ob_l, oc_l], axis=2), pl[6], w_branch, w_out)
    if not emit_ctx:
        return y_l, None
    ob_c = _shortconv_branch(pc[3], conv_b_w)
    y_c = _merge(jnp.stack([oa_c, ob_c, oc_c], axis=2), pc[6], w_branch, w_out)
    return y_l, y_c

def _peer(u, w_query, sub_keys, expert_u, expert_v):
    b, t, d = u.shape
    chunks = u.reshape(-1, PEER_CHUNK, d)

    def chunk_fn(xc):
        qh = (xc @ w_query).reshape(PEER_CHUNK, PEER_HEADS, 2, PEER_DK // 2)
        s = jnp.einsum('chpk,hpnk->chpn', qh, sub_keys).astype(jnp.float32)
        top_s, top_i = lax.top_k(s, PEER_TOPK)
        cand_s = (top_s[:, :, 0, :, None] + top_s[:, :, 1, None, :]).reshape(PEER_CHUNK, PEER_HEADS, PEER_TOPK * PEER_TOPK)
        cand_i = (top_i[:, :, 0, :, None] * PEER_NKEYS + top_i[:, :, 1, None, :]).reshape(PEER_CHUNK, PEER_HEADS, PEER_TOPK * PEER_TOPK)
        best_s, best_j = lax.top_k(cand_s, PEER_TOPK)
        idx = jnp.take_along_axis(cand_i, best_j, axis=-1)
        gate = jax.nn.softmax(best_s, axis=-1).astype(xc.dtype)
        u_sel = jnp.take(expert_u, idx, axis=0)
        act = jax.nn.gelu(jnp.einsum('chkd,cd->chk', u_sel, xc), approximate=False)
        v_sel = jnp.take(expert_v, idx, axis=0)
        return jnp.einsum('chk,chkd->cd', gate * act, v_sel)

    return lax.map(chunk_fn, chunks).reshape(b, t, d)

def setup_inputs(seed: int = 0) -> dict:
    key = jax.random.key(seed)
    ks = jax.random.split(key, 26)
    L, D = DEPTH, D_MODEL
    nrm = lambda k, shape, s: jax.random.normal(k, shape, jnp.float32) * s
    dt = jnp.exp(jax.random.uniform(ks[8], (L, 2, GDN_HEADS), jnp.float32, math.log(1e-3), math.log(1e-1)))
    return {
        'x': nrm(ks[0], (BATCH, SEQ, D), 1.0),
        'c': nrm(ks[1], (BATCH, D), 1.0),
        'ctx': nrm(ks[2], (BATCH, CTX_LEN, D), 1.0),
        'c_ctx': nrm(ks[3], (D,), 1.0),
        'w_mod': nrm(ks[4], (L, D, 6 * D), 0.5 * D ** -0.5),
        'b_mod': nrm(ks[5], (L, 6 * D), 0.01),
        'norm1_w': 1.0 + nrm(ks[6], (L, D), 0.02),
        'w_in': nrm(ks[7], (L, D, D_IN), D ** -0.5),
        'conv_a_w': nrm(ks[9], (L, 3, PROJ_SIZES[0]), 0.5),
        'a_log': jnp.log(jax.random.uniform(ks[10], (L, 2, GDN_HEADS), jnp.float32, 1.0, 16.0)),
        'dt_bias': dt + jnp.log(-jnp.expm1(-dt)),
        'gdn_norm_w': 1.0 + nrm(ks[11], (L, GDN_DV), 0.02),
        'conv_b_w': nrm(ks[12], (L, 3, SCONV_WIDTH), 0.5),
        'q_norm_w': 1.0 + nrm(ks[13], (L, ATT_HD), 0.02),
        'k_norm_w': 1.0 + nrm(ks[14], (L, ATT_HD), 0.02),
        'w_branch': nrm(ks[15], (L, N_BRANCH, BRANCH_WIDTH, D), BRANCH_WIDTH ** -0.5),
        'w_out': nrm(ks[16], (L, D, D), D ** -0.5),
        'norm2_w': 1.0 + nrm(ks[17], (L, D), 0.02),
        'w_query': nrm(ks[18], (L, D, PEER_HEADS * PEER_DK), D ** -0.5),
        'sub_keys': nrm(ks[19], (L, PEER_HEADS, 2, PEER_NKEYS, PEER_DK // 2), (PEER_DK // 2) ** -0.5),
        'expert_u': nrm(ks[20], (L, PEER_EXPERTS, D), D ** -0.5),
        'expert_v': nrm(ks[21], (L, PEER_EXPERTS, D), PEER_HEADS ** -0.5),
        'final_norm_w': 1.0 + nrm(ks[22], (D,), 0.02),
    }

def reference(x, c, ctx, c_ctx, w_mod, b_mod, norm1_w, w_in, conv_a_w, a_log, dt_bias, gdn_norm_w,
              conv_b_w, q_norm_w, k_norm_w, w_branch, w_out, norm2_w, w_query, sub_keys,
              expert_u, expert_v, final_norm_w):
    seq = x.shape[1]
    n_rows = seq // GRID_W
    row = jnp.repeat(jnp.arange(n_rows, dtype=jnp.float32), GRID_W)
    col = jnp.tile(jnp.arange(GRID_W, dtype=jnp.float32), n_rows)
    h, hc = x, ctx
    for layer in range(DEPTH):
        last = layer == DEPTH - 1
        mod = (jax.nn.silu(c) @ w_mod[layer] + b_mod[layer])[:, None, :]
        mod_c = jax.nn.silu(c_ctx) @ w_mod[layer] + b_mod[layer]
        sh1, sc1, g1, sh2, sc2, g2 = jnp.split(mod, 6, axis=-1)
        csh1, csc1, cg1, csh2, csc2, cg2 = jnp.split(mod_c, 6, axis=-1)
        u = _rmsnorm(h, norm1_w[layer]) * (1 + sc1) + sh1
        uc = _rmsnorm(hc, norm1_w[layer]) * (1 + csc1) + csh1
        y, yc = _token_mixers(u, uc, row, col, w_in[layer], conv_a_w[layer], a_log[layer], dt_bias[layer],
                              gdn_norm_w[layer], conv_b_w[layer], q_norm_w[layer], k_norm_w[layer],
                              w_branch[layer], w_out[layer], not last)
        h = h + g1 * y
        h = h + g2 * _peer(_rmsnorm(h, norm2_w[layer]) * (1 + sc2) + sh2,
                           w_query[layer], sub_keys[layer], expert_u[layer], expert_v[layer])
        if not last:
            hc = hc + cg1 * yc
            hc = hc + cg2 * _peer(_rmsnorm(hc, norm2_w[layer]) * (1 + csc2) + csh2,
                                  w_query[layer], sub_keys[layer], expert_u[layer], expert_v[layer])
    return _rmsnorm(h, final_norm_w)


_drawn_inputs = setup_inputs


def setup_inputs(seed=0):
    import zlib

    import numpy as np

    out = dict(_drawn_inputs(seed))
    spreads = {}
    factors = {'b_mod': 3.365,
     'norm1_w': 4.269,
     'gdn_norm_w': 38.71,
     'q_norm_w': 34.284,
     'k_norm_w': 31.016,
     'norm2_w': 34.928,
     'final_norm_w': 7.939}
    for name, (base, spread) in spreads.items():
        noise = np.random.default_rng([zlib.crc32(name.encode()), seed]).standard_normal(out[name].shape)
        drawn = base * np.exp(spread * noise) if base else spread * noise
        out[name] = __import__('jax').numpy.asarray(drawn.astype(out[name].dtype))
    for name, factor in factors.items():
        out[name] = (out[name] * factor).astype(out[name].dtype)
    return out
```

```python
from contextlib import ExitStack

import numpy as np

import concourse.bass as bass
from concourse import mybir

F32 = mybir.dt.float32
U32 = mybir.dt.uint32
ALU = mybir.AluOpType
ACT = mybir.ActivationFunctionType
AX = mybir.AxisListType

P = 128
D = 1024
KD = D // P
T = 256
NT = T // P
CHUNK = 64
HEADS = 4
AHEADS, KVHEADS, HD = 8, 2, 64
PHEADS, TOPK, NKEYS = 8, 16, 128
EXPERTS = NKEYS * NKEYS
SLOTS = PHEADS * TOPK
EPS = 1e-6
NEG = -3.0e38
PASSES = [(0, 0, True), (0, 1, True), (1, 0, False), (1, 1, True)]
ALL = range(len(PASSES))

COL_QKV, COL_Z, COL_AB, COL_SC, COL_GATE = 0, 1536, 2048, 2064, 4368
COL_KV = COL_GATE - 256
T_QKV, T_Z, T_BG, T_CG, T_XIN, T_AQ, T_AK = 0, 12, 16, 20, 24, 28, 32
T_OSUM, T_KTOK, T_VTOK = 0, 4, 8
T_MIX = 0
T_SKRAW, T_SKT = 8, 12
T_OB, T_OC, T_OA = T_BG, T_CG, T_XIN
NPT = 34
V_N1, V_N2, V_BMOD, V_CA, V_CB, V_GN, V_QN, V_KN = 0, 8, 16, 64, 100, 112, 113, 114
NV = 115
NAMES = ["ident", "ones", "blk64", "rot", "dup0", "dup1", "tri0", "tri1", "str0", "str1", "chunk",
         "lv0", "lv1", "lv2", "lv3", "lv4", "lv5"]
C_AT = {n: i * P for i, n in enumerate(NAMES)}
C_COS = len(NAMES) * P
C_SIN = C_COS + T
C_IOTA = C_SIN + T
NC_ = C_IOTA + TOPK

RING = 4
BLOCKS = SLOTS // RING
NBK = 6


def constant_table():
    p, f = np.arange(P)[:, None], np.arange(P)[None, :]
    same = p // CHUNK == f // CHUNK
    m = {"ident": p == f, "ones": p + f >= 0, "blk64": p // HD == f // HD,
         "tri0": same & (p <= f), "tri1": same & (p >= f), "str0": same & (p > f), "str1": same & (p < f),
         "chunk": same}
    for lv in range(6):
        b = 1 << lv
        m[f"lv{lv}"] = (p // (2 * b) == f // (2 * b)) & (p // b != f // b)
    for v in range(KVHEADS):
        m[f"dup{v}"] = p == f % HD + HD * v
    m["rot"] = np.where((f // 16) % 2 == 0, -1.0 * (p == f + 16), 1.0 * (p == f - 16))
    t = np.arange(T)
    freq = np.float32(10000.0) ** (-np.arange(16, dtype=np.float32) / 16)
    ch = np.arange(P) % HD
    pos = np.where((ch // 32)[:, None] == 0, (t // 64)[None, :], (t % 64)[None, :]).astype(np.float32)
    ang = pos * freq[ch % 16][:, None]
    cols = [m[n].astype(np.float32) for n in NAMES] + [np.cos(ang), np.sin(ang),
                                                      np.tile(np.arange(TOPK, dtype=np.float32), (P, 1))]
    return np.ascontiguousarray(np.concatenate(cols, 1).astype(np.float32))


SOLVE = [("x", 0)] + [(k, lv) for lv in range(1, 5) for k in "xut"] + [("x", 5), ("u", 5)]
ATT = [("s", 0)] + [j for i in range(NT * AHEADS)
                    for j in ([("s", i + 1)] if i + 1 < NT * AHEADS else []) + [("p", i), ("o", i)]]


def direction(d):
    return [(f"decay{d}", (2, 2, 2, 2)), (f"gram{d}", (2, 2, 2, 2)), (f"qk{d}", (2, 2, 0, 2)),
            (f"solve{d}", (2 * len(SOLVE),) * 4), (f"rhs{d}", (4, 4, 4, 4)), (f"scan{d}", (12, 12, 8, 12))]


PRODUCTS = [("x_in", (8, 0, 0, 0)), ("cond", (1, 0, 0, 0)), ("vecs", (1, 0, 1, 0)), ("rms1", (1, 1, 1, 1)),
            ("ab", (1, 1, 1, 1)), ("cum", (1, 1, 1, 1)), ("l2", (4, 4, 2, 4)), ("tok", (4, 4, 4, 4)),
            *direction(0), *direction(1), ("gout", (2, 2, 0, 2)), ("an", (3, 3, 1, 3)), ("rope", (0, 3, 0, 3)),
            ("dup", (1, 1, 1, 1)), ("vtok", (1, 1, 1, 1)), ("att", (len(ATT), len(ATT), 0, len(ATT))),
            ("rms2", (1, 1, 0, 1)), ("u2t", (4, 4, 0, 4)), ("skt", (2, 2, 0, 2)), ("keys", (8, 8, 0, 8)),
            ("back", (4, 4, 0, 4)), ("fin", (0, 0, 0, 1)), ("out", (0, 0, 0, 4))]
ROOTS = [(n, dict(PRODUCTS)[n]) for n in ("rms1", "l2", "gout", "an", "rms2", "fin")]
WEIGHTS = [("mod", (24, 0, 24, 0)), ("qkvz", (8, 8, 4, 8)), ("rest", (9, 9, 1, 9)), ("merge", (24, 24, 0, 24)),
           ("out", (4, 4, 0, 4)), ("query", (4, 4, 0, 4))]


def before(series, stage, a, i=0):
    names = [n for n, _ in series]
    k = dict(series)
    assert i < k[stage][a], (stage, a, i)
    return sum(sum(c[:a]) for _, c in series) + sum(k[n][a] for n in names[:names.index(stage)]) + i


PEER_TILES = [(a, t) for a in ALL if PASSES[a][2] for t in range(NT)]


def build(nc, inp, out):
    with ExitStack() as ctx:
        def sb(name, shape, dt=F32):
            return ctx.enter_context(nc.sbuf_tensor(name, shape, dt))

        sems = {}

        def sem(name):
            if name not in sems:
                sems[name] = ctx.enter_context(nc.semaphore("s_" + name))
            return sems[name]

        cst = sb("cst", [P, NC_])
        H = sb("H", [P, 2, KD, T])
        U = sb("U", [P, KD, T])
        W = sb("W", [P, 2, KD * 256])
        PT = sb("PT", [P, NPT * T])
        QC = sb("QC", [P, 12, T])
        S = sb("S", [P, 2, HEADS, P])
        VN = sb("VN", [P, 2, HEADS, P])
        KDUP = sb("KDUP", [P, KVHEADS, 2 * T])
        VV = sb("VV", [P, 2 * NT, P])
        F = sb("F", [P, 10240])
        ROWU = sb("ROWU", [P, RING, D])
        ROWV = sb("ROWV", [P, RING, D])
        U2 = sb("U2", [P, NT, D])
        ACC = sb("ACC", [P, D])
        IDX = sb("IDX", [P, NT, SLOTS], U32)
        IXC = sb("IXC", [P, 2, RING], U32)
        GATE = sb("GATE", [P, NT, SLOTS])
        DOT = sb("DOT", [P, SLOTS])
        GEL = sb("GEL", [P, RING])
        COEF = sb("COEF", [P, RING])
        VROW = sb("VROW", [NV, P])
        VEC = sb("VEC", [P, NV])
        MOD = sb("MOD", [P, 48, 2])
        A12 = sb("A12", [P, 2, KD, 2])
        CROW = sb("CROW", [24, P])
        CVEC = sb("CVEC", [P, 24])
        WAB = sb("WAB", [P, KD, 16])
        ADT = sb("ADT", [P, 2, 8])
        AB = sb("AB", [P, NT, 16])
        GB = sb("GB", [P, NT, 16])
        GC = sb("GC", [P, NT, 16])
        EGC = sb("EGC", [P, NT, 16])
        BEG = sb("BEG", [P, NT, 8])
        TMPC = sb("TMPC", [P, NT, 16])
        DEC = sb("DEC", [P, NT, HEADS, 2])
        SM = sb("SM", [P, 2, 4])
        TOPV = sb("TOPV", [P, 16, TOPK])
        TOPI = sb("TOPI", [P, 16, TOPK], U32)
        BV = sb("BV", [P, PHEADS, TOPK])
        BJ = sb("BJ", [P, 3, PHEADS, TOPK], U32)
        PHS = sb("PHS", [P, 2, PHEADS])
        bank = [ctx.enter_context(nc.psum_tensor(f"bank{i}", [P, 512], F32)) for i in range(NBK)]
        wbank = [ctx.enter_context(nc.psum_tensor(f"wbank{i}", [P, 512], F32)) for i in range(2)]

        def c(name):
            return cst[:, C_AT[name]:C_AT[name] + P]

        def pt(t, n=1):
            return PT[:, t * T:(t + n) * T]

        def pt3(t, n, w=T):
            return PT[:, t * T:(t + n) * T].rearrange("p (a b) -> p a b", b=w)

        def f3(lo, n, w):
            return F[:, lo:lo + n * w].rearrange("p (a b) -> p a b", b=w)

        FA, FQ, FT, FU, FX, FW, FK, FD, FVB, FKB = [F[:, i * 1024:(i + 1) * 1024].rearrange(
            "p (t h n) -> p t h n", t=NT, h=HEADS) for i in range(10)]
        FY = FT
        KTOK = PT[:, T_KTOK * T:(T_KTOK + 4) * T].rearrange("p (t h n) -> p t h n", t=NT, h=HEADS)
        VTOK = PT[:, T_VTOK * T:(T_VTOK + 4) * T].rearrange("p (t h n) -> p t h n", t=NT, h=HEADS)
        OSUM = pt3(T_OSUM, 4)
        SKT = PT[:, T_SKT * T:(T_SKT + 4) * T].rearrange("p (h n) -> p h n", h=PHEADS)
        SKRAW = PT[:, T_SKRAW * T:(T_SKRAW + 4) * T].rearrange("p (h n) -> p h n", h=PHEADS)

        def spot(stage, a, i=0):
            n = before(PRODUCTS, stage, a, i)
            return n % NBK, n // NBK

        def full(eng, stage, a, i=0):
            b, o = spot(stage, a, i)
            eng.wait_ge(sem(f"full{b}"), o + 1)
            return bank[b]

        def free(ins, stage, a, i=0):
            ins.then_inc(sem(f"free{spot(stage, a, i)[0]}"), 1)

        def emptied(eng, stage, a, i=0):
            b, o = spot(stage, a, i)
            eng.wait_ge(sem(f"free{b}"), o + 2)

        seen = {}

        def mark(ins, name, k=1):
            ins.then_inc(sem(name), 1)
            seen[name] = seen.get(name, 0) + 1

        def tell(eng, name):
            eng.sem_inc(sem(name), 1)
            seen[name] = seen.get(name, 0) + 1

        def nth(name, a, per=(1, 1, 1, 1), i=0):
            return sum(per[:a]) + i + 1

        FULLP = (1, 1, 0, 1)

        def after(eng, name, a, per=(1, 1, 1, 1), i=0):
            eng.wait_ge(sem(name), nth(name, a, per, i))

        def chunks(eng, stage, a, body, skip=0):
            n = dict(WEIGHTS)[stage][a]
            if not n:
                return
            c0 = before(WEIGHTS, stage, a)
            if n // 2:
                with eng.Fori(0, n // 2) as i:
                    for j in range(2):
                        body(i * 2 + j, (c0 + j) % 2, i + (c0 + j) // 2)
            if n % 2:
                body(n - 1, (c0 + n - 1) % 2, (c0 + n - 1) // 2)

        def branch_chunks(eng, a, body):
            c0 = before(WEIGHTS, "merge", a)
            for n in range(3):
                with eng.Fori(0, 4) as i:
                    s = c0 + 8 * n
                    body(n, i, (s % 2, s // 2 + i), ((s + 1) % 2, (s + 1) // 2 + i))

        block = ctx.enter_context(nc.Block())

        @block.sync
        def _(sp):
            sp.dma_start(cst[:], inp["constants"]).then_inc(sem("loaded"), 16)
            for t in range(NT):
                sp.dma_start(ROWU[:, t, :], inp["ctx"][0, t * P:(t + 1) * P, :]).then_inc(sem("loaded"), 16)
                sp.dma_start(ROWU[:, NT + t, :], inp["x"][0, t * P:(t + 1) * P, :]).then_inc(sem("loaded"), 16)
            sp.dma_start(CROW[0:8, :], inp["c_ctx"].rearrange("(a b) -> a b", b=P)).then_inc(sem("loaded"), 16)
            sp.dma_start(CROW[8:16, :], inp["c"][0].rearrange("(a b) -> a b", b=P)).then_inc(sem("loaded"), 16)
            sp.dma_start(CROW[16:24, :], inp["final_norm_w"].rearrange("(a b) -> a b", b=P)).then_inc(
                sem("loaded"), 16)

            def vectors(a, l):
                if a:
                    full(sp, "vecs", a - 2)
                    after(sp, "gates_made", a - 1)
                    full(sp, "ab", a - 1)
                rows = [(V_N1, 8, inp["norm1_w"][l]), (V_N2, 8, inp["norm2_w"][l]), (V_BMOD, 48, inp["b_mod"][l]),
                        (V_GN, 1, inp["gdn_norm_w"][l])]
                for at, n, src in rows:
                    sp.dma_start(VROW[at:at + n, :], src.rearrange("(a b) -> a b", b=P)).then_inc(sem("vectors"), 16)
                for j in range(3):
                    sp.dma_start(VROW[V_CA + 12 * j:V_CA + 12 * j + 12, :],
                                 inp["conv_a_w"][l, j].rearrange("(a b) -> a b", b=P)).then_inc(sem("vectors"), 16)
                    sp.dma_start(VROW[V_CB + 4 * j:V_CB + 4 * j + 4, :],
                                 inp["conv_b_w"][l, j].rearrange("(a b) -> a b", b=P)).then_inc(sem("vectors"), 16)
                for at, src in ((V_QN, inp["q_norm_w"]), (V_KN, inp["k_norm_w"])):
                    for half in range(2):
                        sp.dma_start(VROW[at:at + 1, half * HD:(half + 1) * HD], src[l:l + 1, :]).then_inc(
                            sem("vectors"), 16)
                for j, name in enumerate(("a_log", "dt_bias")):
                    sp.dma_start(ADT[:, j, :], inp[name][l:l + 1].rearrange("o a b -> o (a b)").to_broadcast(
                        [P, 8])).then_inc(sem("vectors"), 16)
                sp.dma_start(WAB[:], inp["w_in"][l, :, COL_AB:COL_SC].rearrange("(k p) n -> p k n", p=P)).then_inc(
                    sem("vectors"), 16)

            def load(src, col):
                v = src.rearrange("(k p) n -> p k n", p=P)

                def body(i, b, o):
                    sp.wait_ge(sem(f"wdone{b}"), o + 1)
                    sp.sem_inc(sem("sp_hold"), 1)
                    sp.dma_start(W[:, b, :].rearrange("p (k n) -> p k n", k=KD), v[:, :, bass.ds(i * 256 + col, 256)]
                                 ).then_inc(sem(f"wload{b}"), 16)
                return body

            for a, (l, g, whole) in enumerate(PASSES):
                if g == 0:
                    vectors(a, l)
                    chunks(sp, "mod", a, load(inp["w_mod"][l], 0))
                chunks(sp, "qkvz", a, load(inp["w_in"][l], 0 if whole else 512))
                chunks(sp, "rest", a, load(inp["w_in"][l], COL_SC if whole else COL_KV))
                if not whole:
                    continue
                gates = inp["w_in"][l].rearrange("(k p) n -> p k n", p=P)

                def merge(n, i, gate, branch):
                    b, o = gate
                    sp.wait_ge(sem(f"wdone{b}"), o + 1)
                    sp.sem_inc(sem("sp_hold"), 1)
                    sp.dma_start(W[:, b, :].rearrange("p (k n) -> p k n", k=KD),
                                 gates[:, :, bass.ds(i * 256 + COL_GATE + n * D, 256)]).then_inc(sem(f"wload{b}"), 16)
                    b, o = branch
                    sp.wait_ge(sem(f"wdone{b}"), o + 1)
                    sp.sem_inc(sem("sp_hold"), 1)
                    wb = inp["w_branch"][l, n].rearrange("(k p) n -> p k n", p=P)
                    sp.dma_start(W[:, b, 0:1024].rearrange("p (k n) -> p k n", k=4), wb[:, :, bass.ds(i * 256, 256)]
                                 ).then_inc(sem(f"wload{b}"), 16)
                branch_chunks(sp, a, merge)
                chunks(sp, "out", a, load(inp["w_out"][l], 0))
                after(sp, "branch_a", a, FULLP)
                after(sp, "mixed", a, FULLP)
                sp.dma_start(SKRAW.rearrange("p h (q k) -> p h q k", q=2),
                             inp["sub_keys"][l].rearrange("h q n k -> n h q k")).then_inc(sem("subkeys"), 16)
                chunks(sp, "query", a, load(inp["w_query"][l], 0))
            after(sp, "result", 0)
            sp.dma_start(out[0].rearrange("(t p) d -> p t d", p=P), U2[:]).then_inc(sem("stored"), 16)
            sp.wait_ge(sem("stored"), 16)

        @block.gpsimd
        def _(pool):
            tables = [(ROWU, inp["expert_u"].rearrange("l e d -> (l e) d"), "ufree", "urow"),
                      (ROWV, inp["expert_v"].rearrange("l e d -> (l e) d"), "vfree", "vrow")]
            pool.sem_inc(sem("rowbase"), 1)
            for n, (a, t) in enumerate(PEER_TILES):
                after(pool, "chosen", a, (2, 2, 0, 2), t)
                if n == 0:
                    after(pool, "x_read", 0)
                with pool.Fori(0, BLOCKS // 2) as it:
                    for half in range(2):
                        blk = it * 2 + (n * BLOCKS + half)
                        pool.wait_ge(sem("ufree"), blk * RING + RING)
                        pool.wait_ge(sem("vfree"), blk * RING + RING)
                        pool.sem_inc(sem("rowbase"), 1)
                        pool.tensor_copy(IXC[:, half, :], IDX[:, t, bass.ds(it * 2 * RING + half * RING, RING)]
                                         ).then_inc(sem("idxcol"), 1)
                        pool.wait_ge(sem("idxcol"), blk + 1)
                        pool.sem_inc(sem("rowbase"), 1)
                        for rows, table, freed, landed in tables:
                            for b in range(RING):
                                pool.wait_ge(sem(freed), blk * RING + (RING + b + 1))
                                pool.sem_inc(sem("rowbase"), 1)
                                pool.indirect_dma_start(rows[:, b, :], None, table, bass.IndirectOffsetOnAxis(
                                    ap=IXC[:, half, b:b + 1], axis=0)).then_inc(sem(f"{landed}{b}"), 16)

        @block.tensor
        def _(pe):
            for b in range(NBK):
                pe.sem_inc(sem(f"free{b}"), 1)
            for b in range(2):
                pe.sem_inc(sem(f"wbfree{b}"), 1)
                pe.sem_inc(sem(f"wdone{b}"), 1)
            order = []

            def empty(stage, a, i=0):
                b, o = spot(stage, a, i)
                assert b == len(order) % NBK and o == len(order) // NBK, (stage, a, i, len(order))
                order.append(1)
                pe.wait_ge(sem(f"free{b}"), o + 1)
                return bank[b]

            def filled(ins, stage, a, i=0):
                ins.then_inc(sem(f"full{spot(stage, a, i)[0]}"), 1)

            def mm(o, l, r, start=True, stop=True):
                return pe.matmul(o, l, r, start=start, stop=stop)

            def weight_product(rhs, kn, n):
                def body(i, b, o):
                    pe.wait_ge(sem(f"wload{b}"), o * 16 + 16)
                    pe.wait_ge(sem(f"wbfree{b}"), o + 1)
                    w = W[:, b, 0:kn * 256].rearrange("p (k n) -> p k n", k=kn)
                    for h in range(2):
                        for k in range(kn):
                            ins = mm(wbank[b][:, h * n:(h + 1) * n], w[:, k, h * P:(h + 1) * P], rhs(k),
                                     k == 0, k == kn - 1)
                    ins.then_inc(sem(f"wdone{b}"), 1)
                return body

            def sum_channels(stage, a, lhs, rhs, n, i=0):
                o = empty(stage, a, i)
                for k in range(n):
                    ins = mm(o[:, 0:T], lhs, rhs(k), k == 0, k == n - 1)
                filled(ins, stage, a, i)

            for a, (l, g, whole) in enumerate(PASSES):
                if a == 0:
                    pe.wait_ge(sem("loaded"), 16 * 8)
                    for j in range(8):
                        o = empty("x_in", a, j)
                        for k in range(4):
                            ins = pe.transpose(o[:, k * P:(k + 1) * P],
                                               ROWU[:, j // 2, ((j % 2) * 4 + k) * P:((j % 2) * 4 + k + 1) * P], c("ident"))
                        filled(ins, "x_in", a, j)
                    o = empty("cond", a)
                    filled(pe.transpose(o[:, 0:24], CROW[:], cst[0:24, 0:24]), "cond", a)
                if g == 0:
                    pe.wait_ge(sem("vectors"), 16 * 17 * (l + 1))
                    o = empty("vecs", a)
                    filled(pe.transpose(o[:, 0:NV], VROW[:], cst[0:NV, 0:NV]), "vecs", a)
                    after(pe, "cond_ready", 0)
                    chunks(pe, "mod", a, weight_product(lambda k: CVEC[:, k:16:8], KD, 2))
                after(pe, "sq1", a)
                sum_channels("rms1", a, c("ones"), lambda k: F[:, k * T:(k + 1) * T], KD)
                after(pe, "u1", a)
                chunks(pe, "qkvz", a, weight_product(lambda k: U[:, k, :], KD, T))
                chunks(pe, "rest", a, weight_product(lambda k: U[:, k, :], KD, T))
                o = empty("ab", a)
                for t in range(NT):
                    for k in range(KD):
                        ins = mm(o[:, t * 16:(t + 1) * 16], U[:, k, t * P:(t + 1) * P], WAB[:, k, :], k == 0, k == KD - 1)
                filled(ins, "ab", a)
                after(pe, "gates_made", a)
                o = empty("cum", a)
                for t in range(NT):
                    for d in range(2):
                        mm(o[:, t * 16 + 4 * d:t * 16 + 4 * d + 4], c(f"tri{d}"), GB[:, t, 4 * d:4 * d + 4])
                    ins = mm(o[:, t * 16 + 8:t * 16 + 16], c("chunk"), GB[:, t, 0:8])
                filled(ins, "cum", a)
                after(pe, "sq_l2", a)
                n2 = 4 if whole else 2
                for j in range(n2):
                    o = empty("l2", a, j)
                    filled(mm(o[:], c("ones"), F[:, (j + 4 - n2) * 512:(j + 5 - n2) * 512]), "l2", a, j)
                after(pe, "qk_normed", a)
                for j in range(4):
                    o = empty("tok", a, j)
                    for h in range(HEADS):
                        ins = pe.transpose(o[:, h * P:(h + 1) * P],
                                           QC[:, 4 + 4 * (j // 2) + h, (j % 2) * P:(j % 2 + 1) * P], c("ident"))
                    filled(ins, "tok", a, j)
                for d in range(2):
                    for t in range(NT):
                        o = empty(f"decay{d}", a, t)
                        for h in range(HEADS):
                            ins = mm(o[:, h * P:(h + 1) * P],
                                     GB[:, t, 4 * d + h:4 * d + h + 1].to_broadcast([P, P]), c(f"tri{d}"))
                        filled(ins, f"decay{d}", a, t)
                    for t in range(NT):
                        o = empty(f"gram{d}", a, t)
                        for h in range(HEADS):
                            k = QC[:, 4 + h, t * P:(t + 1) * P]
                            ins = mm(o[:, h * P:(h + 1) * P], k, k)
                        filled(ins, f"gram{d}", a, t)
                    if whole:
                        for t in range(NT):
                            o = empty(f"qk{d}", a, t)
                            for h in range(HEADS):
                                ins = mm(o[:, h * P:(h + 1) * P], QC[:, 4 + h, t * P:(t + 1) * P],
                                         QC[:, h, t * P:(t + 1) * P])
                            filled(ins, f"qk{d}", a, t)
                    for n, (kind, lv) in enumerate(SOLVE):
                        for t in range(NT):
                            i = 2 * n + t
                            if kind == "x":
                                after(pe, "level", a, (24,) * 4, 12 * d + 2 * lv + t)
                            elif kind == "u":
                                after(pe, "x_out", a, (24,) * 4, 12 * d + 2 * lv + t)
                            o = empty(f"solve{d}", a, i)
                            for h in range(HEADS):
                                if kind == "x":
                                    r = c("ident") if lv == 0 else FU[:, t, h, :]
                                    ins = mm(o[:, h * P:(h + 1) * P], FW[:, t, h, :], r)
                                elif kind == "u":
                                    ins = mm(o[:, h * P:(h + 1) * P], FT[:, t, h, :], FX[:, t, h, :])
                                else:
                                    ins = mm(o[:, h * P:(h + 1) * P], FX[:, t, h, :], FT[:, t, h, :])
                            filled(ins, f"solve{d}", a, i)
                    after(pe, "solved", a, (2,) * 4, d)
                    after(pe, "rhs_in", a, (2,) * 4, d)
                    after(pe, "rhs_v", a, (2,) * 4, d)
                    for t in range(NT):
                        o = empty(f"rhs{d}", a, t)
                        for h in range(HEADS):
                            ins = mm(o[:, h * P:(h + 1) * P], FU[:, t, h, :], FVB[:, t, h, :])
                        filled(ins, f"rhs{d}", a, t)
                    for t in range(NT):
                        o = empty(f"rhs{d}", a, 2 + t)
                        for h in range(HEADS):
                            ins = mm(o[:, h * P:(h + 1) * P], FKB[:, t, h, :], FU[:, t, h, :])
                        filled(ins, f"rhs{d}", a, 2 + t)
                    after(pe, "w_out", a, (2,) * 4, d)
                    step = 3 if whole else 2
                    for s in range(4):
                        ch = 3 - s if d else s
                        t, half = ch // 2, ch % 2
                        after(pe, "state", a, (10,) * 4, 5 * d + s)
                        o = empty(f"scan{d}", a, step * s)
                        for h in range(HEADS):
                            ins = mm(o[:, h * P:(h + 1) * P], FW[:, t, h, :], S[:, d, h, :])
                        filled(ins, f"scan{d}", a, step * s)
                        after(pe, "vnew", a, (8,) * 4, 4 * d + s)
                        if whole:
                            o = empty(f"scan{d}", a, step * s + 1)
                            lo = half * CHUNK
                            for h in range(HEADS):
                                mm(o[:, h * CHUNK:(h + 1) * CHUNK], S[:, d, h, :], FD[:, t, h, lo:lo + CHUNK], True, False)
                                ins = mm(o[:, h * CHUNK:(h + 1) * CHUNK], VN[:, half, h, :], FQ[:, t, h, lo:lo + CHUNK],
                                         False, True)
                            filled(ins, f"scan{d}", a, step * s + 1)
                        o = empty(f"scan{d}", a, step * s + step - 1)
                        for h in range(HEADS):
                            ins = mm(o[:, h * P:(h + 1) * P], FK[:, t, h, :], VN[:, half, h, :])
                        filled(ins, f"scan{d}", a, step * s + step - 1)
                if whole:
                    after(pe, "sq_g", a, FULLP)
                    for j in range(2):
                        o = empty("gout", a, j)
                        filled(mm(o[:], c("ones"), F[:, j * 512:(j + 1) * 512]), "gout", a, j)
                after(pe, "sq_a", a)
                lo, n = (0, 5) if whole else (4, 1)
                for j in range(3 if whole else 1):
                    w = min(512, n * T - 512 * j)
                    o = empty("an", a, j)
                    filled(mm(o[:, 0:w], c("blk64"), F[:, 2048 + lo * T + j * 512:2048 + lo * T + j * 512 + w]), "an", a, j)
                if g == 1:
                    after(pe, "a_normed", a)
                    for j in range(3):
                        w = min(512, 5 * T - 512 * j)
                        o = empty("rope", a, j)
                        filled(mm(o[:, 0:w], c("rot"), PT[:, T_AQ * T + j * 512:T_AQ * T + j * 512 + w]), "rope", a, j)
                after(pe, "a_turned", a)
                o = empty("dup", a)
                for v in range(KVHEADS):
                    ins = mm(o[:, v * T:(v + 1) * T], c(f"dup{v}"), pt(T_AK))
                filled(ins, "dup", a)
                o = empty("vtok", a)
                for t in range(NT):
                    ins = pe.transpose(o[:, t * P:(t + 1) * P], PT[:, (T_AK + 1) * T + t * P:(T_AK + 1) * T + (t + 1) * P],
                                       c("ident"))
                filled(ins, "vtok", a)
                if not whole:
                    continue
                after(pe, "kv_ready", a)
                k0, kt = (0, 4) if g else (2, 2)
                for n, (kind, i) in enumerate(ATT):
                    t, h = i // AHEADS, i % AHEADS
                    hp = HD * (h % 2)
                    o = empty("att", a, n) if kind != "p" else None
                    if kind == "s":
                        ins = mm(o[:, 0:kt * P], PT[hp:hp + HD, (T_AQ + h // 2) * T + t * P:(T_AQ + h // 2) * T + (t + 1) * P],
                                 KDUP[hp:hp + HD, h // 4, k0 * P:(k0 + kt) * P])
                    elif kind == "p":
                        after(pe, "probs", a, (16, 16, 0, 16), i)
                        o = empty("att", a, n)
                        for k in range(kt):
                            ins = pe.transpose(o[:, k * P:(k + 1) * P], F[:, (i % 2) * 512 + k * P:(i % 2) * 512 + (k + 1) * P],
                                               c("ident"))
                    else:
                        after(pe, "probs_t", a, (16, 16, 0, 16), i)
                        for k in range(kt):
                            ins = mm(o[hp:hp + HD, 0:P], VV[:, k0 + k, (h // 4) * HD:(h // 4 + 1) * HD],
                                     F[:, 1024 + (i % 2) * 512 + k * P:1024 + (i % 2) * 512 + (k + 1) * P],
                                     k == 0, k == kt - 1)
                    filled(ins, "att", a, n)
                after(pe, "att_out", a, FULLP)

                def merge(n, i, gate, branch):
                    weight_product(lambda k: U[:, k, :], KD, T)(i, *gate)
                    src = (T_OA, T_OB, T_OC)[n]
                    weight_product(lambda k: pt(src + k), 4, T)(i, *branch)
                branch_chunks(pe, a, merge)
                after(pe, "mixed", a, FULLP)
                chunks(pe, "out", a, weight_product(lambda k: pt(T_MIX + k), KD, T))
                after(pe, "sq2", a, FULLP)
                sum_channels("rms2", a, c("ones"), lambda k: F[:, k * T:(k + 1) * T], KD)
                after(pe, "u2", a, FULLP)
                for j in range(4):
                    o = empty("u2t", a, j)
                    for k in range(4):
                        ins = pe.transpose(o[:, k * P:(k + 1) * P], U[:, (j % 2) * 4 + k, (j // 2) * P:(j // 2 + 1) * P],
                                           c("ident"))
                    filled(ins, "u2t", a, j)
                pe.wait_ge(sem("subkeys"), 16 * nth("subkeys", a, FULLP))
                for j in range(2):
                    o = empty("skt", a, j)
                    for k in range(4):
                        ins = pe.transpose(o[:, k * P:(k + 1) * P], SKRAW[:, 4 * j + k, :], c("ident"))
                    filled(ins, "skt", a, j)
                chunks(pe, "query", a, weight_product(lambda k: U[:, k, :], KD, T))
                after(pe, "query_out", a, FULLP)
                for j in range(8):
                    t, q, hb = j // 4, (j // 2) % 2, j % 2
                    o = empty("keys", a, j)
                    for h in range(4):
                        hh = 4 * hb + h
                        ins = mm(o[:, h * P:(h + 1) * P], PT[HD * q:HD * q + HD, (16 + hh) * T + t * P:(16 + hh) * T + (t + 1) * P],
                                 SKT[HD * q:HD * q + HD, hh, :])
                    filled(ins, "keys", a, j)
                for t in range(NT):
                    after(pe, "retrieved", a, (2, 2, 0, 2), t)
                    for j in range(2):
                        o = empty("back", a, 2 * t + j)
                        for k in range(4):
                            ins = pe.transpose(o[:, k * P:(k + 1) * P], ACC[:, (4 * j + k) * P:(4 * j + k + 1) * P], c("ident"))
                        filled(ins, "back", a, 2 * t + j)
            a = 3
            after(pe, "sq3", 0)
            sum_channels("fin", a, c("ones"), lambda k: F[:, k * T:(k + 1) * T], KD)
            after(pe, "u3", 0)
            for j in range(4):
                o = empty("out", a, j)
                for k in range(4):
                    ins = pe.transpose(o[:, k * P:(k + 1) * P], U[:, (j % 2) * 4 + k, (j // 2) * P:(j // 2 + 1) * P], c("ident"))
                filled(ins, "out", a, j)

        @block.scalar
        def _(act):
            own = [0]

            def A(o, i, f=ACT.Copy, **k):
                return nc.scalar.activation(o, i, f, **k)

            def link(ins):
                own[0] += 1
                ins.then_inc(sem("act_step"), 1)

            def settle():
                act.wait_ge(sem("act_step"), own[0])

            def root(stage, a, i=0):
                n = before(ROOTS, stage, a, i)
                act.wait_ge(sem("var"), n + 1)
                return n

            def move(dst, w=512, first=0):
                def body(i, b, o):
                    act.wait_ge(sem(f"wdone{b}"), o + 2)
                    act.sem_inc(sem("act_hold"), 1)
                    A(dst(i, w), wbank[b][:, 0:w]).then_inc(sem(f"wbfree{b}"), 1)
                return body

            def moved(stage, a):
                n = dict(WEIGHTS)[stage][a]
                for i in range(max(0, n - 2), n):
                    cc = before(WEIGHTS, stage, a, i)
                    act.wait_ge(sem(f"wbfree{cc % 2}"), cc // 2 + 2)

            for a, (l, g, whole) in enumerate(PASSES):
                if a == 0:
                    for j in range(8):
                        o = full(act, "x_in", a, j)
                        gi, t, hf = j // 4, (j // 2) % 2, j % 2
                        free(A(H[:, gi, 4 * hf:4 * hf + 4, t * P:(t + 1) * P], o[:].rearrange("p (k n) -> p k n", k=4)),
                             "x_in", a, j)
                    o = full(act, "cond", a)
                    link(A(CVEC[:, 16:24], o[:, 16:24]))
                    free(A(CVEC[:, 0:16], o[:, 0:16], ACT.Silu), "cond", a)
                    emptied(act, "cond", a)
                    settle()
                    tell(act, "x_read")
                    tell(act, "cond_ready")
                if a:
                    after(act, "h_done", min(a, 2) - 1)
                if g == 0:
                    o = full(act, "vecs", a)
                    free(A(VEC[:], o[:, 0:NV]), "vecs", a)
                    chunks(act, "mod", a, move(lambda i, w: MOD[:].rearrange("p a b -> p (a b)")[:, bass.ds(i * 4, 4)], 4))
                if a == 0:
                    for j in range(2, 8):
                        emptied(act, "x_in", a, j)
                mark(A(F[:, 0:KD * T], H[:, g].rearrange("p k n -> p (k n)"), ACT.Square), "sq1")
                root("rms1", a)
                A(F[:, 2304:2560], F[:, 2048:2304], ACT.Sqrt).then_inc(sem("root"), 1)
                after(act, "scaled1", a)
                for k in range(KD):
                    ins = A(U[:, k, :], U[:, k, :], ACT.Identity, bias=MOD[:, k, g:g + 1])
                    mark(ins, "u1") if k == KD - 1 else link(ins)
                if whole:
                    chunks(act, "qkvz", a, move(lambda i, w: PT[:, bass.ds(i * 512, 512)]))
                else:
                    chunks(act, "qkvz", a, move(lambda i, w: PT[:, bass.ds(i * 512 + 4 * T, 512)]))
                if whole:
                    chunks(act, "rest", a, move(lambda i, w: PT[:, bass.ds(i * 512 + T_BG * T, 512)]))
                else:
                    chunks(act, "rest", a, move(lambda i, w: PT[:, T_AK * T:T_AK * T + 512]))
                moved("rest", a)
                o = full(act, "ab", a)
                free(A(AB[:].rearrange("p a b -> p (a b)"), o[:, 0:32]), "ab", a)
                emptied(act, "ab", a)
                mark(A(AB[:, :, 8:16], AB[:, :, 8:16], ACT.Sigmoid), "proj_out")
                after(act, "ab_biased", a)
                link(A(TMPC[:, :, 0:8], AB[:, :, 0:8], ACT.Abs))
                settle()
                link(A(TMPC[:, :, 0:8], TMPC[:, :, 0:8], ACT.Exp, scale=-1.0))
                settle()
                link(A(TMPC[:, :, 0:8], TMPC[:, :, 0:8], ACT.Ln, bias=1.0))
                link(A(TMPC[:, :, 8:16], ADT[:, 0:1, :].to_broadcast([P, NT, 8]), ACT.Exp))
                settle()
                mark(A(AB[:, :, 0:8], AB[:, :, 0:8], ACT.Relu), "softplus")
                o = full(act, "cum", a)
                free(A(GC[:].rearrange("p a b -> p (a b)"), o[:, 0:32]), "cum", a)
                emptied(act, "cum", a)
                tell(act, "cum_out")
                after(act, "conv_a", a)
                q0 = 0 if whole else 4
                link(A(QC[:, q0:12, :], QC[:, q0:12, :], ACT.Silu))
                settle()
                mark(A(f3(q0 * T, 8 - q0, T), QC[:, q0:8, :], ACT.Square), "sq_l2")
                for j in range(4 if whole else 2):
                    root("l2", a, j)
                    A(F[:, 4096 + j * 512:4608 + j * 512], F[:, 2048 + j * 512:2560 + j * 512], ACT.Sqrt).then_inc(
                        sem("root"), 1)
                for j in range(4):
                    o = full(act, "tok", a, j)
                    dst = (KTOK if j < 2 else VTOK)[:, j % 2]
                    ins = A(dst, o[:].rearrange("p (h n) -> p h n", h=HEADS))
                    free(ins, "tok", a, j)
                for j in range(4):
                    emptied(act, "tok", a, j)
                after(act, "cum_diff", a)
                mark(A(EGC[:], EGC[:], ACT.Exp), "cum_exp")
                for d in range(2):
                    for t in range(NT):
                        o = full(act, f"decay{d}", a, t)
                        o3 = o[:].rearrange("p (h n) -> p h n", h=HEADS)
                        ends = (CHUNK - 1, P) if d == 0 else (0, P - CHUNK + 1)
                        if d and t == 0:
                            after(act, "state", a, (10,) * 4, 4)
                        link(A(DEC[:, t], o3[:, :, ends[0]:ends[1]:CHUNK], ACT.Exp))
                        mark(A(FD[:, t], o3, ACT.Exp), "eg")
                    for t in range(NT):
                        after(act, "diffs", a, (4,) * 4, 2 * d + t)
                        link(A(FA[:, t], FA[:, t], ACT.Exp, scale=-1.0))
                        mark(A(FQ[:, t], FQ[:, t], ACT.Exp), "decays")
                    for t in range(NT):
                        for h in range(HEADS):
                            ins = A(FVB[:, t, h, :], VTOK[:, t, h, :], scale=GB[:, t, 8 + 4 * d + h:9 + 4 * d + h])
                            mark(ins, "rhs_v") if (t, h) == (NT - 1, HEADS - 1) else link(ins)
                    for lv in range(6):
                        for t in range(NT):
                            i = 2 * SOLVE.index(("x", lv)) + t
                            o = full(act, f"solve{d}", a, i)
                            ins = A(FX[:, t], o[:].rearrange("p (h n) -> p h n", h=HEADS))
                            free(ins, f"solve{d}", a, i)
                            emptied(act, f"solve{d}", a, i)
                            tell(act, "x_out")
                    for t in range(NT):
                        o = full(act, f"rhs{d}", a, 2 + t)
                        free(A(FW[:, t], o[:].rearrange("p (h n) -> p h n", h=HEADS)), f"rhs{d}", a, 2 + t)
                    for t in range(NT):
                        emptied(act, f"rhs{d}", a, 2 + t)
                    tell(act, "w_out")
                if whole:
                    after(act, "osum", a, FULLP)
                    link(A(pt(T_Z, 4), pt(T_Z, 4), ACT.Silu))
                    settle()
                    mark(A(F[:, 0:1024], pt(T_OSUM, 4), ACT.Square), "sq_g")
                    for j in range(2):
                        root("gout", a, j)
                        A(F[:, 4096 + j * 512:4608 + j * 512], F[:, 2048 + j * 512:2560 + j * 512], ACT.Sqrt).then_inc(
                            sem("root"), 1)
                    after(act, "branch_a", a, FULLP)
                else:
                    after(act, "state", a, (10,) * 4, 9)
                lo, n = (0, 5) if whole else (4, 1)
                mark(A(F[:, 2048 + lo * T:2048 + (lo + n) * T], PT[:, (T_AQ + lo) * T:(T_AQ + lo + n) * T], ACT.Square), "sq_a")
                for j in range(3 if whole else 1):
                    w = min(512, n * T - 512 * j)
                    root("an", a, j)
                    A(F[:, 6144 + j * 512:6144 + j * 512 + w], F[:, 4096 + j * 512:4096 + j * 512 + w], ACT.Sqrt).then_inc(
                        sem("root"), 1)
                o = full(act, "dup", a)
                free(A(KDUP[:, :, (1 - g) * T:(2 - g) * T], o[:].rearrange("p (v n) -> p v n", v=2)), "dup", a)
                o = full(act, "vtok", a)
                free(A(VV[:, NT * (1 - g):NT * (2 - g), :], o[:, 0:T].rearrange("p (t n) -> p t n", t=NT)), "vtok", a)
                emptied(act, "dup", a)
                emptied(act, "vtok", a)
                tell(act, "kv_ready")
                if not whole:
                    continue
                kt = 4 if g else 2
                for n, (kind, i) in enumerate(ATT):
                    if kind == "s":
                        after(act, "maxed", a, (16, 16, 0, 16), i)
                        o = full(act, "att", a, n)
                        free(A(F[:, (i % 2) * 512:(i % 2) * 512 + kt * P], o[:, 0:kt * P], ACT.Exp, scale=HD ** -0.5,
                               bias=SM[:, 0, i % 2:i % 2 + 1], accum_out=SM[:, 0, 2 + i % 2:3 + i % 2]), "att", a, n)
                    elif kind == "p":
                        o = full(act, "att", a, n)
                        free(A(F[:, 1024 + (i % 2) * 512:1024 + (i % 2) * 512 + kt * P], o[:, 0:kt * P]), "att", a, n)
                        emptied(act, "att", a, n)
                        tell(act, "probs_t")

                def merge(n, i, gate, branch):
                    b, o = gate
                    act.wait_ge(sem(f"wdone{b}"), o + 2)
                    act.wait_ge(sem("sgfree"), i + (nth("sgfree", a, (12, 12, 0, 12), 4 * n)))
                    act.sem_inc(sem("act_hold"), 1)
                    A(F[:, 0:512], wbank[b][:], ACT.Sigmoid).then_inc(sem(f"wbfree{b}"), 1)
                after(act, "att_out", a, FULLP)
                branch_chunks(act, a, merge)
                after(act, "h_mid", a, FULLP)
                mark(A(F[:, 0:KD * T], H[:, g].rearrange("p k n -> p (k n)"), ACT.Square), "sq2")
                root("rms2", a)
                A(F[:, 2304:2560], F[:, 2048:2304], ACT.Sqrt).then_inc(sem("root"), 1)
                after(act, "scaled2", a, FULLP)
                for k in range(KD):
                    ins = A(U[:, k, :], U[:, k, :], ACT.Identity, bias=MOD[:, 24 + k, g:g + 1])
                    mark(ins, "u2") if k == KD - 1 else link(ins)
                for j in range(4):
                    o = full(act, "u2t", a, j)
                    free(A(U2[:, j // 2, (j % 2) * 512:(j % 2) * 512 + 512], o[:]), "u2t", a, j)
                for j in range(2):
                    o = full(act, "skt", a, j)
                    free(A(SKT[:, 4 * j:4 * j + 4, :], o[:].rearrange("p (h n) -> p h n", h=4)), "skt", a, j)
                chunks(act, "query", a, move(lambda i, w: PT[:, bass.ds(i * 512 + 16 * T, 512)]))
                moved("query", a)
                for j in range(2):
                    emptied(act, "skt", a, j)
                for j in range(4):
                    emptied(act, "u2t", a, j)
                tell(act, "query_out")
                for t in range(NT):
                    after(act, "best", a, (2, 2, 0, 2), t)
                    mark(A(GATE[:, t, :], GATE[:, t, :], ACT.Exp), "gate_exp")
                for t in range(NT):
                    n = PEER_TILES.index((a, t))
                    with act.Fori(0, BLOCKS) as i:
                        act.wait_ge(sem("dots"), i + (n * BLOCKS + 1))
                        act.sem_inc(sem("act_hold"), 1)
                        A(GEL[:], DOT[:, bass.ds(i * RING, RING)], ACT.Gelu).then_inc(sem("gelu"), 1)
            after(act, "h_done", 2)
            mark(A(F[:, 0:KD * T], H[:, 1].rearrange("p k n -> p (k n)"), ACT.Square), "sq3")
            root("fin", 3)
            A(F[:, 2304:2560], F[:, 2048:2304], ACT.Sqrt).then_inc(sem("root"), 1)
            for j in range(4):
                o = full(act, "out", 3, j)
                free(A(U2[:, j // 2, (j % 2) * 512:(j % 2) * 512 + 512], o[:]), "out", 3, j)
            for j in range(4):
                emptied(act, "out", 3, j)
            tell(act, "result")

        @block.vector
        def _(dve):
            own = [0]
            v = nc.vector

            def post(ins):
                own[0] += 1
                ins.then_inc(sem("dve_step"), 1)

            def settle():
                dve.wait_ge(sem("dve_step"), own[0])

            def step(ins):
                post(ins)
                settle()

            def rsqrt(stage, a, i, w, scale, at, rt, tmp):
                o = full(dve, stage, a, i)
                free(v.tensor_scalar(F[:, at:at + w], o[:, 0:w], scale, EPS, ALU.mult, ALU.add), stage, a, i)
                emptied(dve, stage, a, i)
                dve.sem_inc(sem("var"), 1)
                dve.wait_ge(sem("root"), before(ROOTS, stage, a, i) + 1)
                x, y, z = F[:, at:at + w], F[:, rt:rt + w], F[:, tmp:tmp + w]
                step(v.reciprocal(y, y))
                step(v.tensor_tensor(z, y, y, ALU.mult))
                step(v.tensor_tensor(z, z, x, ALU.mult))
                step(v.tensor_scalar(z, z, -0.5, 1.5, ALU.mult, ALU.add))
                step(v.tensor_tensor(y, y, z, ALU.mult))
                return y

            def conv(dst, src, w, n):
                for i in range(n):
                    post(v.tensor_scalar(dst(i), src(i), w(1, i), None, ALU.mult))
                settle()
                for i in range(n):
                    post(v.scalar_tensor_tensor(out=dst(i)[:, 1:T], in0=src(i)[:, 0:T - 1], scalar=w(0, i),
                                                in1=dst(i)[:, 1:T], op0=ALU.mult, op1=ALU.add))
                settle()
                for i in range(n):
                    post(v.scalar_tensor_tensor(out=dst(i)[:, 0:T - 1], in0=src(i)[:, 1:T], scalar=w(2, i),
                                                in1=dst(i)[:, 0:T - 1], op0=ALU.mult, op1=ALU.add))
                settle()

            def bc(ap, n):
                return ap.unsqueeze(len(ap.shape)).to_broadcast(list(ap.shape) + [n])

            step(v.memset(VN[:], 0.0))
            step(v.memset(SM[:], 0.0))
            for name in ("ufree", "vfree"):
                for _ in range(2 * RING):
                    dve.sem_inc(sem(name), 1)
            dve.sem_inc(sem("sgfree"), 1)
            for a, (l, g, whole) in enumerate(PASSES):
                if g == 0:
                    cl = before(WEIGHTS, "mod", a, 23)
                    for cc in (cl - 1, cl):
                        dve.wait_ge(sem(f"wbfree{cc % 2}"), cc // 2 + 2)
                    emptied(dve, "vecs", a)
                    step(v.tensor_tensor(MOD[:], MOD[:], bc(VEC[:, V_BMOD:V_BMOD + 48], 2), ALU.add))
                    for n, (vn, sc) in enumerate(((V_N1, 8), (V_N2, 32))):
                        step(v.tensor_scalar(A12[:, n], MOD[:, sc:sc + 8, :], 1.0, None, ALU.add))
                        step(v.tensor_tensor(A12[:, n], A12[:, n], bc(VEC[:, vn:vn + 8], 2), ALU.mult))
                rs = rsqrt("rms1", a, 0, T, 1.0 / D, 2048, 2304, 2560)
                for k in range(KD):
                    ins = v.scalar_tensor_tensor(out=U[:, k, :], in0=H[:, g, k, :], scalar=A12[:, 0, k, g:g + 1],
                                                 in1=rs, op0=ALU.mult, op1=ALU.mult)
                    mark(ins, "scaled1") if k == KD - 1 else post(ins)
                after(dve, "proj_out", a)
                mark(v.tensor_tensor(AB[:, :, 0:8], AB[:, :, 0:8], ADT[:, 1:2, :].to_broadcast([P, NT, 8]), ALU.add),
                     "ab_biased")
                after(dve, "softplus", a)
                step(v.tensor_tensor(TMPC[:, :, 0:8], TMPC[:, :, 0:8], AB[:, :, 0:8], ALU.add))
                step(v.tensor_copy(GB[:, :, 8:16], AB[:, :, 8:16]))
                mark(v.scalar_tensor_tensor(out=GB[:, :, 0:8], in0=TMPC[:, :, 0:8], scalar=-1.0, in1=TMPC[:, :, 8:16],
                                            op0=ALU.mult, op1=ALU.mult), "gates_made")
                q0 = 0 if whole else 4
                conv(lambda i: QC[:, q0 + i, :], lambda i: pt(T_QKV + q0 + i),
                     lambda j, i: VEC[:, V_CA + 12 * j + q0 + i:V_CA + 12 * j + q0 + i + 1], 12 - q0)
                tell(dve, "conv_a")
                if whole:
                    step(v.tensor_tensor(pt(T_CG, 4), pt(T_CG, 4), pt(T_XIN, 4), ALU.mult))
                    conv(lambda i: pt(T_XIN + i), lambda i: pt(T_CG + i),
                         lambda j, i: VEC[:, V_CB + 4 * j + i:V_CB + 4 * j + i + 1], 4)
                    step(v.tensor_tensor(pt(T_OB, 4), pt(T_BG, 4), pt(T_XIN, 4), ALU.mult))
                for j in range(4 if whole else 2):
                    jj = j if whole else j + 2
                    y = rsqrt("l2", a, j, 512, 1.0, 2048 + j * 512, 4096 + j * 512, 6144 + j * 512)
                    qk = QC[:, 2 * jj:2 * jj + 2, :].rearrange("p a b -> p (a b)")
                    ins = v.scalar_tensor_tensor(out=qk, in0=qk, scalar=P ** -0.5 if jj < 2 else 1.0, in1=y,
                                                 op0=ALU.mult, op1=ALU.mult)
                    mark(ins, "qk_normed") if jj == 3 else post(ins)
                after(dve, "cum_out", a)
                post(v.tensor_copy(EGC[:, :, 0:8], GC[:, :, 0:8]))
                mark(v.tensor_tensor(EGC[:, :, 8:16], GC[:, :, 8:16], GC[:, :, 0:8], ALU.subtract), "cum_diff")
                after(dve, "cum_exp", a)
                mark(v.tensor_tensor(BEG[:], EGC[:, :, 0:8], GB[:, :, 8:16], ALU.mult), "columns")
                after(dve, "columns", a)
                for d in range(2):
                    for t in range(NT):
                        o = full(dve, f"decay{d}", a, t)
                        after(dve, "eg", a, (4,) * 4, 2 * d + t)
                        for h in range(HEADS):
                            col = GC[:, t, 4 * d + h:4 * d + h + 1]
                            post(v.tensor_scalar(FA[:, t, h, :], o[:, h * P:(h + 1) * P], col, 0.0, ALU.subtract, ALU.max))
                            ins = v.tensor_scalar(FQ[:, t, h, :], o[:, h * P:(h + 1) * P], col, 0.0, ALU.subtract, ALU.min)
                            if h < HEADS - 1:
                                post(ins)
                            else:
                                free(ins, f"decay{d}", a, t)
                        emptied(dve, f"decay{d}", a, t)
                        tell(dve, "diffs")
                    for t in range(NT):
                        if whole:
                            step(v.tensor_tensor(FD[:, t], FD[:, t], QC[:, 0:HEADS, t * P:(t + 1) * P], ALU.mult))
                        for h in range(HEADS):
                            k = 4 * d + h
                            post(v.tensor_scalar(FKB[:, t, h, :], KTOK[:, t, h, :], BEG[:, t, k:k + 1], None, ALU.mult))
                            post(v.tensor_scalar(FK[:, t, h, :], KTOK[:, t, h, :], EGC[:, t, 8 + k:9 + k], None, ALU.mult))
                    settle()
                    tell(dve, "rhs_in")
                    for t in range(NT):
                        after(dve, "decays", a, (4,) * 4, 2 * d + t)
                        m = c(f"str{d}").unsqueeze(1).to_broadcast([P, HEADS, P])
                        step(v.tensor_tensor(FA[:, t], FA[:, t], m, ALU.mult))
                        o = full(dve, f"gram{d}", a, t)
                        for h in range(HEADS):
                            ins = v.scalar_tensor_tensor(out=FA[:, t, h, :], in0=o[:, h * P:(h + 1) * P],
                                                         scalar=GB[:, t, 8 + 4 * d + h:9 + 4 * d + h], in1=FA[:, t, h, :],
                                                         op0=ALU.mult, op1=ALU.mult)
                            post(ins) if h < HEADS - 1 else free(ins, f"gram{d}", a, t)
                        emptied(dve, f"gram{d}", a, t)
                    if whole:
                        for t in range(NT):
                            m = c(f"tri{d}").unsqueeze(1).to_broadcast([P, HEADS, P])
                            step(v.tensor_tensor(FQ[:, t], FQ[:, t], m, ALU.mult))
                            o = full(dve, f"qk{d}", a, t)
                            free(v.tensor_tensor(FQ[:, t], FQ[:, t], o[:].rearrange("p (h n) -> p h n", h=HEADS), ALU.mult),
                                 f"qk{d}", a, t)
                    for lv in range(6):
                        m = c(f"lv{lv}").unsqueeze(1).to_broadcast([P, HEADS, P])
                        for t in range(NT):
                            mark(v.tensor_tensor(FW[:, t], FA[:, t], m, ALU.mult), "level")
                        ident = c("ident").unsqueeze(1).to_broadcast([P, HEADS, P])
                        if lv == 0:
                            for t in range(NT):
                                i = 2 * SOLVE.index(("x", 0)) + t
                                after(dve, "level", a, (24,) * 4, 12 * d + t)
                                post(v.tensor_tensor(FT[:, t], ident, FW[:, t], ALU.subtract))
                                after(dve, "x_out", a, (24,) * 4, 12 * d + t)
                                step(v.tensor_tensor(FU[:, t], ident, FX[:, t], ALU.subtract))
                            continue
                        for kind, dst in (("u", FU), ("t", FT)):
                            if (kind, lv) not in SOLVE:
                                continue
                            for t in range(NT):
                                i = 2 * SOLVE.index((kind, lv)) + t
                                o = full(dve, f"solve{d}", a, i)
                                free(v.tensor_tensor(dst[:, t], dst[:, t], o[:].rearrange("p (h n) -> p h n", h=HEADS),
                                                     ALU.subtract), f"solve{d}", a, i)
                                emptied(dve, f"solve{d}", a, i)
                    tell(dve, "solved")
                    for t in range(NT):
                        o = full(dve, f"rhs{d}", a, t)
                        free(v.tensor_copy(FY[:, t], o[:].rearrange("p (h n) -> p h n", h=HEADS)), f"rhs{d}", a, t)
                    for t in range(NT):
                        emptied(dve, f"rhs{d}", a, t)
                    if g == 0:
                        step(v.memset(S[:, d], 0.0))
                    tell(dve, "state")
                    sn = 3 if whole else 2
                    for s in range(4):
                        ch = 3 - s if d else s
                        t, half = ch // 2, ch % 2
                        lo = half * CHUNK
                        o = full(dve, f"scan{d}", a, sn * s)
                        rows = slice(lo, lo + CHUNK)
                        free(v.tensor_tensor(VN[rows, half], FY[rows, t], o[rows, :].rearrange("p (h n) -> p h n", h=HEADS),
                                             ALU.subtract), f"scan{d}", a, sn * s)
                        emptied(dve, f"scan{d}", a, sn * s)
                        tell(dve, "vnew")
                        if whole:
                            o = full(dve, f"scan{d}", a, sn * s + 1)
                            oo = OSUM[:, :, ch * CHUNK:(ch + 1) * CHUNK]
                            src = o[:, 0:256].rearrange("p (h n) -> p h n", h=HEADS)
                            free(v.tensor_copy(oo, src) if d == 0 else v.tensor_tensor(oo, oo, src, ALU.add),
                                 f"scan{d}", a, sn * s + 1)
                        o = full(dve, f"scan{d}", a, sn * s + sn - 1)
                        for h in range(HEADS):
                            ins = v.scalar_tensor_tensor(out=S[:, d, h, :], in0=S[:, d, h, :], scalar=DEC[:, t, h, half:half + 1],
                                                         in1=o[:, h * P:(h + 1) * P], op0=ALU.mult, op1=ALU.add)
                            post(ins) if h < HEADS - 1 else free(ins, f"scan{d}", a, sn * s + sn - 1)
                        emptied(dve, f"scan{d}", a, sn * s + sn - 1)
                        tell(dve, "state")
                if whole:
                    tell(dve, "osum")
                    for j in range(2):
                        y = rsqrt("gout", a, j, 512, 1.0 / P, 2048 + j * 512, 4096 + j * 512, 6144 + j * 512)
                        step(v.scalar_tensor_tensor(out=y, in0=y, scalar=VEC[:, V_GN:V_GN + 1], in1=pt(T_Z + 2 * j, 2),
                                                    op0=ALU.mult, op1=ALU.mult))
                        ins = v.tensor_tensor(pt(T_OA + 2 * j, 2), pt(T_OSUM + 2 * j, 2), y, ALU.mult)
                        mark(ins, "branch_a") if j else post(ins)
                lo, n = (0, 5) if whole else (4, 1)
                for j in range(3 if whole else 1):
                    w = min(512, n * T - 512 * j)
                    y = rsqrt("an", a, j, w, 1.0 / HD, 4096 + j * 512, 6144 + j * 512, 8192 + j * 512)
                    at = (T_AQ + lo) * T + j * 512
                    col = V_KN if (not whole or j == 2) else V_QN
                    ins = v.scalar_tensor_tensor(out=PT[:, at:at + w], in0=PT[:, at:at + w], scalar=VEC[:, col:col + 1], in1=y,
                                                 op0=ALU.mult, op1=ALU.mult)
                    step(ins)
                if g:
                    tell(dve, "a_normed")
                    cos, sin = cst[:, C_COS:C_COS + T], cst[:, C_SIN:C_SIN + T]
                    for j in range(3):
                        w = min(512, 5 * T - 512 * j)
                        n2 = w // T
                        o = full(dve, "rope", a, j)
                        free(v.tensor_tensor(f3(4096 + j * 512, n2, T), o[:, 0:w].rearrange("p (a b) -> p a b", b=T),
                                             sin.unsqueeze(1).to_broadcast([P, n2, T]), ALU.mult), "rope", a, j)
                        emptied(dve, "rope", a, j)
                    for j in range(3):
                        n2 = min(2, 5 - 2 * j)
                        q = pt3(T_AQ + 2 * j, n2)
                        step(v.tensor_tensor(q, q, cos.unsqueeze(1).to_broadcast([P, n2, T]), ALU.mult))
                        step(v.tensor_tensor(q, q, f3(4096 + j * 512, n2, T), ALU.add))
                else:
                    tell(dve, "a_normed")
                tell(dve, "a_turned")
                if not whole:
                    continue
                kt = 4 if g else 2
                def normalise(i):
                    n = ATT.index(("s", i))
                    emptied(dve, "att", a, n)
                    step(v.reciprocal(SM[:, 0, 2 + i % 2:3 + i % 2], SM[:, 0, 2 + i % 2:3 + i % 2]))
                    mark(v.tensor_scalar(F[:, (i % 2) * 512:(i % 2) * 512 + kt * P], F[:, (i % 2) * 512:(i % 2) * 512 + kt * P],
                                         SM[:, 0, 2 + i % 2:3 + i % 2], None, ALU.mult), "probs")
                for n, (kind, i) in enumerate(ATT):
                    t, h = i // AHEADS, i % AHEADS
                    if kind == "s":
                        o = full(dve, "att", a, n)
                        if i >= 2:
                            full(dve, "att", a, ATT.index(("p", i - 2)))
                        step(v.tensor_reduce(SM[:, 0, i % 2:i % 2 + 1], o[:, 0:kt * P], AX.X, ALU.max))
                        mark(v.tensor_scalar(SM[:, 0, i % 2:i % 2 + 1], SM[:, 0, i % 2:i % 2 + 1], -(HD ** -0.5), None, ALU.mult),
                             "maxed")
                        normalise(i)
                    elif kind == "o":
                        hp = HD * (h % 2)
                        o = full(dve, "att", a, n)
                        at = (T_OC + h // 2) * T + t * P
                        free(v.tensor_copy(PT[hp:hp + HD, at:at + P], o[hp:hp + HD, 0:P]), "att", a, n)
                        emptied(dve, "att", a, n)
                tell(dve, "att_out")

                def merge(n, i, gate, branch):
                    gb, go = gate
                    bb, bo = branch
                    dve.wait_ge(sem(f"wbfree{gb}"), go + 2)
                    dve.wait_ge(sem(f"wdone{bb}"), bo + 2)
                    if n == 0:
                        v.tensor_tensor(PT[:, bass.ds(i * 512 + T_MIX * T, 512)], F[:, 0:512], wbank[bb][:], ALU.mult).then_inc(
                            sem(f"wbfree{bb}"), 1)
                    else:
                        v.tensor_tensor(F[:, 512:1024], F[:, 0:512], wbank[bb][:], ALU.mult).then_inc(sem(f"wbfree{bb}"), 1)
                        dve.wait_ge(sem(f"wbfree{bb}"), bo + 2)
                        m = PT[:, bass.ds(i * 512 + T_MIX * T, 512)]
                        v.tensor_tensor(m, m, F[:, 512:1024], ALU.add).then_inc(sem("mixstep"), 1)
                        dve.wait_ge(sem("mixstep"), i + (1 + 8 * FULL_INDEX[a] + 4 * (n - 1)))
                    dve.wait_ge(sem(f"wbfree{bb}"), bo + 2)
                    dve.sem_inc(sem("sgfree"), 1)
                branch_chunks(dve, a, merge)
                tell(dve, "mixed")

                def residual(i, b, o):
                    dve.wait_ge(sem(f"wdone{b}"), o + 2)
                    h2 = H[:, g].rearrange("p k n -> p (k n)")
                    gcol = MOD[:, 16:24, :].rearrange("p k n -> p (k n)")
                    for j in range(2):
                        hh = h2[:, bass.ds(i * 512 + j * T, T)]
                        ins = v.scalar_tensor_tensor(out=hh, in0=wbank[b][:, j * T:(j + 1) * T],
                                                     scalar=gcol[:, bass.ds(i * 4 + 2 * j + g, 1)], in1=hh,
                                                     op0=ALU.mult, op1=ALU.add)
                        if j:
                            ins.then_inc(sem(f"wbfree{b}"), 1)
                chunks(dve, "out", a, residual)
                for i in (2, 3):
                    cc = before(WEIGHTS, "out", a, i)
                    dve.wait_ge(sem(f"wbfree{cc % 2}"), cc // 2 + 2)
                tell(dve, "h_mid")
                rs = rsqrt("rms2", a, 0, T, 1.0 / D, 2048, 2304, 2560)
                full(dve, "rms2", a)
                for k in range(KD):
                    ins = v.scalar_tensor_tensor(out=U[:, k, :], in0=H[:, g, k, :], scalar=A12[:, 1, k, g:g + 1],
                                                 in1=rs, op0=ALU.mult, op1=ALU.mult)
                    mark(ins, "scaled2") if k == KD - 1 else post(ins)
                for t in range(NT):
                    sc = F[:, 0:2048].rearrange("p (r n) -> p r n", n=P)
                    s2 = F[:, 2048:4096].rearrange("p (r n) -> p r n", n=P)
                    for j in range(4):
                        o = full(dve, "keys", a, 4 * t + j)
                        free(v.tensor_copy(F[:, j * 512:(j + 1) * 512], o[:]), "keys", a, 4 * t + j)
                    for j in range(4):
                        emptied(dve, "keys", a, 4 * t + j)

                    def top16(vals, spare, best, at, n):
                        for r in range(n):
                            post(v.max(best[:, r, 0:8], vals[:, r, :]))
                        settle()
                        for r in range(n):
                            post(v.max_index(at[:, r, 0:8], best[:, r, 0:8], vals[:, r, :]))
                            post(v.match_replace(spare[:, r, :], best[:, r, 0:8], vals[:, r, :], NEG))
                        settle()
                        for r in range(n):
                            post(v.max(best[:, r, 8:16], spare[:, r, :]))
                        settle()
                        for r in range(n):
                            post(v.max_index(at[:, r, 8:16], best[:, r, 8:16], spare[:, r, :]))
                        settle()

                    top16(sc, s2, TOPV, TOPI, 16)
                    cand = F[:, 4096:6144].rearrange("p (h n) -> p h n", n=256)
                    cand2 = F[:, 6144:8192].rearrange("p (h n) -> p h n", n=256)
                    for h in range(PHEADS):
                        post(v.tensor_tensor(cand[:, h].rearrange("p (x y) -> p x y", x=TOPK), bc(TOPV[:, h, :], TOPK),
                                             TOPV[:, 8 + h, :].unsqueeze(1).to_broadcast([P, TOPK, TOPK]), ALU.add))
                    tif = F[:, 8192:8448].rearrange("p (r n) -> p r n", n=TOPK)
                    step(v.tensor_copy(tif, TOPI[:]))
                    top16(cand, cand2, BV, BJ[:, 0], PHEADS)
                    step(v.tensor_scalar(BJ[:, 1], BJ[:, 0], 4, None, ALU.logical_shift_right))
                    step(v.tensor_scalar(BJ[:, 2], BJ[:, 0], 15, None, ALU.bitwise_and))
                    ab = F[:, 8448:8704].rearrange("p (q n) -> p q n", q=2)
                    step(v.tensor_copy(ab.rearrange("p q n -> p (q n)"), BJ[:, 1:3].rearrange("p q h n -> p (q h n)")))
                    iota = cst[:, C_IOTA:C_IOTA + TOPK].unsqueeze(1).to_broadcast([P, SLOTS, TOPK])
                    pick = F[:, 8704:8960].rearrange("p (q n) -> p q n", q=2)
                    for q in range(2):
                        hot = F[:, 0:2048].rearrange("p (s x) -> p s x", x=TOPK)
                        step(v.tensor_tensor(hot, bc(ab[:, q], TOPK), iota, ALU.is_equal))
                        for h in range(PHEADS):
                            hh = hot[:, h * TOPK:(h + 1) * TOPK, :]
                            post(v.tensor_tensor(hh, hh, tif[:, 8 * q + h, :].unsqueeze(1).to_broadcast([P, TOPK, TOPK]),
                                                 ALU.mult))
                        settle()
                        step(v.tensor_reduce(pick[:, q], hot, AX.X, ALU.add))
                    step(v.tensor_scalar(pick[:, 0], pick[:, 0], float(NKEYS), float(l * EXPERTS), ALU.mult, ALU.add))
                    step(v.tensor_tensor(pick[:, 0], pick[:, 0], pick[:, 1], ALU.add))
                    mark(v.tensor_copy(IDX[:, t, :], pick[:, 0]), "chosen")
                    gt = GATE[:, t, :].rearrange("p (h n) -> p h n", h=PHEADS)
                    mark(v.tensor_tensor(gt, BV[:], BV[:, :, 0:1].to_broadcast([P, PHEADS, TOPK]), ALU.subtract), "best")
                    after(dve, "gate_exp", a, (2, 2, 0, 2), t)
                    step(v.tensor_reduce(PHS[:, 0], gt, AX.X, ALU.add))
                    step(v.reciprocal(PHS[:, 0], PHS[:, 0]))
                    step(v.tensor_tensor(gt, gt, bc(PHS[:, 0], TOPK), ALU.mult))
                after(dve, "query_out", a, FULLP)
                for t in range(NT):
                    n = PEER_TILES.index((a, t))
                    if t:
                        full(dve, "back", a, 2 * t - 1)
                    step(v.memset(ACC[:], 0.0))
                    tell(dve, "acc_clear")
                    with dve.Fori(0, BLOCKS) as i:
                        for b in range(RING):
                            dve.wait_ge(sem(f"urow{b}"), i * 16 + (n * BLOCKS * 16 + 16))
                            v.scalar_tensor_tensor(out=F[:, b * D:(b + 1) * D], in0=ROWU[:, b, :], scalar=1.0, in1=U2[:, t, :], op0=ALU.mult,
                                                   op1=ALU.mult, accum_out=DOT[:, bass.ds(i * RING + b, 1)]).then_inc(
                                                       sem("ufree"), 1)
                        dve.wait_ge(sem("ufree"), i * RING + (n * SLOTS + 3 * RING))
                        dve.sem_inc(sem("dots"), 1)
                        dve.wait_ge(sem("gelu"), i + (n * BLOCKS + 1))
                        v.tensor_tensor(COEF[:], GEL[:], GATE[:, t, bass.ds(i * RING, RING)], ALU.mult).then_inc(sem("coef"), 1)
                        dve.wait_ge(sem("coef"), i + (n * BLOCKS + 1))
                        for b in range(RING):
                            dve.wait_ge(sem(f"vrow{b}"), i * 16 + (n * BLOCKS * 16 + 16))
                            v.scalar_tensor_tensor(out=ACC[:], in0=ROWV[:, b, :], scalar=COEF[:, b:b + 1], in1=ACC[:],
                                                   op0=ALU.mult, op1=ALU.add).then_inc(sem("vfree"), 1)
                            dve.wait_ge(sem("vfree"), i * RING + (n * SLOTS + 2 * RING + b + 1))
                    tell(dve, "retrieved")
                    for j in range(2):
                        o = full(dve, "back", a, 2 * t + j)
                        for k in range(4):
                            kk = 4 * j + k
                            hh = H[:, g, kk, t * P:(t + 1) * P]
                            ins = v.scalar_tensor_tensor(out=hh, in0=o[:, k * P:(k + 1) * P], scalar=MOD[:, 40 + kk, g:g + 1],
                                                         in1=hh, op0=ALU.mult, op1=ALU.add)
                            post(ins) if k < 3 else free(ins, "back", a, 2 * t + j)
                        emptied(dve, "back", a, 2 * t + j)
                tell(dve, "h_done")
            rs = rsqrt("fin", 3, 0, T, 1.0 / D, 2048, 2304, 2560)
            for k in range(KD):
                ins = v.scalar_tensor_tensor(out=U[:, k, :], in0=H[:, 1, k, :], scalar=CVEC[:, 16 + k:17 + k],
                                             in1=rs, op0=ALU.mult, op1=ALU.mult)
                mark(ins, "u3") if k == KD - 1 else post(ins)


FULL_INDEX = {0: 0, 1: 1, 3: 2}
_INS = ["x", "c", "ctx", "c_ctx", "w_mod", "b_mod", "norm1_w", "w_in", "conv_a_w", "a_log", "dt_bias", "gdn_norm_w",
        "conv_b_w", "q_norm_w", "k_norm_w", "w_branch", "w_out", "norm2_w", "w_query", "sub_keys", "expert_u",
        "expert_v", "final_norm_w"]


def kernel(**inputs):
    import concourse.bacc as bacc
    from concourse.bass_utils import run_bass_kernel_spmd

    nc = bacc.Bacc("TRN2", target_bir_lowering=False, num_devices=1)
    arrays = {f"in_{n}": np.ascontiguousarray(inputs[n]) for n in _INS}
    arrays["in_constants"] = constant_table()
    inp = {n[3:]: nc.dram_tensor(n, v.shape, mybir.dt.from_np(v.dtype), kind="ExternalInput").ap()
           for n, v in arrays.items()}
    out = nc.dram_tensor("out_0", (1, T, D), F32, kind="ExternalOutput").ap()
    build(nc, inp, out)
    r = run_bass_kernel_spmd(nc, [arrays], core_ids=[0])
    return r.results[0]["out_0"]
```

```python
from contextlib import ExitStack

import numpy as np

import concourse.bass as bass
from concourse import mybir

F32 = mybir.dt.float32
U32 = mybir.dt.uint32
ALU = mybir.AluOpType
ACT = mybir.ActivationFunctionType
AX = mybir.AxisListType

P = 128
D = 1024
KD = D // P
T = 256
NT = T // P
CHUNK = 64
HEADS = 4
AHEADS, KVHEADS, HD = 8, 2, 64
PHEADS, TOPK, NKEYS = 8, 16, 128
EXPERTS = NKEYS * NKEYS
SLOTS = PHEADS * TOPK
EPS = 1e-6
NEG = -3.0e38
PASSES = [(0, 0, True), (0, 1, True), (1, 0, False), (1, 1, True)]
ALL = range(len(PASSES))

COL_QKV, COL_Z, COL_AB, COL_SC, COL_GATE = 0, 1536, 2048, 2064, 4368
COL_KV = COL_GATE - 256
T_QKV, T_Z, T_BG, T_CG, T_XIN, T_AQ, T_AK = 0, 12, 16, 20, 24, 28, 32
T_OSUM, T_KTOK, T_VTOK = 0, 4, 8
T_MIX = 0
T_SKRAW, T_SKT = 8, 12
T_OB, T_OC, T_OA = T_BG, T_CG, T_XIN
NPT = 34
V_N1, V_N2, V_BMOD, V_CA, V_CB, V_GN, V_QN, V_KN = 0, 8, 16, 64, 100, 112, 113, 114
NV = 115
NAMES = ["ident", "ones", "blk64", "rot", "dup0", "dup1", "tri0", "tri1", "str0", "str1", "chunk",
         "lv0", "lv1", "lv2", "lv3", "lv4", "lv5"]
C_AT = {n: i * P for i, n in enumerate(NAMES)}
C_COS = len(NAMES) * P
C_SIN = C_COS + T
C_IOTA = C_SIN + T
NC_ = C_IOTA + TOPK

RING = 8
BLOCKS = SLOTS // RING
STEPS = 2 * NT * BLOCKS
NBK = 6


def constant_table():
    p, f = np.arange(P)[:, None], np.arange(P)[None, :]
    same = p // CHUNK == f // CHUNK
    m = {"ident": p == f, "ones": p + f >= 0, "blk64": p // HD == f // HD,
         "tri0": same & (p <= f), "tri1": same & (p >= f), "str0": same & (p > f), "str1": same & (p < f),
         "chunk": same}
    for lv in range(6):
        b = 1 << lv
        m[f"lv{lv}"] = (p // (2 * b) == f // (2 * b)) & (p // b != f // b)
    for v in range(KVHEADS):
        m[f"dup{v}"] = p == f % HD + HD * v
    m["rot"] = np.where((f // 16) % 2 == 0, -1.0 * (p == f + 16), 1.0 * (p == f - 16))
    t = np.arange(T)
    freq = np.float32(10000.0) ** (-np.arange(16, dtype=np.float32) / 16)
    ch = np.arange(P) % HD
    pos = np.where((ch // 32)[:, None] == 0, (t // 64)[None, :], (t % 64)[None, :]).astype(np.float32)
    ang = pos * freq[ch % 16][:, None]
    cols = [m[n].astype(np.float32) for n in NAMES] + [np.cos(ang), np.sin(ang),
                                                      np.tile(np.arange(TOPK, dtype=np.float32), (P, 1))]
    return np.ascontiguousarray(np.concatenate(cols, 1).astype(np.float32))


SOLVE = [("x", 0)] + [(k, lv) for lv in range(1, 5) for k in "xut"] + [("x", 5), ("u", 5)]
ATT = [("s", 0)] + [j for i in range(NT * AHEADS)
                    for j in ([("s", i + 1)] if i + 1 < NT * AHEADS else []) + [("p", i), ("o", i)]]


def direction(d):
    return [(f"decay{d}", (2, 2, 2, 2)), (f"gram{d}", (2, 2, 2, 2)), (f"qk{d}", (2, 2, 0, 2)),
            (f"solve{d}", (2 * len(SOLVE),) * 4), (f"rhs{d}", (4, 4, 4, 4)), (f"scan{d}", (12, 12, 8, 12))]


PRODUCTS = [("x_in", (8, 0, 0, 0)), ("cond", (1, 0, 0, 0)), ("vecs", (1, 0, 1, 0)), ("modt", (1, 0, 1, 0)), ("rms1", (1, 1, 1, 1)),
            ("ab", (1, 1, 1, 1)), ("cum", (1, 1, 1, 1)), ("l2", (4, 4, 2, 4)), ("tok", (4, 4, 4, 4)),
            *direction(0), *direction(1), ("gout", (2, 2, 0, 2)), ("an", (3, 3, 1, 3)), ("rope", (0, 3, 0, 3)),
            ("dup", (1, 1, 1, 1)), ("vtok", (1, 1, 1, 1)), ("att", (len(ATT), len(ATT), 0, len(ATT))),
            ("back", (0, 4, 4, 0)), ("rms2", (1, 1, 0, 1)), ("u2t", (4, 4, 0, 4)), ("skt", (2, 2, 0, 2)), ("keys", (8, 8, 0, 8)),
            ("back_last", (0, 0, 0, 4)), ("fin", (0, 0, 0, 1)), ("out", (0, 0, 0, 4))]
ROOTS = [(n, dict(PRODUCTS)[n]) for n in ("rms1", "l2", "gout", "an", "rms2", "fin")]
WEIGHTS = [("mod", (24, 0, 24, 0)), ("qkvz", (8, 8, 4, 8)), ("rest", (9, 9, 1, 9)), ("merge", (24, 24, 0, 24)),
           ("out", (4, 4, 0, 4)), ("query", (4, 4, 0, 4))]


def before(series, stage, a, i=0):
    names = [n for n, _ in series]
    k = dict(series)
    assert i < k[stage][a], (stage, a, i)
    return sum(sum(c[:a]) for _, c in series) + sum(k[n][a] for n in names[:names.index(stage)]) + i


EARLY = 6
OWN = 8
DIRS = [f"{k}{d}{i}" for d in range(2) for k, n in (("prep", 1), ("solve", 6), ("scan", 4)) for i in range(n)]
SERVE = {1: [("proj", 6), ("gates", 3), ("l2", 1), ("cols", 1), *[(x, 1) for x in DIRS], ("gout", 1),
             *[(f"att{i}", 1) for i in range(2, 8)], ("merge0", 4), ("merge1", 4), ("merge2", 4), ("rest", 4)],
         2: [("mod", 8), ("proj", 2), ("gates", 1), ("l2", 1), ("cols", 1), *[(x, 1) for x in DIRS], ("gout", 1), ("rest", 20)]}
assert all(OWN + sum(n for _, n in v) == STEPS for v in SERVE.values())


def served(a, point):
    if point.startswith("own"):
        return int(point[3:]), int(point[3:]) + 1
    if a == 4:
        return OWN, STEPS
    lo = OWN
    for name, n in SERVE.get(a, []):
        if name == point:
            return lo, lo + n
        lo += n
    return 0, 0


def segments(lo, hi):
    while lo < hi:
        seg = lo // BLOCKS
        top = min(hi, (seg + 1) * BLOCKS)
        yield seg // 2, seg % 2, lo % BLOCKS, top - seg * BLOCKS
        lo = top


PEER_TILES = [(a, t) for a in ALL if PASSES[a][2] for t in range(NT)]


def build(nc, inp, out):
    with ExitStack() as ctx:
        def sb(name, shape, dt=F32):
            return ctx.enter_context(nc.sbuf_tensor(name, shape, dt))

        sems = {}

        def sem(name):
            if name not in sems:
                sems[name] = ctx.enter_context(nc.semaphore("s_" + name))
            return sems[name]

        cst = sb("cst", [P, NC_])
        H = sb("H", [P, 2, KD, T])
        U = sb("U", [P, KD, T])
        W = sb("W", [P, 2, KD * 256])
        PT = sb("PT", [P, NPT * T])
        QC = sb("QC", [P, 12, T])
        S = sb("S", [P, 2, HEADS, P])
        VN = sb("VN", [P, 2, HEADS, P])
        KDUP = sb("KDUP", [P, KVHEADS, 2 * T])
        VV = sb("VV", [P, 2 * NT, P])
        F = sb("F", [P, 10240])
        ROW = sb("ROW", [P, RING, D])
        U2 = sb("U2", [P, NT, D])
        ACC = sb("ACC", [P, NT, D])
        IDX = sb("IDX", [P, NT, SLOTS], U32)
        IXC = sb("IXC", [P, 2, RING], U32)
        GATE = sb("GATE", [P, NT, SLOTS])
        DOT = sb("DOT", [P, SLOTS])
        COEF = sb("COEF", [P, SLOTS])
        VROW = sb("VROW", [NV, P])
        VEC = sb("VEC", [P, NV])
        MOD = sb("MOD", [P, 2, 48, 2])
        A12 = sb("A12", [P, 2, KD, 2])
        CROW = sb("CROW", [24, P])
        CVEC = sb("CVEC", [P, 24])
        WAB = sb("WAB", [P, KD, 16])
        ADT = sb("ADT", [P, 2, 8])
        AB = sb("AB", [P, NT, 16])
        GB = sb("GB", [P, NT, 16])
        GC = sb("GC", [P, NT, 16])
        EGC = sb("EGC", [P, NT, 16])
        BEG = sb("BEG", [P, NT, 8])
        TMPC = sb("TMPC", [P, NT, 16])
        DEC = sb("DEC", [P, NT, HEADS, 2])
        SM = sb("SM", [P, 2, 4])
        TOPV = F[:, 8960:9216].rearrange("p (r n) -> p r n", n=TOPK)
        TOPI = F[:, 9216:9472].bitcast(U32).rearrange("p (r n) -> p r n", n=TOPK)
        BV = F[:, 9472:9600].rearrange("p (h n) -> p h n", n=TOPK)
        BJ = F[:, 9600:9984].bitcast(U32).rearrange("p (q h n) -> p q h n", q=3, n=TOPK)
        PHS = sb("PHS", [P, 2, PHEADS])
        bank = [ctx.enter_context(nc.psum_tensor(f"bank{i}", [P, 512], F32)) for i in range(NBK)]
        wbank = [ctx.enter_context(nc.psum_tensor(f"wbank{i}", [P, 512], F32)) for i in range(2)]

        def c(name):
            return cst[:, C_AT[name]:C_AT[name] + P]

        def pt(t, n=1):
            return PT[:, t * T:(t + n) * T]

        def pt3(t, n, w=T):
            return PT[:, t * T:(t + n) * T].rearrange("p (a b) -> p a b", b=w)

        def f3(lo, n, w):
            return F[:, lo:lo + n * w].rearrange("p (a b) -> p a b", b=w)

        FA, FQ, FT, FU, FX, FW, FK, FD, FVB, FKB = [F[:, i * 1024:(i + 1) * 1024].rearrange(
            "p (t h n) -> p t h n", t=NT, h=HEADS) for i in range(10)]
        FY = FT
        KTOK = PT[:, T_KTOK * T:(T_KTOK + 4) * T].rearrange("p (t h n) -> p t h n", t=NT, h=HEADS)
        VTOK = PT[:, T_VTOK * T:(T_VTOK + 4) * T].rearrange("p (t h n) -> p t h n", t=NT, h=HEADS)
        OSUM = pt3(T_OSUM, 4)
        SKT = PT[:, T_SKT * T:(T_SKT + 4) * T].rearrange("p (h n) -> p h n", h=PHEADS)
        SKRAW = PT[:, T_SKRAW * T:(T_SKRAW + 4) * T].rearrange("p (h n) -> p h n", h=PHEADS)

        def spot(stage, a, i=0):
            n = before(PRODUCTS, stage, a, i)
            return n % NBK, n // NBK

        def full(eng, stage, a, i=0):
            b, o = spot(stage, a, i)
            eng.wait_ge(sem(f"full{b}"), o + 1)
            return bank[b]

        def free(ins, stage, a, i=0):
            ins.then_inc(sem(f"free{spot(stage, a, i)[0]}"), 1)

        def emptied(eng, stage, a, i=0):
            b, o = spot(stage, a, i)
            eng.wait_ge(sem(f"free{b}"), o + 2)

        seen = {}

        def mark(ins, name, k=1):
            ins.then_inc(sem(name), 1)
            seen[name] = seen.get(name, 0) + 1

        def tell(eng, name):
            eng.sem_inc(sem(name), 1)
            seen[name] = seen.get(name, 0) + 1

        def nth(name, a, per=(1, 1, 1, 1), i=0):
            return sum(per[:a]) + i + 1

        FULLP = (1, 1, 0, 1)

        def after(eng, name, a, per=(1, 1, 1, 1), i=0):
            eng.wait_ge(sem(name), nth(name, a, per, i))

        def chunks(eng, stage, a, body, lo=0, hi=None):
            n = min(dict(WEIGHTS)[stage][a], hi or 99) - lo
            if n <= 0:
                return
            c0 = before(WEIGHTS, stage, a, lo)
            if n // 2:
                with eng.Fori(0, n // 2) as i:
                    for j in range(2):
                        body(i * 2 + (lo + j), (c0 + j) % 2, i + (c0 + j) // 2)
            if n % 2:
                body(lo + n - 1, (c0 + n - 1) % 2, (c0 + n - 1) // 2)

        def branch_chunks(eng, a, body):
            c0 = before(WEIGHTS, "merge", a)
            for n in range(3):
                with eng.Fori(0, 4) as i:
                    s = c0 + 8 * n
                    body(n, i, (s % 2, s // 2 + i), ((s + 1) % 2, (s + 1) // 2 + i))

        def last_block(a, t, table, blk):
            return (PEER_TILES.index((a, t)) * 2 + table) * BLOCKS + blk

        block = ctx.enter_context(nc.Block())

        @block.sync
        def _(sp):
            sp.dma_start(cst[:], inp["constants"]).then_inc(sem("loaded"), 16)
            for t in range(NT):
                sp.dma_start(ROW[:, t, :], inp["ctx"][0, t * P:(t + 1) * P, :]).then_inc(sem("loaded"), 16)
                sp.dma_start(ROW[:, NT + t, :], inp["x"][0, t * P:(t + 1) * P, :]).then_inc(sem("loaded"), 16)
            sp.dma_start(CROW[0:8, :], inp["c_ctx"].rearrange("(a b) -> a b", b=P)).then_inc(sem("loaded"), 16)
            sp.dma_start(CROW[8:16, :], inp["c"][0].rearrange("(a b) -> a b", b=P)).then_inc(sem("loaded"), 16)
            sp.dma_start(CROW[16:24, :], inp["final_norm_w"].rearrange("(a b) -> a b", b=P)).then_inc(
                sem("loaded"), 16)

            def vectors(a, l):
                if a:
                    full(sp, "vecs", a - 2)
                    after(sp, "gates_made", a - 1)
                    full(sp, "ab", a - 1)
                rows = [(V_N1, 8, inp["norm1_w"][l]), (V_N2, 8, inp["norm2_w"][l]), (V_BMOD, 48, inp["b_mod"][l]),
                        (V_GN, 1, inp["gdn_norm_w"][l])]
                for at, n, src in rows:
                    sp.dma_start(VROW[at:at + n, :], src.rearrange("(a b) -> a b", b=P)).then_inc(sem("vectors"), 16)
                for j in range(3):
                    sp.dma_start(VROW[V_CA + 12 * j:V_CA + 12 * j + 12, :],
                                 inp["conv_a_w"][l, j].rearrange("(a b) -> a b", b=P)).then_inc(sem("vectors"), 16)
                    sp.dma_start(VROW[V_CB + 4 * j:V_CB + 4 * j + 4, :],
                                 inp["conv_b_w"][l, j].rearrange("(a b) -> a b", b=P)).then_inc(sem("vectors"), 16)
                for at, src in ((V_QN, inp["q_norm_w"]), (V_KN, inp["k_norm_w"])):
                    for half in range(2):
                        sp.dma_start(VROW[at:at + 1, half * HD:(half + 1) * HD], src[l:l + 1, :]).then_inc(
                            sem("vectors"), 16)
                for j, name in enumerate(("a_log", "dt_bias")):
                    sp.dma_start(ADT[:, j, :], inp[name][l:l + 1].rearrange("o a b -> o (a b)").to_broadcast(
                        [P, 8])).then_inc(sem("vectors"), 16)
                sp.dma_start(WAB[:], inp["w_in"][l, :, COL_AB:COL_SC].rearrange("(k p) n -> p k n", p=P)).then_inc(
                    sem("vectors"), 16)

            def load(src, col):
                v = src.rearrange("(k p) n -> p k n", p=P)

                def body(i, b, o):
                    sp.wait_ge(sem(f"wdone{b}"), o + 1)
                    sp.sem_inc(sem("sp_hold"), 1)
                    sp.dma_start(W[:, b, :].rearrange("p (k n) -> p k n", k=KD), v[:, :, bass.ds(i * 256 + col, 256)]
                                 ).then_inc(sem(f"wload{b}"), 16)
                return body

            for a, (l, g, whole) in enumerate(PASSES):
                if g == 0:
                    vectors(a, l)
                    chunks(sp, "mod", a, load(inp["w_mod"][l], 0))
                chunks(sp, "qkvz", a, load(inp["w_in"][l], 0 if whole else 512))
                chunks(sp, "rest", a, load(inp["w_in"][l], COL_SC if whole else COL_KV))
                if not whole:
                    continue
                gates = inp["w_in"][l].rearrange("(k p) n -> p k n", p=P)

                def merge(n, i, gate, branch):
                    b, o = gate
                    sp.wait_ge(sem(f"wdone{b}"), o + 1)
                    sp.sem_inc(sem("sp_hold"), 1)
                    sp.dma_start(W[:, b, :].rearrange("p (k n) -> p k n", k=KD),
                                 gates[:, :, bass.ds(i * 256 + COL_GATE + n * D, 256)]).then_inc(sem(f"wload{b}"), 16)
                    b, o = branch
                    sp.wait_ge(sem(f"wdone{b}"), o + 1)
                    sp.sem_inc(sem("sp_hold"), 1)
                    wb = inp["w_branch"][l, n].rearrange("(k p) n -> p k n", p=P)
                    sp.dma_start(W[:, b, 0:1024].rearrange("p (k n) -> p k n", k=4), wb[:, :, bass.ds(i * 256, 256)]
                                 ).then_inc(sem(f"wload{b}"), 16)
                branch_chunks(sp, a, merge)
                chunks(sp, "out", a, load(inp["w_out"][l], 0))
                after(sp, "branch_a", a, FULLP)
                after(sp, "mixed", a, FULLP)
                sp.dma_start(SKRAW.rearrange("p h (q k) -> p h q k", q=2),
                             inp["sub_keys"][l].rearrange("h q n k -> n h q k")).then_inc(sem("subkeys"), 16)
                chunks(sp, "query", a, load(inp["w_query"][l], 0))
            after(sp, "result", 0)
            sp.dma_start(out[0].rearrange("(t p) d -> p t d", p=P), U2[:]).then_inc(sem("stored"), 16)
            sp.wait_ge(sem("stored"), 16)

        @block.gpsimd
        def _(pool):
            tables = [inp["expert_u"].rearrange("l e d -> (l e) d"), inp["expert_v"].rearrange("l e d -> (l e) d")]
            for a, t in PEER_TILES:
                after(pool, "chosen", a, (2, 2, 0, 2), t)
                if (a, t) == PEER_TILES[0]:
                    after(pool, "x_read", 0)
                for kind, table in enumerate(tables):
                    with pool.Fori(0, BLOCKS // 2) as it:
                        for half in range(2):
                            blk = it * 2 + (last_block(a, t, kind, 0) + half)
                            pool.wait_ge(sem("rowfree"), blk * RING + RING)
                            pool.sem_inc(sem("pool_hold"), 1)
                            pool.tensor_copy(IXC[:, half, :], IDX[:, t, bass.ds(it * 2 * RING + half * RING, RING)]
                                             ).then_inc(sem("idxcol"), 1)
                            pool.wait_ge(sem("idxcol"), blk + 1)
                            pool.sem_inc(sem("pool_hold"), 1)
                            for b in range(RING):
                                pool.wait_ge(sem("rowfree"), blk * RING + (RING + b + 1))
                                pool.sem_inc(sem("pool_hold"), 1)
                                pool.indirect_dma_start(ROW[:, b, :], None, table, bass.IndirectOffsetOnAxis(
                                    ap=IXC[:, half, b:b + 1], axis=0)).then_inc(sem(f"row{b}"), 16)

        @block.tensor
        def _(pe):
            for b in range(NBK):
                pe.sem_inc(sem(f"free{b}"), 1)
            for b in range(2):
                pe.sem_inc(sem(f"wbfree{b}"), 1)
                pe.sem_inc(sem(f"wdone{b}"), 1)
            order = []

            def empty(stage, a, i=0):
                b, o = spot(stage, a, i)
                assert b == len(order) % NBK and o == len(order) // NBK, (stage, a, i, len(order))
                order.append(1)
                pe.wait_ge(sem(f"free{b}"), o + 1)
                return bank[b]

            def filled(ins, stage, a, i=0):
                ins.then_inc(sem(f"full{spot(stage, a, i)[0]}"), 1)

            def mm(o, l, r, start=True, stop=True):
                return pe.matmul(o, l, r, start=start, stop=stop)

            def weight_product(rhs, kn, n):
                def body(i, b, o):
                    pe.wait_ge(sem(f"wload{b}"), o * 16 + 16)
                    pe.wait_ge(sem(f"wbfree{b}"), o + 1)
                    w = W[:, b, 0:kn * 256].rearrange("p (k n) -> p k n", k=kn)
                    for h in range(2):
                        for k in range(kn):
                            ins = mm(wbank[b][:, h * n:(h + 1) * n], w[:, k, h * P:(h + 1) * P], rhs(k),
                                     k == 0, k == kn - 1)
                    ins.then_inc(sem(f"wdone{b}"), 1)
                return body

            def sum_channels(stage, a, lhs, rhs, n, i=0):
                o = empty(stage, a, i)
                for k in range(n):
                    ins = mm(o[:, 0:T], lhs, rhs(k), k == 0, k == n - 1)
                filled(ins, stage, a, i)

            def back(a, stage, src):
                after(pe, "retrieved", src, FULLP)
                for j in range(2 * NT):
                    o = empty(stage, a, j)
                    for k in range(4):
                        at = ((j % 2) * 4 + k) * P
                        ins = pe.transpose(o[:, k * P:(k + 1) * P], ACC[:, j // 2, at:at + P], c("ident"))
                    filled(ins, stage, a, j)

            for a, (l, g, whole) in enumerate(PASSES):
                if a == 0:
                    pe.wait_ge(sem("loaded"), 16 * 8)
                    for j in range(8):
                        o = empty("x_in", a, j)
                        for k in range(4):
                            ins = pe.transpose(o[:, k * P:(k + 1) * P],
                                               ROW[:, j // 2, ((j % 2) * 4 + k) * P:((j % 2) * 4 + k + 1) * P], c("ident"))
                        filled(ins, "x_in", a, j)
                    o = empty("cond", a)
                    filled(pe.transpose(o[:, 0:24], CROW[:], cst[0:24, 0:24]), "cond", a)
                if g == 0:
                    pe.wait_ge(sem("vectors"), 16 * 17 * (l + 1))
                    o = empty("vecs", a)
                    filled(pe.transpose(o[:, 0:NV], VROW[:], cst[0:NV, 0:NV]), "vecs", a)
                    after(pe, "cond_ready", 0)

                    def mod(i, b, o):
                        pe.wait_ge(sem(f"wload{b}"), o * 16 + 16)
                        pe.wait_ge(sem(f"wbfree{b}"), o + 1)
                        for k in range(KD):
                            ins = mm(wbank[b][0:2, 0:256], CVEC[:, k:16:8], W[:, b, k * 256:(k + 1) * 256], k == 0, k == KD - 1)
                        ins.then_inc(sem(f"wdone{b}"), 1)
                    chunks(pe, "mod", a, mod)
                    after(pe, "mod_rows", a, (1, 0, 1, 0))
                    o = empty("modt", a)
                    for k in range(48):
                        ins = mm(o[:, 2 * k:2 * k + 2], PT[0:2, k * P:(k + 1) * P], cst[0:2, 0:2])
                    filled(ins, "modt", a)
                after(pe, "sq1", a)
                sum_channels("rms1", a, c("ones"), lambda k: F[:, k * T:(k + 1) * T], KD)
                after(pe, "u1", a)
                chunks(pe, "qkvz", a, weight_product(lambda k: U[:, k, :], KD, T))
                o = empty("ab", a)
                for t in range(NT):
                    for k in range(KD):
                        ins = mm(o[:, t * 16:(t + 1) * 16], U[:, k, t * P:(t + 1) * P], WAB[:, k, :], k == 0, k == KD - 1)
                filled(ins, "ab", a)
                chunks(pe, "rest", a, weight_product(lambda k: U[:, k, :], KD, T), 0, EARLY)
                after(pe, "gates_made", a)
                o = empty("cum", a)
                for t in range(NT):
                    for d in range(2):
                        mm(o[:, t * 16 + 4 * d:t * 16 + 4 * d + 4], c(f"tri{d}"), GB[:, t, 4 * d:4 * d + 4])
                    ins = mm(o[:, t * 16 + 8:t * 16 + 16], c("chunk"), GB[:, t, 0:8])
                filled(ins, "cum", a)
                after(pe, "sq_l2", a)
                n2 = 4 if whole else 2
                for j in range(n2):
                    o = empty("l2", a, j)
                    filled(mm(o[:], c("ones"), F[:, (j + 4 - n2) * 512:(j + 5 - n2) * 512]), "l2", a, j)
                chunks(pe, "rest", a, weight_product(lambda k: U[:, k, :], KD, T), EARLY)
                after(pe, "qk_normed", a)
                for j in range(4):
                    o = empty("tok", a, j)
                    for h in range(HEADS):
                        ins = pe.transpose(o[:, h * P:(h + 1) * P],
                                           QC[:, 4 + 4 * (j // 2) + h, (j % 2) * P:(j % 2 + 1) * P], c("ident"))
                    filled(ins, "tok", a, j)
                for d in range(2):
                    for t in range(NT):
                        o = empty(f"decay{d}", a, t)
                        for h in range(HEADS):
                            ins = mm(o[:, h * P:(h + 1) * P],
                                     GB[:, t, 4 * d + h:4 * d + h + 1].to_broadcast([P, P]), c(f"tri{d}"))
                        filled(ins, f"decay{d}", a, t)
                    for t in range(NT):
                        o = empty(f"gram{d}", a, t)
                        for h in range(HEADS):
                            k = QC[:, 4 + h, t * P:(t + 1) * P]
                            ins = mm(o[:, h * P:(h + 1) * P], k, k)
                        filled(ins, f"gram{d}", a, t)
                    if whole:
                        for t in range(NT):
                            o = empty(f"qk{d}", a, t)
                            for h in range(HEADS):
                                ins = mm(o[:, h * P:(h + 1) * P], QC[:, 4 + h, t * P:(t + 1) * P],
                                         QC[:, h, t * P:(t + 1) * P])
                            filled(ins, f"qk{d}", a, t)
                    for n, (kind, lv) in enumerate(SOLVE):
                        for t in range(NT):
                            i = 2 * n + t
                            if kind == "x":
                                after(pe, "level", a, (24,) * 4, 12 * d + 2 * lv + t)
                            elif kind == "u":
                                after(pe, "x_out", a, (24,) * 4, 12 * d + 2 * lv + t)
                            o = empty(f"solve{d}", a, i)
                            for h in range(HEADS):
                                if kind == "x":
                                    r = c("ident") if lv == 0 else FU[:, t, h, :]
                                    ins = mm(o[:, h * P:(h + 1) * P], FW[:, t, h, :], r)
                                elif kind == "u":
                                    ins = mm(o[:, h * P:(h + 1) * P], FT[:, t, h, :], FX[:, t, h, :])
                                else:
                                    ins = mm(o[:, h * P:(h + 1) * P], FX[:, t, h, :], FT[:, t, h, :])
                            filled(ins, f"solve{d}", a, i)
                    after(pe, "solved", a, (2,) * 4, d)
                    after(pe, "rhs_in", a, (2,) * 4, d)
                    after(pe, "rhs_v", a, (2,) * 4, d)
                    for t in range(NT):
                        o = empty(f"rhs{d}", a, t)
                        for h in range(HEADS):
                            ins = mm(o[:, h * P:(h + 1) * P], FU[:, t, h, :], FVB[:, t, h, :])
                        filled(ins, f"rhs{d}", a, t)
                    for t in range(NT):
                        o = empty(f"rhs{d}", a, 2 + t)
                        for h in range(HEADS):
                            ins = mm(o[:, h * P:(h + 1) * P], FKB[:, t, h, :], FU[:, t, h, :])
                        filled(ins, f"rhs{d}", a, 2 + t)
                    after(pe, "w_out", a, (2,) * 4, d)
                    step = 3 if whole else 2
                    for s in range(4):
                        ch = 3 - s if d else s
                        t, half = ch // 2, ch % 2
                        after(pe, "state", a, (10,) * 4, 5 * d + s)
                        o = empty(f"scan{d}", a, step * s)
                        for h in range(HEADS):
                            ins = mm(o[:, h * P:(h + 1) * P], FW[:, t, h, :], S[:, d, h, :])
                        filled(ins, f"scan{d}", a, step * s)
                        after(pe, "vnew", a, (8,) * 4, 4 * d + s)
                        if whole:
                            o = empty(f"scan{d}", a, step * s + 1)
                            lo = half * CHUNK
                            for h in range(HEADS):
                                mm(o[:, h * CHUNK:(h + 1) * CHUNK], S[:, d, h, :], FD[:, t, h, lo:lo + CHUNK], True, False)
                                ins = mm(o[:, h * CHUNK:(h + 1) * CHUNK], VN[:, half, h, :], FQ[:, t, h, lo:lo + CHUNK],
                                         False, True)
                            filled(ins, f"scan{d}", a, step * s + 1)
                        o = empty(f"scan{d}", a, step * s + step - 1)
                        for h in range(HEADS):
                            ins = mm(o[:, h * P:(h + 1) * P], FK[:, t, h, :], VN[:, half, h, :])
                        filled(ins, f"scan{d}", a, step * s + step - 1)
                if whole:
                    after(pe, "sq_g", a, FULLP)
                    for j in range(2):
                        o = empty("gout", a, j)
                        filled(mm(o[:], c("ones"), F[:, j * 512:(j + 1) * 512]), "gout", a, j)
                after(pe, "sq_a", a)
                lo, n = (0, 5) if whole else (4, 1)
                for j in range(3 if whole else 1):
                    w = min(512, n * T - 512 * j)
                    o = empty("an", a, j)
                    filled(mm(o[:, 0:w], c("blk64"), F[:, 2048 + lo * T + j * 512:2048 + lo * T + j * 512 + w]), "an", a, j)
                if g == 1:
                    after(pe, "a_normed", a)
                    for j in range(3):
                        w = min(512, 5 * T - 512 * j)
                        o = empty("rope", a, j)
                        filled(mm(o[:, 0:w], c("rot"), PT[:, T_AQ * T + j * 512:T_AQ * T + j * 512 + w]), "rope", a, j)
                after(pe, "a_turned", a)
                o = empty("dup", a)
                for v in range(KVHEADS):
                    ins = mm(o[:, v * T:(v + 1) * T], c(f"dup{v}"), pt(T_AK))
                filled(ins, "dup", a)
                o = empty("vtok", a)
                for t in range(NT):
                    ins = pe.transpose(o[:, t * P:(t + 1) * P], PT[:, (T_AK + 1) * T + t * P:(T_AK + 1) * T + (t + 1) * P],
                                       c("ident"))
                filled(ins, "vtok", a)
                if not whole:
                    back(a, "back", a - 1)
                    continue
                after(pe, "kv_ready", a)
                k0, kt = (0, 4) if g else (2, 2)
                for n, (kind, i) in enumerate(ATT):
                    t, h = i // AHEADS, i % AHEADS
                    hp = HD * (h % 2)
                    o = empty("att", a, n) if kind != "p" else None
                    if kind == "s":
                        ins = mm(o[:, 0:kt * P], PT[hp:hp + HD, (T_AQ + h // 2) * T + t * P:(T_AQ + h // 2) * T + (t + 1) * P],
                                 KDUP[hp:hp + HD, h // 4, k0 * P:(k0 + kt) * P])
                    elif kind == "p":
                        after(pe, "probs", a, (16, 16, 0, 16), i)
                        o = empty("att", a, n)
                        for k in range(kt):
                            ins = pe.transpose(o[:, k * P:(k + 1) * P], F[:, (i % 2) * 512 + k * P:(i % 2) * 512 + (k + 1) * P],
                                               c("ident"))
                    else:
                        after(pe, "probs_t", a, (16, 16, 0, 16), i)
                        for k in range(kt):
                            ins = mm(o[hp:hp + HD, 0:P], VV[:, k0 + k, (h // 4) * HD:(h // 4 + 1) * HD],
                                     F[:, 1024 + (i % 2) * 512 + k * P:1024 + (i % 2) * 512 + (k + 1) * P],
                                     k == 0, k == kt - 1)
                    filled(ins, "att", a, n)
                after(pe, "att_out", a, FULLP)

                def merge(n, i, gate, branch):
                    weight_product(lambda k: U[:, k, :], KD, T)(i, *gate)
                    src = (T_OA, T_OB, T_OC)[n]
                    weight_product(lambda k: pt(src + k), 4, T)(i, *branch)
                branch_chunks(pe, a, merge)
                after(pe, "mixed", a, FULLP)
                chunks(pe, "out", a, weight_product(lambda k: pt(T_MIX + k), KD, T))
                if a == 1:
                    back(a, "back", 0)
                after(pe, "sq2", a, FULLP)
                sum_channels("rms2", a, c("ones"), lambda k: F[:, k * T:(k + 1) * T], KD)
                after(pe, "u2", a, FULLP)
                for j in range(4):
                    o = empty("u2t", a, j)
                    for k in range(4):
                        ins = pe.transpose(o[:, k * P:(k + 1) * P], U[:, (j % 2) * 4 + k, (j // 2) * P:(j // 2 + 1) * P],
                                           c("ident"))
                    filled(ins, "u2t", a, j)
                pe.wait_ge(sem("subkeys"), 16 * nth("subkeys", a, FULLP))
                for j in range(2):
                    o = empty("skt", a, j)
                    for k in range(4):
                        ins = pe.transpose(o[:, k * P:(k + 1) * P], SKRAW[:, 4 * j + k, :], c("ident"))
                    filled(ins, "skt", a, j)
                chunks(pe, "query", a, weight_product(lambda k: U[:, k, :], KD, T))
                after(pe, "query_out", a, FULLP)
                for j in range(8):
                    t, q, hb = j // 4, (j // 2) % 2, j % 2
                    o = empty("keys", a, j)
                    for h in range(4):
                        hh = 4 * hb + h
                        ins = mm(o[:, h * P:(h + 1) * P], PT[HD * q:HD * q + HD, (16 + hh) * T + t * P:(16 + hh) * T + (t + 1) * P],
                                 SKT[HD * q:HD * q + HD, hh, :])
                    filled(ins, "keys", a, j)
            back(3, "back_last", 3)
            a = 3
            after(pe, "sq3", 0)
            sum_channels("fin", a, c("ones"), lambda k: F[:, k * T:(k + 1) * T], KD)
            after(pe, "u3", 0)
            for j in range(4):
                o = empty("out", a, j)
                for k in range(4):
                    ins = pe.transpose(o[:, k * P:(k + 1) * P], U[:, (j % 2) * 4 + k, (j // 2) * P:(j // 2 + 1) * P], c("ident"))
                filled(ins, "out", a, j)

        @block.scalar
        def _(act):
            own = [0]

            def A(o, i, f=ACT.Copy, **k):
                return nc.scalar.activation(o, i, f, **k)

            def link(ins):
                own[0] += 1
                ins.then_inc(sem("act_step"), 1)

            def settle():
                act.wait_ge(sem("act_step"), own[0])

            def root(stage, a, i=0):
                n = before(ROOTS, stage, a, i)
                act.wait_ge(sem("var"), n + 1)

            def root_of(dst, src):
                link(A(dst, src, ACT.Ln))
                settle()
                A(dst, dst, ACT.Exp, scale=-0.5).then_inc(sem("root"), 1)

            def move(dst, w=512, first=0):
                def body(i, b, o):
                    act.wait_ge(sem(f"wdone{b}"), o + 2)
                    act.sem_inc(sem("act_hold"), 1)
                    A(dst(i, w), wbank[b][:, 0:w]).then_inc(sem(f"wbfree{b}"), 1)
                return body

            def moved(stage, a, hi=99):
                n = min(hi, dict(WEIGHTS)[stage][a])
                for i in range(max(0, n - 2), n):
                    cc = before(WEIGHTS, stage, a, i)
                    act.wait_ge(sem(f"wbfree{cc % 2}"), cc // 2 + 2)

            def serve(a, point):
                for t, kind, lo, hi in segments(*served(a, point)):
                    if kind == 0 and hi == BLOCKS:
                        src = min(a - 1, 3)
                        after(act, "dots", src, (2, 2, 0, 2), t)
                        mark(A(COEF[:], DOT[:], ACT.Gelu), "gelu")

            for a, (l, g, whole) in enumerate(PASSES):
                if a == 0:
                    for j in range(8):
                        o = full(act, "x_in", a, j)
                        gi, t, hf = j // 4, (j // 2) % 2, j % 2
                        free(A(H[:, gi, 4 * hf:4 * hf + 4, t * P:(t + 1) * P], o[:].rearrange("p (k n) -> p k n", k=4)),
                             "x_in", a, j)
                    o = full(act, "cond", a)
                    link(A(CVEC[:, 16:24], o[:, 16:24]))
                    free(A(CVEC[:, 0:16], o[:, 0:16], ACT.Silu), "cond", a)
                    emptied(act, "cond", a)
                    settle()
                    tell(act, "x_read")
                    tell(act, "cond_ready")
                if a:
                    after(act, "pass_over", a - 1)
                if g == 0:
                    o = full(act, "vecs", a)
                    free(A(VEC[:], o[:, 0:NV]), "vecs", a)

                    def mod(i, b, o):
                        act.wait_ge(sem(f"wdone{b}"), o + 2)
                        act.sem_inc(sem("act_hold"), 1)
                        A(PT[0:2, bass.ds(i * 256, 256)], wbank[b][0:2, 0:256]).then_inc(sem(f"wbfree{b}"), 1)
                    chunks(act, "mod", a, mod)
                    serve(a, "mod")
                    moved("mod", a)
                    tell(act, "mod_rows")
                if a == 0:
                    for j in range(2, 8):
                        emptied(act, "x_in", a, j)
                mark(A(F[:, 0:KD * T], H[:, g].rearrange("p k n -> p (k n)"), ACT.Square), "sq1")
                root("rms1", a)
                root_of(F[:, 2304:2560], F[:, 2048:2304])
                after(act, "scaled1", a)
                for k in range(KD):
                    ins = A(U[:, k, :], U[:, k, :], ACT.Identity, bias=MOD[:, l, k, g:g + 1])
                    mark(ins, "u1") if k == KD - 1 else link(ins)
                if whole:
                    chunks(act, "qkvz", a, move(lambda i, w: PT[:, bass.ds(i * 512, 512)]))
                else:
                    chunks(act, "qkvz", a, move(lambda i, w: PT[:, bass.ds(i * 512 + 4 * T, 512)]))
                moved("qkvz", a)
                tell(act, "qkv_out")
                o = full(act, "ab", a)
                free(A(AB[:].rearrange("p a b -> p (a b)"), o[:, 0:32]), "ab", a)
                emptied(act, "ab", a)
                mark(A(AB[:, :, 8:16], AB[:, :, 8:16], ACT.Sigmoid), "ab_out")
                if whole:
                    rest = move(lambda i, w: PT[:, bass.ds(i * 512 + T_BG * T, 512)])
                else:
                    rest = move(lambda i, w: PT[:, T_AK * T:T_AK * T + 512])
                chunks(act, "rest", a, rest, 0, EARLY)
                moved("rest", a, EARLY)
                tell(act, "rest_out")
                serve(a, "proj")
                after(act, "ab_biased", a)
                link(A(TMPC[:, :, 0:8], AB[:, :, 0:8], ACT.Abs))
                settle()
                link(A(TMPC[:, :, 0:8], TMPC[:, :, 0:8], ACT.Exp, scale=-1.0))
                settle()
                link(A(TMPC[:, :, 0:8], TMPC[:, :, 0:8], ACT.Ln, bias=1.0))
                link(A(TMPC[:, :, 8:16], ADT[:, 0:1, :].to_broadcast([P, NT, 8]), ACT.Exp))
                settle()
                mark(A(AB[:, :, 0:8], AB[:, :, 0:8], ACT.Relu), "softplus")
                q0 = 0 if whole else 4
                after(act, "conv_a", a)
                link(A(QC[:, q0:12, :], QC[:, q0:12, :], ACT.Silu))
                settle()
                mark(A(f3(q0 * T, 8 - q0, T), QC[:, q0:8, :], ACT.Square), "sq_l2")
                o = full(act, "cum", a)
                free(A(GC[:].rearrange("p a b -> p (a b)"), o[:, 0:32]), "cum", a)
                emptied(act, "cum", a)
                tell(act, "cum_out")
                serve(a, "gates")
                for j in range(4 if whole else 2):
                    root("l2", a, j)
                    root_of(F[:, 4096 + j * 512:4608 + j * 512], F[:, 2048 + j * 512:2560 + j * 512])
                chunks(act, "rest", a, rest, EARLY)
                moved("rest", a)
                serve(a, "l2")
                serve(a, "cols")
                for j in range(4):
                    o = full(act, "tok", a, j)
                    dst = (KTOK if j < 2 else VTOK)[:, j % 2]
                    ins = A(dst, o[:].rearrange("p (h n) -> p h n", h=HEADS))
                    free(ins, "tok", a, j)
                for j in range(4):
                    emptied(act, "tok", a, j)
                after(act, "cum_diff", a)
                mark(A(EGC[:], EGC[:], ACT.Exp), "cum_exp")
                for d in range(2):
                    for t in range(NT):
                        o = full(act, f"decay{d}", a, t)
                        o3 = o[:].rearrange("p (h n) -> p h n", h=HEADS)
                        ends = (CHUNK - 1, P) if d == 0 else (0, P - CHUNK + 1)
                        if d and t == 0:
                            after(act, "state", a, (10,) * 4, 4)
                        link(A(DEC[:, t], o3[:, :, ends[0]:ends[1]:CHUNK], ACT.Exp))
                        mark(A(FD[:, t], o3, ACT.Exp), "eg")
                    for t in range(NT):
                        after(act, "diffs", a, (4,) * 4, 2 * d + t)
                        link(A(FA[:, t], FA[:, t], ACT.Exp, scale=-1.0))
                        mark(A(FQ[:, t], FQ[:, t], ACT.Exp), "decays")
                    serve(a, f"prep{d}0")
                    for t in range(NT):
                        for h in range(HEADS):
                            ins = A(FVB[:, t, h, :], VTOK[:, t, h, :], scale=GB[:, t, 8 + 4 * d + h:9 + 4 * d + h])
                            mark(ins, "rhs_v") if (t, h) == (NT - 1, HEADS - 1) else link(ins)
                    for lv in range(6):
                        for t in range(NT):
                            i = 2 * SOLVE.index(("x", lv)) + t
                            o = full(act, f"solve{d}", a, i)
                            ins = A(FX[:, t], o[:].rearrange("p (h n) -> p h n", h=HEADS))
                            free(ins, f"solve{d}", a, i)
                            emptied(act, f"solve{d}", a, i)
                            tell(act, "x_out")
                        serve(a, f"solve{d}{lv}")
                    for t in range(NT):
                        o = full(act, f"rhs{d}", a, 2 + t)
                        free(A(FW[:, t], o[:].rearrange("p (h n) -> p h n", h=HEADS)), f"rhs{d}", a, 2 + t)
                    for t in range(NT):
                        emptied(act, f"rhs{d}", a, 2 + t)
                    tell(act, "w_out")
                    for st in range(4):
                        serve(a, f"scan{d}{st}")
                if whole:
                    after(act, "osum", a, FULLP)
                    link(A(pt(T_Z, 4), pt(T_Z, 4), ACT.Silu))
                    settle()
                    mark(A(F[:, 0:1024], pt(T_OSUM, 4), ACT.Square), "sq_g")
                    for j in range(2):
                        root("gout", a, j)
                        root_of(F[:, 4096 + j * 512:4608 + j * 512], F[:, 2048 + j * 512:2560 + j * 512])
                    after(act, "branch_a", a, FULLP)
                else:
                    after(act, "state", a, (10,) * 4, 9)
                lo, n = (0, 5) if whole else (4, 1)
                serve(a, "gout")
                mark(A(F[:, 2048 + lo * T:2048 + (lo + n) * T], PT[:, (T_AQ + lo) * T:(T_AQ + lo + n) * T], ACT.Square), "sq_a")
                for j in range(3 if whole else 1):
                    w = min(512, n * T - 512 * j)
                    root("an", a, j)
                    root_of(F[:, 6144 + j * 512:6144 + j * 512 + w], F[:, 4096 + j * 512:4096 + j * 512 + w])
                o = full(act, "dup", a)
                free(A(KDUP[:, :, (1 - g) * T:(2 - g) * T], o[:].rearrange("p (v n) -> p v n", v=2)), "dup", a)
                o = full(act, "vtok", a)
                free(A(VV[:, NT * (1 - g):NT * (2 - g), :], o[:, 0:T].rearrange("p (t n) -> p t n", t=NT)), "vtok", a)
                emptied(act, "dup", a)
                emptied(act, "vtok", a)
                tell(act, "kv_ready")
                if not whole:
                    serve(a, "rest")
                    continue
                kt = 4 if g else 2
                for n, (kind, i) in enumerate(ATT):
                    if kind == "s":
                        after(act, "maxed", a, (16, 16, 0, 16), i)
                        o = full(act, "att", a, n)
                        free(A(F[:, (i % 2) * 512:(i % 2) * 512 + kt * P], o[:, 0:kt * P], ACT.Exp, scale=HD ** -0.5,
                               bias=SM[:, 0, i % 2:i % 2 + 1], accum_out=SM[:, 0, 2 + i % 2:3 + i % 2]), "att", a, n)
                    elif kind == "p":
                        o = full(act, "att", a, n)
                        free(A(F[:, 1024 + (i % 2) * 512:1024 + (i % 2) * 512 + kt * P], o[:, 0:kt * P]), "att", a, n)
                        emptied(act, "att", a, n)
                        tell(act, "probs_t")
                        serve(a, f"att{i}")

                def merge(n, i, gate, branch):
                    b, o = gate
                    act.wait_ge(sem(f"wdone{b}"), o + 2)
                    act.wait_ge(sem("sgfree"), i + (nth("sgfree", a, (12, 12, 0, 12), 4 * n)))
                    act.sem_inc(sem("act_hold"), 1)
                    A(F[:, 0:512], wbank[b][:], ACT.Sigmoid).then_inc(sem(f"wbfree{b}"), 1)
                after(act, "att_out", a, FULLP)
                branch_chunks(act, a, merge)
                for n in range(3):
                    serve(a, f"merge{n}")
                serve(a, "rest")
                after(act, "h_mid", a, FULLP)
                mark(A(F[:, 0:KD * T], H[:, g].rearrange("p k n -> p (k n)"), ACT.Square), "sq2")
                root("rms2", a)
                root_of(F[:, 2304:2560], F[:, 2048:2304])
                after(act, "scaled2", a, FULLP)
                for k in range(KD):
                    ins = A(U[:, k, :], U[:, k, :], ACT.Identity, bias=MOD[:, l, 24 + k, g:g + 1])
                    mark(ins, "u2") if k == KD - 1 else link(ins)
                for j in range(4):
                    o = full(act, "u2t", a, j)
                    free(A(U2[:, j // 2, (j % 2) * 512:(j % 2) * 512 + 512], o[:]), "u2t", a, j)
                for j in range(2):
                    o = full(act, "skt", a, j)
                    free(A(SKT[:, 4 * j:4 * j + 4, :], o[:].rearrange("p (h n) -> p h n", h=4)), "skt", a, j)
                chunks(act, "query", a, move(lambda i, w: PT[:, bass.ds(i * 512 + 16 * T, 512)]))
                moved("query", a)
                for j in range(2):
                    emptied(act, "skt", a, j)
                for j in range(4):
                    emptied(act, "u2t", a, j)
                tell(act, "query_out")
                for t in range(NT):
                    after(act, "best", a, (2, 2, 0, 2), t)
                    mark(A(GATE[:, t, :], GATE[:, t, :], ACT.Exp), "gate_exp")
            serve(4, "")
            after(act, "h_done", 0)
            mark(A(F[:, 0:KD * T], H[:, 1].rearrange("p k n -> p (k n)"), ACT.Square), "sq3")
            root("fin", 3)
            root_of(F[:, 2304:2560], F[:, 2048:2304])
            for j in range(4):
                o = full(act, "out", 3, j)
                free(A(U2[:, j // 2, (j % 2) * 512:(j % 2) * 512 + 512], o[:]), "out", 3, j)
            for j in range(4):
                emptied(act, "out", 3, j)
            tell(act, "result")

        @block.vector
        def _(dve):
            own = [0]
            v = nc.vector

            def post(ins):
                own[0] += 1
                ins.then_inc(sem("dve_step"), 1)

            def settle():
                dve.wait_ge(sem("dve_step"), own[0])

            def step(ins):
                post(ins)
                settle()

            def rsqrt(stage, a, i, w, scale, at, rt, tmp):
                o = full(dve, stage, a, i)
                free(v.tensor_scalar(F[:, at:at + w], o[:, 0:w], scale, EPS, ALU.mult, ALU.add), stage, a, i)
                emptied(dve, stage, a, i)
                dve.sem_inc(sem("var"), 1)
                dve.wait_ge(sem("root"), before(ROOTS, stage, a, i) + 1)
                x, y, z = F[:, at:at + w], F[:, rt:rt + w], F[:, tmp:tmp + w]
                step(v.scalar_tensor_tensor(out=z, in0=y, scalar=-0.5, in1=y, op0=ALU.mult, op1=ALU.mult))
                step(v.tensor_tensor(z, z, x, ALU.mult))
                step(v.scalar_tensor_tensor(out=y, in0=z, scalar=1.5, in1=y, op0=ALU.add, op1=ALU.mult))
                return y

            def conv(dst, src, w, n):
                for i in range(n):
                    post(v.tensor_scalar(dst(i), src(i), w(1, i), None, ALU.mult))
                settle()
                for i in range(n):
                    post(v.scalar_tensor_tensor(out=dst(i)[:, 1:T], in0=src(i)[:, 0:T - 1], scalar=w(0, i),
                                                in1=dst(i)[:, 1:T], op0=ALU.mult, op1=ALU.add))
                settle()
                for i in range(n):
                    post(v.scalar_tensor_tensor(out=dst(i)[:, 0:T - 1], in0=src(i)[:, 1:T], scalar=w(2, i),
                                                in1=dst(i)[:, 0:T - 1], op0=ALU.mult, op1=ALU.add))
                settle()

            def bc(ap, n):
                return ap.unsqueeze(len(ap.shape)).to_broadcast(list(ap.shape) + [n])

            step(v.memset(VN[:], 0.0))
            step(v.memset(SM[:], 0.0))
            for _ in range(2 * RING):
                dve.sem_inc(sem("rowfree"), 1)

            def rows(src, t, kind, blk):
                g0 = last_block(src, t, kind, 0)
                for b in range(RING):
                    dve.wait_ge(sem(f"row{b}"), blk * 16 + (g0 * 16 + 16))
                    col = bass.ds(blk * RING + b, 1)
                    if kind == 0:
                        v.scalar_tensor_tensor(out=ROW[:, b, :], in0=ROW[:, b, :], scalar=1.0, in1=U2[:, t, :], op0=ALU.mult,
                                               op1=ALU.mult, accum_out=DOT[:, col]).then_inc(sem("rowfree"), 1)
                    else:
                        v.scalar_tensor_tensor(out=ACC[:, t, :], in0=ROW[:, b, :], scalar=COEF[:, col], in1=ACC[:, t, :],
                                               op0=ALU.mult, op1=ALU.add).then_inc(sem("rowfree"), 1)
                        dve.wait_ge(sem("rowfree"), blk * RING + (g0 * RING + 2 * RING + b + 1))

            def open_segment(src, t, kind, lo):
                if kind and lo == 0:
                    after(dve, "gelu", src, (2, 2, 0, 2), t)
                    step(v.tensor_tensor(COEF[:], COEF[:], GATE[:, t, :], ALU.mult))
                    step(v.memset(ACC[:, t, :], 0.0))

            def close_segment(src, t, kind, hi):
                if kind == 0 and hi == BLOCKS:
                    dve.wait_ge(sem("rowfree"), (last_block(src, t, 0, BLOCKS) + 2) * RING)
                    tell(dve, "dots")

            def serve(a, point):
                src = a if point.startswith("own") else min(a - 1, 3)
                for t, kind, lo, hi in segments(*served(a, point)):
                    open_segment(src, t, kind, lo)
                    if hi - lo > 2:
                        with dve.Fori(lo, hi) as i:
                            rows(src, t, kind, i)
                    else:
                        for i in range(lo, hi):
                            rows(src, t, kind, i)
                    close_segment(src, t, kind, hi)

            def back(a, stage, src):
                tell(dve, "retrieved")
                l, g, _ = PASSES[src]
                for j in range(2 * NT):
                    o = full(dve, stage, a, j)
                    for k in range(4):
                        kk = 4 * (j % 2) + k
                        hh = H[:, g, kk, (j // 2) * P:(j // 2 + 1) * P]
                        ins = v.scalar_tensor_tensor(out=hh, in0=o[:, k * P:(k + 1) * P], scalar=MOD[:, l, 40 + kk, g:g + 1],
                                                     in1=hh, op0=ALU.mult, op1=ALU.add)
                        post(ins) if k < 3 else free(ins, stage, a, j)
                    emptied(dve, stage, a, j)

            dve.sem_inc(sem("sgfree"), 1)
            for a, (l, g, whole) in enumerate(PASSES):
                if g == 0:
                    serve(a, "mod")
                    o = full(dve, "modt", a)
                    emptied(dve, "vecs", a)
                    free(v.tensor_tensor(MOD[:, l], o[:, 0:96].rearrange("p (a b) -> p a b", b=2),
                                         bc(VEC[:, V_BMOD:V_BMOD + 48], 2), ALU.add), "modt", a)
                    emptied(dve, "modt", a)
                    for n, (vn, sc) in enumerate(((V_N1, 8), (V_N2, 32))):
                        step(v.tensor_scalar(A12[:, n], MOD[:, l, sc:sc + 8, :], 1.0, None, ALU.add))
                        step(v.tensor_tensor(A12[:, n], A12[:, n], bc(VEC[:, vn:vn + 8], 2), ALU.mult))
                rs = rsqrt("rms1", a, 0, T, 1.0 / D, 2048, 2304, 2560)
                for k in range(KD):
                    ins = v.scalar_tensor_tensor(out=U[:, k, :], in0=H[:, g, k, :], scalar=A12[:, 0, k, g:g + 1],
                                                 in1=rs, op0=ALU.mult, op1=ALU.mult)
                    mark(ins, "scaled1") if k == KD - 1 else post(ins)
                serve(a, "proj")
                after(dve, "ab_out", a)
                mark(v.tensor_tensor(AB[:, :, 0:8], AB[:, :, 0:8], ADT[:, 1:2, :].to_broadcast([P, NT, 8]), ALU.add),
                     "ab_biased")
                q0 = 0 if whole else 4
                conv(lambda i: QC[:, q0 + i, :], lambda i: pt(T_QKV + q0 + i),
                     lambda j, i: VEC[:, V_CA + 12 * j + q0 + i:V_CA + 12 * j + q0 + i + 1], 12 - q0)
                tell(dve, "conv_a")
                after(dve, "softplus", a)
                step(v.tensor_tensor(TMPC[:, :, 0:8], TMPC[:, :, 0:8], AB[:, :, 0:8], ALU.add))
                step(v.tensor_copy(GB[:, :, 8:16], AB[:, :, 8:16]))
                mark(v.scalar_tensor_tensor(out=GB[:, :, 0:8], in0=TMPC[:, :, 0:8], scalar=-1.0, in1=TMPC[:, :, 8:16],
                                            op0=ALU.mult, op1=ALU.mult), "gates_made")
                serve(a, "gates")
                for j in range(4 if whole else 2):
                    jj = j if whole else j + 2
                    y = rsqrt("l2", a, j, 512, 1.0, 2048 + j * 512, 4096 + j * 512, 6144 + j * 512)
                    qk = QC[:, 2 * jj:2 * jj + 2, :].rearrange("p a b -> p (a b)")
                    ins = v.scalar_tensor_tensor(out=qk, in0=qk, scalar=P ** -0.5 if jj < 2 else 1.0, in1=y,
                                                 op0=ALU.mult, op1=ALU.mult)
                    mark(ins, "qk_normed") if jj == 3 else post(ins)
                if whole:
                    after(dve, "rest_out", a)
                    step(v.tensor_tensor(pt(T_CG, 4), pt(T_CG, 4), pt(T_XIN, 4), ALU.mult))
                    conv(lambda i: pt(T_XIN + i), lambda i: pt(T_CG + i),
                         lambda j, i: VEC[:, V_CB + 4 * j + i:V_CB + 4 * j + i + 1], 4)
                    step(v.tensor_tensor(pt(T_OB, 4), pt(T_BG, 4), pt(T_XIN, 4), ALU.mult))
                serve(a, "l2")
                after(dve, "cum_out", a)
                post(v.tensor_copy(EGC[:, :, 0:8], GC[:, :, 0:8]))
                mark(v.tensor_tensor(EGC[:, :, 8:16], GC[:, :, 8:16], GC[:, :, 0:8], ALU.subtract), "cum_diff")
                after(dve, "cum_exp", a)
                mark(v.tensor_tensor(BEG[:], EGC[:, :, 0:8], GB[:, :, 8:16], ALU.mult), "columns")
                after(dve, "columns", a)
                serve(a, "cols")
                for d in range(2):
                    for t in range(NT):
                        o = full(dve, f"decay{d}", a, t)
                        after(dve, "eg", a, (4,) * 4, 2 * d + t)
                        for h in range(HEADS):
                            col = GC[:, t, 4 * d + h:4 * d + h + 1]
                            post(v.tensor_scalar(FA[:, t, h, :], o[:, h * P:(h + 1) * P], col, 0.0, ALU.subtract, ALU.max))
                            ins = v.tensor_scalar(FQ[:, t, h, :], o[:, h * P:(h + 1) * P], col, 0.0, ALU.subtract, ALU.min)
                            if h < HEADS - 1:
                                post(ins)
                            else:
                                free(ins, f"decay{d}", a, t)
                        emptied(dve, f"decay{d}", a, t)
                        tell(dve, "diffs")
                    for t in range(NT):
                        if whole:
                            step(v.tensor_tensor(FD[:, t], FD[:, t], QC[:, 0:HEADS, t * P:(t + 1) * P], ALU.mult))
                        for h in range(HEADS):
                            k = 4 * d + h
                            post(v.tensor_scalar(FKB[:, t, h, :], KTOK[:, t, h, :], BEG[:, t, k:k + 1], None, ALU.mult))
                            post(v.tensor_scalar(FK[:, t, h, :], KTOK[:, t, h, :], EGC[:, t, 8 + k:9 + k], None, ALU.mult))
                    settle()
                    tell(dve, "rhs_in")
                    serve(a, f"prep{d}0")
                    for t in range(NT):
                        after(dve, "decays", a, (4,) * 4, 2 * d + t)
                        m = c(f"str{d}").unsqueeze(1).to_broadcast([P, HEADS, P])
                        step(v.tensor_tensor(FA[:, t], FA[:, t], m, ALU.mult))
                        o = full(dve, f"gram{d}", a, t)
                        for h in range(HEADS):
                            ins = v.scalar_tensor_tensor(out=FA[:, t, h, :], in0=o[:, h * P:(h + 1) * P],
                                                         scalar=GB[:, t, 8 + 4 * d + h:9 + 4 * d + h], in1=FA[:, t, h, :],
                                                         op0=ALU.mult, op1=ALU.mult)
                            post(ins) if h < HEADS - 1 else free(ins, f"gram{d}", a, t)
                        emptied(dve, f"gram{d}", a, t)
                    if whole:
                        for t in range(NT):
                            m = c(f"tri{d}").unsqueeze(1).to_broadcast([P, HEADS, P])
                            step(v.tensor_tensor(FQ[:, t], FQ[:, t], m, ALU.mult))
                            o = full(dve, f"qk{d}", a, t)
                            free(v.tensor_tensor(FQ[:, t], FQ[:, t], o[:].rearrange("p (h n) -> p h n", h=HEADS), ALU.mult),
                                 f"qk{d}", a, t)
                    for lv in range(6):
                        m = c(f"lv{lv}").unsqueeze(1).to_broadcast([P, HEADS, P])
                        for t in range(NT):
                            mark(v.tensor_tensor(FW[:, t], FA[:, t], m, ALU.mult), "level")
                        serve(a, f"solve{d}{lv}") if lv else None
                        ident = c("ident").unsqueeze(1).to_broadcast([P, HEADS, P])
                        if lv == 0:
                            for t in range(NT):
                                i = 2 * SOLVE.index(("x", 0)) + t
                                after(dve, "level", a, (24,) * 4, 12 * d + t)
                                post(v.tensor_tensor(FT[:, t], ident, FW[:, t], ALU.subtract))
                                after(dve, "x_out", a, (24,) * 4, 12 * d + t)
                                step(v.tensor_tensor(FU[:, t], ident, FX[:, t], ALU.subtract))
                            serve(a, f"solve{d}{lv}")
                            continue
                        for kind, dst in (("u", FU), ("t", FT)):
                            if (kind, lv) not in SOLVE:
                                continue
                            for t in range(NT):
                                i = 2 * SOLVE.index((kind, lv)) + t
                                o = full(dve, f"solve{d}", a, i)
                                free(v.tensor_tensor(dst[:, t], dst[:, t], o[:].rearrange("p (h n) -> p h n", h=HEADS),
                                                     ALU.subtract), f"solve{d}", a, i)
                                emptied(dve, f"solve{d}", a, i)
                    tell(dve, "solved")
                    for t in range(NT):
                        o = full(dve, f"rhs{d}", a, t)
                        free(v.tensor_copy(FY[:, t], o[:].rearrange("p (h n) -> p h n", h=HEADS)), f"rhs{d}", a, t)
                    for t in range(NT):
                        emptied(dve, f"rhs{d}", a, t)
                    if g == 0:
                        step(v.memset(S[:, d], 0.0))
                    tell(dve, "state")
                    sn = 3 if whole else 2
                    for s in range(4):
                        ch = 3 - s if d else s
                        t, half = ch // 2, ch % 2
                        lo = half * CHUNK
                        o = full(dve, f"scan{d}", a, sn * s)
                        hr = slice(lo, lo + CHUNK)
                        free(v.tensor_tensor(VN[hr, half], FY[hr, t], o[hr, :].rearrange("p (h n) -> p h n", h=HEADS),
                                             ALU.subtract), f"scan{d}", a, sn * s)
                        emptied(dve, f"scan{d}", a, sn * s)
                        tell(dve, "vnew")
                        serve(a, f"scan{d}{s}")
                        if whole:
                            o = full(dve, f"scan{d}", a, sn * s + 1)
                            oo = OSUM[:, :, ch * CHUNK:(ch + 1) * CHUNK]
                            src = o[:, 0:256].rearrange("p (h n) -> p h n", h=HEADS)
                            free(v.tensor_copy(oo, src) if d == 0 else v.tensor_tensor(oo, oo, src, ALU.add),
                                 f"scan{d}", a, sn * s + 1)
                        o = full(dve, f"scan{d}", a, sn * s + sn - 1)
                        for h in range(HEADS):
                            ins = v.scalar_tensor_tensor(out=S[:, d, h, :], in0=S[:, d, h, :], scalar=DEC[:, t, h, half:half + 1],
                                                         in1=o[:, h * P:(h + 1) * P], op0=ALU.mult, op1=ALU.add)
                            post(ins) if h < HEADS - 1 else free(ins, f"scan{d}", a, sn * s + sn - 1)
                        emptied(dve, f"scan{d}", a, sn * s + sn - 1)
                        tell(dve, "state")
                if whole:
                    tell(dve, "osum")
                    for j in range(2):
                        y = rsqrt("gout", a, j, 512, 1.0 / P, 2048 + j * 512, 4096 + j * 512, 6144 + j * 512)
                        step(v.scalar_tensor_tensor(out=y, in0=y, scalar=VEC[:, V_GN:V_GN + 1], in1=pt(T_Z + 2 * j, 2),
                                                    op0=ALU.mult, op1=ALU.mult))
                        ins = v.tensor_tensor(pt(T_OA + 2 * j, 2), pt(T_OSUM + 2 * j, 2), y, ALU.mult)
                        mark(ins, "branch_a") if j else post(ins)
                serve(a, "gout")
                lo, n = (0, 5) if whole else (4, 1)
                for j in range(3 if whole else 1):
                    w = min(512, n * T - 512 * j)
                    y = rsqrt("an", a, j, w, 1.0 / HD, 4096 + j * 512, 6144 + j * 512, 8192 + j * 512)
                    at = (T_AQ + lo) * T + j * 512
                    col = V_KN if (not whole or j == 2) else V_QN
                    ins = v.scalar_tensor_tensor(out=PT[:, at:at + w], in0=PT[:, at:at + w], scalar=VEC[:, col:col + 1], in1=y,
                                                 op0=ALU.mult, op1=ALU.mult)
                    step(ins)
                if g:
                    tell(dve, "a_normed")
                    cos, sin = cst[:, C_COS:C_COS + T], cst[:, C_SIN:C_SIN + T]
                    for j in range(3):
                        w = min(512, 5 * T - 512 * j)
                        n2 = w // T
                        o = full(dve, "rope", a, j)
                        free(v.tensor_tensor(f3(4096 + j * 512, n2, T), o[:, 0:w].rearrange("p (a b) -> p a b", b=T),
                                             sin.unsqueeze(1).to_broadcast([P, n2, T]), ALU.mult), "rope", a, j)
                        emptied(dve, "rope", a, j)
                    for j in range(3):
                        n2 = min(2, 5 - 2 * j)
                        q = pt3(T_AQ + 2 * j, n2)
                        step(v.tensor_tensor(q, q, cos.unsqueeze(1).to_broadcast([P, n2, T]), ALU.mult))
                        step(v.tensor_tensor(q, q, f3(4096 + j * 512, n2, T), ALU.add))
                else:
                    tell(dve, "a_normed")
                tell(dve, "a_turned")
                if not whole:
                    serve(a, "rest")
                    back(a, "back", a - 1)
                    tell(dve, "pass_over")
                    continue
                kt = 4 if g else 2

                def normalise(i):
                    n = ATT.index(("s", i))
                    emptied(dve, "att", a, n)
                    step(v.reciprocal(SM[:, 0, 2 + i % 2:3 + i % 2], SM[:, 0, 2 + i % 2:3 + i % 2]))
                    mark(v.tensor_scalar(F[:, (i % 2) * 512:(i % 2) * 512 + kt * P], F[:, (i % 2) * 512:(i % 2) * 512 + kt * P],
                                         SM[:, 0, 2 + i % 2:3 + i % 2], None, ALU.mult), "probs")
                for n, (kind, i) in enumerate(ATT):
                    t, h = i // AHEADS, i % AHEADS
                    if kind == "s":
                        o = full(dve, "att", a, n)
                        if i >= 2:
                            full(dve, "att", a, ATT.index(("p", i - 2)))
                        step(v.tensor_reduce(SM[:, 0, i % 2:i % 2 + 1], o[:, 0:kt * P], AX.X, ALU.max))
                        mark(v.tensor_scalar(SM[:, 0, i % 2:i % 2 + 1], SM[:, 0, i % 2:i % 2 + 1], -(HD ** -0.5), None, ALU.mult),
                             "maxed")
                        serve(a, f"att{i - 1}") if i else None
                        normalise(i)
                    elif kind == "o":
                        hp = HD * (h % 2)
                        o = full(dve, "att", a, n)
                        at = (T_OC + h // 2) * T + t * P
                        free(v.tensor_copy(PT[hp:hp + HD, at:at + P], o[hp:hp + HD, 0:P]), "att", a, n)
                        emptied(dve, "att", a, n)
                tell(dve, "att_out")

                def merge(n, i, gate, branch):
                    gb, go = gate
                    bb, bo = branch
                    dve.wait_ge(sem(f"wbfree{gb}"), go + 2)
                    dve.wait_ge(sem(f"wdone{bb}"), bo + 2)
                    if n == 0:
                        v.tensor_tensor(PT[:, bass.ds(i * 512 + T_MIX * T, 512)], F[:, 0:512], wbank[bb][:], ALU.mult).then_inc(
                            sem(f"wbfree{bb}"), 1)
                    else:
                        v.tensor_tensor(F[:, 512:1024], F[:, 0:512], wbank[bb][:], ALU.mult).then_inc(sem(f"wbfree{bb}"), 1)
                        dve.wait_ge(sem(f"wbfree{bb}"), bo + 2)
                        m = PT[:, bass.ds(i * 512 + T_MIX * T, 512)]
                        v.tensor_tensor(m, m, F[:, 512:1024], ALU.add).then_inc(sem("mixstep"), 1)
                        dve.wait_ge(sem("mixstep"), i + (1 + 8 * FULL_INDEX[a] + 4 * (n - 1)))
                    dve.wait_ge(sem(f"wbfree{bb}"), bo + 2)
                    dve.sem_inc(sem("sgfree"), 1)
                    for t, kind, lo, hi in segments(*served(a, f"merge{n}")):
                        rows(a - 1, t, kind, i + lo)
                for t, kind, lo, hi in segments(*served(a, "merge0")):
                    open_segment(a - 1, t, kind, lo)
                branch_chunks(dve, a, merge)
                tell(dve, "mixed")

                def residual(i, b, o):
                    dve.wait_ge(sem(f"wdone{b}"), o + 2)
                    h2 = H[:, g].rearrange("p k n -> p (k n)")
                    gcol = MOD[:, l, 16:24, :].rearrange("p k n -> p (k n)")
                    for j in range(2):
                        hh = h2[:, bass.ds(i * 512 + j * T, T)]
                        ins = v.scalar_tensor_tensor(out=hh, in0=wbank[b][:, j * T:(j + 1) * T],
                                                     scalar=gcol[:, bass.ds(i * 4 + 2 * j + g, 1)], in1=hh,
                                                     op0=ALU.mult, op1=ALU.add)
                        if j:
                            ins.then_inc(sem(f"wbfree{b}"), 1)
                chunks(dve, "out", a, residual)
                for i in (2, 3):
                    cc = before(WEIGHTS, "out", a, i)
                    dve.wait_ge(sem(f"wbfree{cc % 2}"), cc // 2 + 2)
                serve(a, "rest")
                if a == 1:
                    back(a, "back", 0)
                tell(dve, "h_mid")
                rs = rsqrt("rms2", a, 0, T, 1.0 / D, 2048, 2304, 2560)
                full(dve, "rms2", a)
                for k in range(KD):
                    ins = v.scalar_tensor_tensor(out=U[:, k, :], in0=H[:, g, k, :], scalar=A12[:, 1, k, g:g + 1],
                                                 in1=rs, op0=ALU.mult, op1=ALU.mult)
                    mark(ins, "scaled2") if k == KD - 1 else post(ins)
                after(dve, "query_out", a, FULLP)
                for t in range(NT):
                    sc = F[:, 0:2048].rearrange("p (r n) -> p r n", n=P)
                    s2 = F[:, 2048:4096].rearrange("p (r n) -> p r n", n=P)
                    for j in range(4):
                        o = full(dve, "keys", a, 4 * t + j)
                        free(v.tensor_copy(F[:, j * 512:(j + 1) * 512], o[:]), "keys", a, 4 * t + j)
                    for j in range(4):
                        emptied(dve, "keys", a, 4 * t + j)

                    def beside(i):
                        if t:
                            serve(a, f"own{i}")

                    def top16(vals, spare, best, at, n):
                        for r in range(n):
                            post(v.max(best[:, r, 0:8], vals[:, r, :]))
                        settle()
                        for r in range(n):
                            post(v.max_index(at[:, r, 0:8], best[:, r, 0:8], vals[:, r, :]))
                            post(v.match_replace(spare[:, r, :], best[:, r, 0:8], vals[:, r, :], NEG))
                        settle()
                        for r in range(n):
                            post(v.max(best[:, r, 8:16], spare[:, r, :]))
                        settle()
                        for r in range(n):
                            post(v.max_index(at[:, r, 8:16], best[:, r, 8:16], spare[:, r, :]))
                        settle()

                    beside(0)
                    top16(sc, s2, TOPV, TOPI, 16)
                    beside(1)
                    beside(2)
                    cand = F[:, 4096:6144].rearrange("p (h n) -> p h n", n=256)
                    cand2 = F[:, 6144:8192].rearrange("p (h n) -> p h n", n=256)
                    for h in range(PHEADS):
                        post(v.tensor_tensor(cand[:, h].rearrange("p (x y) -> p x y", x=TOPK), bc(TOPV[:, h, :], TOPK),
                                             TOPV[:, 8 + h, :].unsqueeze(1).to_broadcast([P, TOPK, TOPK]), ALU.add))
                    tif = F[:, 8192:8448].rearrange("p (r n) -> p r n", n=TOPK)
                    step(v.tensor_copy(tif, TOPI))
                    top16(cand, cand2, BV, BJ[:, 0], PHEADS)
                    beside(3)
                    beside(4)
                    step(v.tensor_scalar(BJ[:, 1], BJ[:, 0], 4, None, ALU.logical_shift_right))
                    step(v.tensor_scalar(BJ[:, 2], BJ[:, 0], 15, None, ALU.bitwise_and))
                    ab = F[:, 8448:8704].rearrange("p (q n) -> p q n", q=2)
                    step(v.tensor_copy(ab.rearrange("p q n -> p (q n)"), BJ[:, 1:3].rearrange("p q h n -> p (q h n)")))
                    iota = cst[:, C_IOTA:C_IOTA + TOPK].unsqueeze(1).to_broadcast([P, SLOTS, TOPK])
                    pick = F[:, 8704:8960].rearrange("p (q n) -> p q n", q=2)
                    for q in range(2):
                        hot = F[:, 0:2048].rearrange("p (s x) -> p s x", x=TOPK)
                        step(v.tensor_tensor(hot, bc(ab[:, q], TOPK), iota, ALU.is_equal))
                        for h in range(PHEADS):
                            hh = hot[:, h * TOPK:(h + 1) * TOPK, :]
                            post(v.tensor_tensor(hh, hh, tif[:, 8 * q + h, :].unsqueeze(1).to_broadcast([P, TOPK, TOPK]),
                                                 ALU.mult))
                        settle()
                        step(v.tensor_reduce(pick[:, q], hot, AX.X, ALU.add))
                        beside(5 + q)
                    step(v.tensor_scalar(pick[:, 0], pick[:, 0], float(NKEYS), float(l * EXPERTS), ALU.mult, ALU.add))
                    step(v.tensor_tensor(pick[:, 0], pick[:, 0], pick[:, 1], ALU.add))
                    mark(v.tensor_copy(IDX[:, t, :], pick[:, 0]), "chosen")
                    gt = GATE[:, t, :].rearrange("p (h n) -> p h n", h=PHEADS)
                    mark(v.tensor_tensor(gt, BV, BV[:, :, 0:1].to_broadcast([P, PHEADS, TOPK]), ALU.subtract), "best")
                    after(dve, "gate_exp", a, (2, 2, 0, 2), t)
                    step(v.tensor_reduce(PHS[:, 0], gt, AX.X, ALU.add))
                    step(v.reciprocal(PHS[:, 0], PHS[:, 0]))
                    step(v.tensor_tensor(gt, gt, bc(PHS[:, 0], TOPK), ALU.mult))
                    beside(7)
                tell(dve, "pass_over")
            serve(4, "")
            back(3, "back_last", 3)
            tell(dve, "h_done")
            rs = rsqrt("fin", 3, 0, T, 1.0 / D, 2048, 2304, 2560)
            for k in range(KD):
                ins = v.scalar_tensor_tensor(out=U[:, k, :], in0=H[:, 1, k, :], scalar=CVEC[:, 16 + k:17 + k],
                                             in1=rs, op0=ALU.mult, op1=ALU.mult)
                mark(ins, "u3") if k == KD - 1 else post(ins)


FULL_INDEX = {0: 0, 1: 1, 3: 2}
_INS = ["x", "c", "ctx", "c_ctx", "w_mod", "b_mod", "norm1_w", "w_in", "conv_a_w", "a_log", "dt_bias", "gdn_norm_w",
        "conv_b_w", "q_norm_w", "k_norm_w", "w_branch", "w_out", "norm2_w", "w_query", "sub_keys", "expert_u",
        "expert_v", "final_norm_w"]


def kernel(**inputs):
    import concourse.bacc as bacc
    from concourse.bass_utils import run_bass_kernel_spmd

    nc = bacc.Bacc("TRN2", target_bir_lowering=False, num_devices=1)
    arrays = {f"in_{n}": np.ascontiguousarray(inputs[n]) for n in _INS}
    arrays["in_constants"] = constant_table()
    inp = {n[3:]: nc.dram_tensor(n, v.shape, mybir.dt.from_np(v.dtype), kind="ExternalInput").ap()
           for n, v in arrays.items()}
    out = nc.dram_tensor("out_0", (1, T, D), F32, kind="ExternalOutput").ap()
    build(nc, inp, out)
    r = run_bass_kernel_spmd(nc, [arrays], core_ids=[0])
    return r.results[0]["out_0"]
```

```python
from contextlib import ExitStack

import numpy as np

import concourse.bass as bass
from concourse import mybir

F32 = mybir.dt.float32
U32 = mybir.dt.uint32
ALU = mybir.AluOpType
ACT = mybir.ActivationFunctionType
AX = mybir.AxisListType

P = 128
D = 1024
KD = D // P
T = 256
NT = T // P
CHUNK = 64
HEADS = 4
AHEADS, KVHEADS, HD = 8, 2, 64
PHEADS, TOPK, NKEYS = 8, 16, 128
EXPERTS = NKEYS * NKEYS
SLOTS = PHEADS * TOPK
EPS = 1e-6
NEG = -3.0e38
PASSES = [(0, 0, True), (0, 1, True), (1, 0, False), (1, 1, True)]
ALL = range(len(PASSES))

COL_QKV, COL_Z, COL_AB, COL_SC, COL_GATE = 0, 1536, 2048, 2064, 4368
COL_KV = COL_GATE - 256
T_QKV, T_Z, T_BG, T_CG, T_XIN, T_AQ, T_AK = 0, 12, 16, 20, 24, 28, 32
T_OSUM, T_KTOK, T_VTOK = 0, 4, 8
T_MIX = 0
T_SKRAW, T_SKT = 8, 12
T_OB, T_OC, T_OA = T_BG, T_CG, T_XIN
NPT = 34
V_N1, V_N2, V_BMOD, V_CA, V_CB, V_GN, V_QN, V_KN = 0, 8, 16, 64, 100, 112, 113, 114
NV = 115
NAMES = ["ident", "ones", "blk64", "rot", "dup0", "dup1", "tri0", "tri1", "str0", "str1", "chunk",
         "lv0", "lv1", "lv2", "lv3", "lv4", "lv5"]
C_AT = {n: i * P for i, n in enumerate(NAMES)}
C_COS = len(NAMES) * P
C_SIN = C_COS + T
C_IOTA = C_SIN + T
NC_ = C_IOTA + TOPK

RING = 8
BLOCKS = SLOTS // RING
STEPS = 2 * NT * BLOCKS
NBK = 6


def constant_table():
    p, f = np.arange(P)[:, None], np.arange(P)[None, :]
    same = p // CHUNK == f // CHUNK
    m = {"ident": p == f, "ones": p + f >= 0, "blk64": p // HD == f // HD,
         "tri0": same & (p <= f), "tri1": same & (p >= f), "str0": same & (p > f), "str1": same & (p < f),
         "chunk": same}
    for lv in range(6):
        b = 1 << lv
        m[f"lv{lv}"] = (p // (2 * b) == f // (2 * b)) & (p // b != f // b)
    for v in range(KVHEADS):
        m[f"dup{v}"] = p == f % HD + HD * v
    m["rot"] = np.where((f // 16) % 2 == 0, -1.0 * (p == f + 16), 1.0 * (p == f - 16))
    t = np.arange(T)
    freq = np.float32(10000.0) ** (-np.arange(16, dtype=np.float32) / 16)
    ch = np.arange(P) % HD
    pos = np.where((ch // 32)[:, None] == 0, (t // 64)[None, :], (t % 64)[None, :]).astype(np.float32)
    ang = pos * freq[ch % 16][:, None]
    cols = [m[n].astype(np.float32) for n in NAMES] + [np.cos(ang), np.sin(ang),
                                                      np.tile(np.arange(TOPK, dtype=np.float32), (P, 1))]
    return np.ascontiguousarray(np.concatenate(cols, 1).astype(np.float32))


SOLVE = [("x", 0)] + [(k, lv) for lv in range(1, 5) for k in "xut"] + [("x", 5), ("u", 5)]
ATT = [("s", 0)] + [j for i in range(NT * AHEADS)
                    for j in ([("s", i + 1)] if i + 1 < NT * AHEADS else []) + [("p", i), ("o", i)]]


def direction(d):
    return [(f"decay{d}", (2, 2, 2, 2)), (f"gram{d}", (2, 2, 2, 2)), (f"qk{d}", (2, 2, 0, 2)),
            (f"solve{d}", (2 * len(SOLVE),) * 4), (f"rhs{d}", (4, 4, 4, 4)), (f"scan{d}", (12, 12, 8, 12))]


PRODUCTS = [("x_in", (8, 0, 0, 0)), ("cond", (1, 0, 0, 0)), ("vecs", (1, 0, 1, 0)), ("modt", (1, 0, 1, 0)), ("rms1", (1, 1, 1, 1)),
            ("ab", (1, 1, 1, 1)), ("cum", (1, 1, 1, 1)), ("l2", (4, 4, 2, 4)), ("tok", (4, 4, 4, 4)),
            *direction(0), *direction(1), ("gout", (2, 2, 0, 2)), ("an", (3, 3, 1, 3)), ("rope", (0, 3, 0, 3)),
            ("dup", (1, 1, 1, 1)), ("vtok", (1, 1, 1, 1)), ("att", (len(ATT), len(ATT), 0, len(ATT))), ("modt2", (1, 0, 0, 0)),
            ("rms2", (1, 1, 0, 1)), ("u2t", (4, 4, 0, 4)), ("skt", (2, 2, 0, 2)), ("keys", (8, 8, 0, 8)),
            ("back", (0, 4, 4, 0)),
            ("back_last", (0, 0, 0, 4)), ("fin", (0, 0, 0, 1)), ("out", (0, 0, 0, 4))]
ROOTS = [(n, dict(PRODUCTS)[n]) for n in ("rms1", "l2", "gout", "an", "rms2", "fin")]
WEIGHTS = [("mod", (8, 0, 24, 0)), ("qkvz", (8, 8, 4, 8)), ("rest", (9, 9, 1, 9)), ("gates", (12, 0, 0, 12)),
           ("mod2", (16, 0, 0, 0)), ("merge", (12, 24, 0, 12)),
           ("out", (4, 4, 0, 4)), ("query", (4, 4, 0, 4))]


def before(series, stage, a, i=0):
    names = [n for n, _ in series]
    k = dict(series)
    assert i < k[stage][a], (stage, a, i)
    return sum(sum(c[:a]) for _, c in series) + sum(k[n][a] for n in names[:names.index(stage)]) + i


EARLY_GATES = [a for a in ALL if dict(WEIGHTS)["gates"][a]]
PAUSES = [f"{k}{d}" for d in range(2) for k in ("decayed", "weighed", *[f"solved{lv}_" for lv in range(6)], "righted",
                                                *[f"stepped{s}_" for s in range(4)])] + ["gout"] + [f"att{i}" for i in range(16)]


def filler(a, pause):
    k = dict(WEIGHTS)
    items = [("gates", i, h) for i in range(k["gates"][a]) for h in range(2)] + [("mod2", i, 1) for i in range(k["mod2"][a])]
    k, n = len(items), PAUSES.index(pause)
    assert k <= len(PAUSES)
    here = n * k // len(PAUSES)
    return items[here] if (n + 1) * k // len(PAUSES) > here else None


EARLY = 6
OWN = 8
DIRS = [f"{k}{d}{i}" for d in range(2) for k, ii in (("prep", [0]), ("solve", range(1, 6)), ("scan", range(4))) for i in ii]
SERVE = {1: [("proj", 8), ("gates", 3), ("l2", 1), ("cols", 1), *[(x, 1) for x in DIRS], ("gout", 1), ("turn", 1),
             *[(f"att{i}", 1) for i in (2, 5, 8, 11, 14)], ("merge0", 4), ("merge1", 4), ("merge2", 4), ("out", 1), ("query", 3)],
         2: [("mod", 13), ("proj", 3), ("gates", 2), ("l2", 1), ("cols", 1), *[(x, 1) for x in DIRS], ("gout", 1), ("rest", 15)]}
assert all(OWN + sum(n for _, n in v) == STEPS for v in SERVE.values())


def served(a, point):
    if point.startswith("own"):
        return int(point[3:]), int(point[3:]) + 1
    if a == 4:
        return OWN, STEPS
    lo = OWN
    for name, n in SERVE.get(a, []):
        if name == point:
            return lo, lo + n
        lo += n
    return 0, 0


def segments(lo, hi):
    while lo < hi:
        seg = lo // BLOCKS
        top = min(hi, (seg + 1) * BLOCKS)
        yield seg // 2, seg % 2, lo % BLOCKS, top - seg * BLOCKS
        lo = top


PEER_TILES = [(a, t) for a in ALL if PASSES[a][2] for t in range(NT)]


def build(nc, inp, out):
    with ExitStack() as ctx:
        def sb(name, shape, dt=F32):
            return ctx.enter_context(nc.sbuf_tensor(name, shape, dt))

        sems = {}

        def sem(name):
            if name not in sems:
                sems[name] = ctx.enter_context(nc.semaphore("s_" + name))
            return sems[name]

        cst = sb("cst", [P, NC_])
        H = sb("H", [P, 2, KD, T])
        U = sb("U", [P, KD, T])
        W = sb("W", [P, 2, KD * 256])
        PT = sb("PT", [P, NPT * T])
        QC = sb("QC", [P, 12, T])
        S = sb("S", [P, 2, HEADS, P])
        VN = sb("VN", [P, 2, HEADS, P])
        KDUP = sb("KDUP", [P, KVHEADS, 2 * T])
        VV = sb("VV", [P, 2 * NT, P])
        F = sb("F", [P, 10240])
        ROW = sb("ROW", [P, RING, D])
        U2 = sb("U2", [P, NT, D])
        ACC = sb("ACC", [P, NT, D])
        IDX = sb("IDX", [P, NT, SLOTS], U32)
        IXC = sb("IXC", [P, 2, RING], U32)
        GATE = sb("GATE", [P, NT, SLOTS])
        DOT = sb("DOT", [P, SLOTS])
        COEF = sb("COEF", [P, SLOTS])
        VROW = sb("VROW", [NV, P])
        VEC = sb("VEC", [P, NV])
        MOD = sb("MOD", [P, 2, 48, 2])
        A12 = sb("A12", [P, 2, KD, 2])
        CROW = sb("CROW", [24, P])
        CVEC = sb("CVEC", [P, 24])
        WAB = sb("WAB", [P, KD, 16])
        ADT = sb("ADT", [P, 2, 8])
        AB = sb("AB", [P, NT, 16])
        GB = sb("GB", [P, NT, 16])
        GC = sb("GC", [P, NT, 16])
        EGC = sb("EGC", [P, NT, 16])
        BEG = sb("BEG", [P, NT, 8])
        TMPC = sb("TMPC", [P, NT, 16])
        DEC = sb("DEC", [P, NT, HEADS, 2])
        SM = sb("SM", [P, 2, 4])
        TOPV = F[:, 8960:9216].rearrange("p (r n) -> p r n", n=TOPK)
        TOPI = F[:, 9216:9472].bitcast(U32).rearrange("p (r n) -> p r n", n=TOPK)
        BV = F[:, 9472:9600].rearrange("p (h n) -> p h n", n=TOPK)
        BJ = F[:, 9600:9984].bitcast(U32).rearrange("p (q h n) -> p q h n", q=3, n=TOPK)
        PHS = sb("PHS", [P, 1, PHEADS])
        bank = [ctx.enter_context(nc.psum_tensor(f"bank{i}", [P, 512], F32)) for i in range(NBK)]
        wbank = [ctx.enter_context(nc.psum_tensor(f"wbank{i}", [P, 512], F32)) for i in range(2)]

        def c(name):
            return cst[:, C_AT[name]:C_AT[name] + P]

        def pt(t, n=1):
            return PT[:, t * T:(t + n) * T]

        def pt3(t, n, w=T):
            return PT[:, t * T:(t + n) * T].rearrange("p (a b) -> p a b", b=w)

        def f3(lo, n, w):
            return F[:, lo:lo + n * w].rearrange("p (a b) -> p a b", b=w)

        FA, FQ, FT, FU, FX, FW, FK, FD, FVB, FKB = [F[:, i * 1024:(i + 1) * 1024].rearrange(
            "p (t h n) -> p t h n", t=NT, h=HEADS) for i in range(10)]
        FY = FT
        LEVEL = (FVB, FW)
        KTOK = PT[:, T_KTOK * T:(T_KTOK + 4) * T].rearrange("p (t h n) -> p t h n", t=NT, h=HEADS)
        VTOK = PT[:, T_VTOK * T:(T_VTOK + 4) * T].rearrange("p (t h n) -> p t h n", t=NT, h=HEADS)
        OSUM = pt3(T_OSUM, 4)
        SKT = PT[:, T_SKT * T:(T_SKT + 4) * T].rearrange("p (h n) -> p h n", h=PHEADS)
        SKRAW = PT[:, T_SKRAW * T:(T_SKRAW + 4) * T].rearrange("p (h n) -> p h n", h=PHEADS)

        GATES = ROW[:].rearrange("p r n -> p (r n)")
        MROW = [t_[:].rearrange("p t n -> p (t n)") for t_ in (ACC, U2)]

        def spot(stage, a, i=0):
            n = before(PRODUCTS, stage, a, i)
            return n % NBK, n // NBK

        def full(eng, stage, a, i=0):
            b, o = spot(stage, a, i)
            eng.wait_ge(sem(f"full{b}"), o + 1)
            return bank[b]

        def free(ins, stage, a, i=0):
            ins.then_inc(sem(f"free{spot(stage, a, i)[0]}"), 1)

        def emptied(eng, stage, a, i=0):
            b, o = spot(stage, a, i)
            eng.wait_ge(sem(f"free{b}"), o + 2)

        def mark(ins, name):
            ins.then_inc(sem(name), 1)

        def tell(eng, name):
            eng.sem_inc(sem(name), 1)

        def nth(name, a, per=(1, 1, 1, 1), i=0):
            return sum(per[:a]) + i + 1

        FULLP = (1, 1, 0, 1)

        def after(eng, name, a, per=(1, 1, 1, 1), i=0):
            eng.wait_ge(sem(name), nth(name, a, per, i))

        def chunks(eng, stage, a, body, lo=0, hi=None):
            n = min(dict(WEIGHTS)[stage][a], hi or 99) - lo
            if n <= 0:
                return
            c0 = before(WEIGHTS, stage, a, lo)
            if n // 2:
                with eng.Fori(0, n // 2) as i:
                    for j in range(2):
                        body(i * 2 + (lo + j), (c0 + j) % 2, i + (c0 + j) // 2)
            if n % 2:
                body(lo + n - 1, (c0 + n - 1) % 2, (c0 + n - 1) // 2)

        def branch_chunks(eng, a, body):
            c0 = before(WEIGHTS, "merge", a)
            for n in range(3):
                with eng.Fori(0, 4) as i:
                    s = c0 + 8 * n
                    body(n, i, (s % 2, s // 2 + i), ((s + 1) % 2, (s + 1) // 2 + i))

        def last_block(a, t, table, blk):
            return (PEER_TILES.index((a, t)) * 2 + table) * BLOCKS + blk

        block = ctx.enter_context(nc.Block())

        @block.sync
        def _(sp):
            sp.dma_start(cst[:], inp["constants"]).then_inc(sem("loaded"), 16)
            for t in range(NT):
                sp.dma_start(ROW[:, t, :], inp["ctx"][0, t * P:(t + 1) * P, :]).then_inc(sem("loaded"), 16)
                sp.dma_start(ROW[:, NT + t, :], inp["x"][0, t * P:(t + 1) * P, :]).then_inc(sem("loaded"), 16)
            sp.dma_start(CROW[0:8, :], inp["c_ctx"].rearrange("(a b) -> a b", b=P)).then_inc(sem("loaded"), 16)
            sp.dma_start(CROW[8:16, :], inp["c"][0].rearrange("(a b) -> a b", b=P)).then_inc(sem("loaded"), 16)
            sp.dma_start(CROW[16:24, :], inp["final_norm_w"].rearrange("(a b) -> a b", b=P)).then_inc(
                sem("loaded"), 16)

            def vectors(a, l):
                if a:
                    full(sp, "vecs", a - 2)
                    after(sp, "gates_made", a - 1)
                    full(sp, "ab", a - 1)
                rows = [(V_N1, 8, inp["norm1_w"][l]), (V_N2, 8, inp["norm2_w"][l]), (V_BMOD, 48, inp["b_mod"][l]),
                        (V_GN, 1, inp["gdn_norm_w"][l])]
                for at, n, src in rows:
                    sp.dma_start(VROW[at:at + n, :], src.rearrange("(a b) -> a b", b=P)).then_inc(sem("vectors"), 16)
                for j in range(3):
                    sp.dma_start(VROW[V_CA + 12 * j:V_CA + 12 * j + 12, :],
                                 inp["conv_a_w"][l, j].rearrange("(a b) -> a b", b=P)).then_inc(sem("vectors"), 16)
                    sp.dma_start(VROW[V_CB + 4 * j:V_CB + 4 * j + 4, :],
                                 inp["conv_b_w"][l, j].rearrange("(a b) -> a b", b=P)).then_inc(sem("vectors"), 16)
                for at, src in ((V_QN, inp["q_norm_w"]), (V_KN, inp["k_norm_w"])):
                    for half in range(2):
                        sp.dma_start(VROW[at:at + 1, half * HD:(half + 1) * HD], src[l:l + 1, :]).then_inc(
                            sem("vectors"), 16)
                for j, name in enumerate(("a_log", "dt_bias")):
                    sp.dma_start(ADT[:, j, :], inp[name][l:l + 1].rearrange("o a b -> o (a b)").to_broadcast(
                        [P, 8])).then_inc(sem("vectors"), 16)
                sp.dma_start(WAB[:], inp["w_in"][l, :, COL_AB:COL_SC].rearrange("(k p) n -> p k n", p=P)).then_inc(
                    sem("vectors"), 16)

            def load(src, col):
                v = src.rearrange("(k p) n -> p k n", p=P)

                def body(i, b, o):
                    sp.wait_ge(sem(f"wdone{b}"), o + 1)
                    sp.sem_inc(sem("sp_hold"), 1)
                    sp.dma_start(W[:, b, :].rearrange("p (k n) -> p k n", k=KD), v[:, :, bass.ds(i * 256 + col, 256)]
                                 ).then_inc(sem(f"wload{b}"), 16)
                return body

            for a, (l, g, whole) in enumerate(PASSES):
                if g == 0:
                    chunks(sp, "mod", a, load(inp["w_mod"][l], 0), 0, 2)
                    vectors(a, l)
                    chunks(sp, "mod", a, load(inp["w_mod"][l], 0), 2)
                chunks(sp, "qkvz", a, load(inp["w_in"][l], 0 if whole else 512))
                chunks(sp, "rest", a, load(inp["w_in"][l], COL_SC if whole else COL_KV))
                if not whole:
                    continue
                gates = inp["w_in"][l].rearrange("(k p) n -> p k n", p=P)

                def merge(n, i, gate, branch):
                    b, o = gate
                    sp.wait_ge(sem(f"wdone{b}"), o + 1)
                    sp.sem_inc(sem("sp_hold"), 1)
                    sp.dma_start(W[:, b, :].rearrange("p (k n) -> p k n", k=KD),
                                 gates[:, :, bass.ds(i * 256 + COL_GATE + n * D, 256)]).then_inc(sem(f"wload{b}"), 16)
                    b, o = branch
                    sp.wait_ge(sem(f"wdone{b}"), o + 1)
                    sp.sem_inc(sem("sp_hold"), 1)
                    wb = inp["w_branch"][l, n].rearrange("(k p) n -> p k n", p=P)
                    sp.dma_start(W[:, b, 0:1024].rearrange("p (k n) -> p k n", k=4), wb[:, :, bass.ds(i * 256, 256)]
                                 ).then_inc(sem(f"wload{b}"), 16)
                if a in EARLY_GATES:
                    chunks(sp, "gates", a, load(inp["w_in"][l], COL_GATE))
                    chunks(sp, "mod2", a, load(inp["w_mod"][l], 8 * 256))
                    for n in range(3):
                        wb = inp["w_branch"][l, n].rearrange("(k p) n -> p k n", p=P)

                        def branch(i, b, o):
                            sp.wait_ge(sem(f"wdone{b}"), o + 1)
                            sp.sem_inc(sem("sp_hold"), 1)
                            sp.dma_start(W[:, b, 0:1024].rearrange("p (k n) -> p k n", k=4),
                                         wb[:, :, bass.ds(i * 256 - n * D, 256)]).then_inc(sem(f"wload{b}"), 16)
                        chunks(sp, "merge", a, branch, 4 * n, 4 * n + 4)
                else:
                    branch_chunks(sp, a, merge)
                chunks(sp, "out", a, load(inp["w_out"][l], 0))
                after(sp, "branch_a", a, FULLP)
                after(sp, "mixed", a, FULLP)
                sp.dma_start(SKRAW.rearrange("p h (q k) -> p h q k", q=2),
                             inp["sub_keys"][l].rearrange("h q n k -> n h q k")).then_inc(sem("subkeys"), 16)
                chunks(sp, "query", a, load(inp["w_query"][l], 0))
            after(sp, "result", 0)
            sp.dma_start(out[0].rearrange("(t p) d -> p t d", p=P), U2[:]).then_inc(sem("stored"), 16)
            sp.wait_ge(sem("stored"), 16)

        @block.gpsimd
        def _(pool):
            tables = [inp["expert_u"].rearrange("l e d -> (l e) d"), inp["expert_v"].rearrange("l e d -> (l e) d")]
            for a, t in PEER_TILES:
                after(pool, "chosen", a, (2, 2, 0, 2), t)
                if (a, t) == PEER_TILES[0]:
                    after(pool, "x_read", 0)
                for kind, table in enumerate(tables):
                    with pool.Fori(0, BLOCKS // 2) as it:
                        for half in range(2):
                            blk = it * 2 + (last_block(a, t, kind, 0) + half)
                            pool.wait_ge(sem("rowfree"), blk * RING + RING)
                            pool.sem_inc(sem("pool_hold"), 1)
                            pool.tensor_copy(IXC[:, half, :], IDX[:, t, bass.ds(it * 2 * RING + half * RING, RING)]
                                             ).then_inc(sem("idxcol"), 1)
                            pool.wait_ge(sem("idxcol"), blk + 1)
                            pool.sem_inc(sem("pool_hold"), 1)
                            for b in range(RING):
                                pool.wait_ge(sem("rowfree"), blk * RING + (RING + b + 1))
                                pool.sem_inc(sem("pool_hold"), 1)
                                pool.indirect_dma_start(ROW[:, b, :], None, table, bass.IndirectOffsetOnAxis(
                                    ap=IXC[:, half, b:b + 1], axis=0)).then_inc(sem(f"row{b}"), 16)

        @block.tensor
        def _(pe):
            for b in range(NBK):
                pe.sem_inc(sem(f"free{b}"), 1)
            for b in range(2):
                pe.sem_inc(sem(f"wbfree{b}"), 1)
                pe.sem_inc(sem(f"wdone{b}"), 1)
            order = []

            def empty(stage, a, i=0):
                b, o = spot(stage, a, i)
                assert b == len(order) % NBK and o == len(order) // NBK, (stage, a, i, len(order))
                order.append(1)
                pe.wait_ge(sem(f"free{b}"), o + 1)
                return bank[b]

            def filled(ins, stage, a, i=0):
                ins.then_inc(sem(f"full{spot(stage, a, i)[0]}"), 1)

            def mm(o, l, r, start=True, stop=True):
                return pe.matmul(o, l, r, start=start, stop=stop)

            def weight_product(rhs, kn, n):
                def body(i, b, o):
                    pe.wait_ge(sem(f"wload{b}"), o * 16 + 16)
                    pe.wait_ge(sem(f"wbfree{b}"), o + 1)
                    w = W[:, b, 0:kn * 256].rearrange("p (k n) -> p k n", k=kn)
                    for h in range(2):
                        for k in range(kn):
                            ins = mm(wbank[b][:, h * n:(h + 1) * n], w[:, k, h * P:(h + 1) * P], rhs(k),
                                     k == 0, k == kn - 1)
                    ins.then_inc(sem(f"wdone{b}"), 1)
                return body

            def fill(a, pause):
                if not filler(a, pause):
                    return
                stage, i, h = filler(a, pause)
                c0 = before(WEIGHTS, stage, a, i)
                b = c0 % 2
                if stage == "mod2":
                    mod_product(i, b, c0 // 2)
                    return
                if h == 0:
                    pe.wait_ge(sem(f"wload{b}"), c0 // 2 * 16 + 16)
                    pe.wait_ge(sem(f"wbfree{b}"), c0 // 2 + 1)
                for k in range(KD):
                    ins = mm(wbank[b][:, h * T:(h + 1) * T], W[:, b, k * 256 + h * P:k * 256 + (h + 1) * P], U[:, k, :],
                             k == 0, k == KD - 1)
                if h:
                    ins.then_inc(sem(f"wdone{b}"), 1)

            def mod_product(i, b, o):
                pe.wait_ge(sem(f"wload{b}"), o * 16 + 16)
                pe.wait_ge(sem(f"wbfree{b}"), o + 1)
                for k in range(KD):
                    ins = mm(wbank[b][0:2, 0:256], CVEC[:, k:16:8], W[:, b, k * 256:(k + 1) * 256], k == 0, k == KD - 1)
                ins.then_inc(sem(f"wdone{b}"), 1)

            def sum_channels(stage, a, lhs, rhs, n, i=0):
                o = empty(stage, a, i)
                for k in range(n):
                    ins = mm(o[:, 0:T], lhs, rhs(k), k == 0, k == n - 1)
                filled(ins, stage, a, i)

            def back(a, stage, src):
                after(pe, "retrieved", src, FULLP)
                for j in range(2 * NT):
                    o = empty(stage, a, j)
                    for k in range(4):
                        at = ((j % 2) * 4 + k) * P
                        ins = pe.transpose(o[:, k * P:(k + 1) * P], ACC[:, j // 2, at:at + P], c("ident"))
                    filled(ins, stage, a, j)

            for a, (l, g, whole) in enumerate(PASSES):
                if a == 0:
                    pe.wait_ge(sem("loaded"), 16 * 8)
                    for j in range(8):
                        o = empty("x_in", a, j)
                        for k in range(4):
                            ins = pe.transpose(o[:, k * P:(k + 1) * P],
                                               ROW[:, j // 2, ((j % 2) * 4 + k) * P:((j % 2) * 4 + k + 1) * P], c("ident"))
                        filled(ins, "x_in", a, j)
                    o = empty("cond", a)
                    filled(pe.transpose(o[:, 0:24], CROW[:], cst[0:24, 0:24]), "cond", a)
                if g == 0:
                    pe.wait_ge(sem("vectors"), 16 * 17 * (l + 1))
                    o = empty("vecs", a)
                    filled(pe.transpose(o[:, 0:NV], VROW[:], cst[0:NV, 0:NV]), "vecs", a)
                    after(pe, "cond_ready", 0)
                    chunks(pe, "mod", a, mod_product)
                    after(pe, "mod_rows", a, (1, 0, 1, 0))
                    o = empty("modt", a)
                    for k in range(2 * dict(WEIGHTS)["mod"][a]):
                        ins = mm(o[:, 2 * k:2 * k + 2], PT[0:2, k * P:(k + 1) * P], cst[0:2, 0:2])
                    filled(ins, "modt", a)
                after(pe, "sq1", a)
                sum_channels("rms1", a, c("ones"), lambda k: F[:, k * T:(k + 1) * T], KD)
                after(pe, "u1", a)
                chunks(pe, "qkvz", a, weight_product(lambda k: U[:, k, :], KD, T))
                o = empty("ab", a)
                for t in range(NT):
                    for k in range(KD):
                        ins = mm(o[:, t * 16:(t + 1) * 16], U[:, k, t * P:(t + 1) * P], WAB[:, k, :], k == 0, k == KD - 1)
                filled(ins, "ab", a)
                chunks(pe, "rest", a, weight_product(lambda k: U[:, k, :], KD, T), 0, EARLY)
                after(pe, "gates_made", a)
                o = empty("cum", a)
                for t in range(NT):
                    for d in range(2):
                        mm(o[:, t * 16 + 4 * d:t * 16 + 4 * d + 4], c(f"tri{d}"), GB[:, t, 4 * d:4 * d + 4])
                    ins = mm(o[:, t * 16 + 8:t * 16 + 16], c("chunk"), GB[:, t, 0:8])
                filled(ins, "cum", a)
                after(pe, "sq_l2", a)
                n2 = 4 if whole else 2
                for j in range(n2):
                    o = empty("l2", a, j)
                    filled(mm(o[:], c("ones"), F[:, (j + 4 - n2) * 512:(j + 5 - n2) * 512]), "l2", a, j)
                chunks(pe, "rest", a, weight_product(lambda k: U[:, k, :], KD, T), EARLY)
                after(pe, "qk_normed", a)
                for j in range(4):
                    o = empty("tok", a, j)
                    for h in range(HEADS):
                        ins = pe.transpose(o[:, h * P:(h + 1) * P],
                                           QC[:, 4 + 4 * (j // 2) + h, (j % 2) * P:(j % 2 + 1) * P], c("ident"))
                    filled(ins, "tok", a, j)
                for d in range(2):
                    for t in range(NT):
                        o = empty(f"decay{d}", a, t)
                        for h in range(HEADS):
                            ins = mm(o[:, h * P:(h + 1) * P],
                                     GB[:, t, 4 * d + h:4 * d + h + 1].to_broadcast([P, P]), c(f"tri{d}"))
                        filled(ins, f"decay{d}", a, t)
                    fill(a, f"decayed{d}")
                    for t in range(NT):
                        o = empty(f"gram{d}", a, t)
                        for h in range(HEADS):
                            k = QC[:, 4 + h, t * P:(t + 1) * P]
                            ins = mm(o[:, h * P:(h + 1) * P], k, k)
                        filled(ins, f"gram{d}", a, t)
                    if whole:
                        for t in range(NT):
                            o = empty(f"qk{d}", a, t)
                            for h in range(HEADS):
                                ins = mm(o[:, h * P:(h + 1) * P], QC[:, 4 + h, t * P:(t + 1) * P],
                                         QC[:, h, t * P:(t + 1) * P])
                            filled(ins, f"qk{d}", a, t)
                    fill(a, f"weighed{d}")
                    ride = a in SERVE
                    for n, (kind, lv) in enumerate(SOLVE):
                        for t in range(NT):
                            i = 2 * n + t
                            if kind == "x":
                                after(pe, "level", a, (24,) * 4, 12 * d + 2 * lv + t)
                                if lv == 1:
                                    after(pe, "x_out", a, (24,) * 4, 12 * d + t)
                                elif lv:
                                    after(pe, "u_out", a, (20,) * 4, 10 * d + 2 * (lv - 2) + t)
                            elif kind == "u":
                                after(pe, "x_out", a, (24,) * 4, 12 * d + 2 * lv + t)
                                if lv > 1:
                                    after(pe, "t_out", a, (16,) * 4, 8 * d + 2 * (lv - 2) + t)
                            o = empty(f"solve{d}", a, i)
                            old, lhs, rhs = {"x": (None, LEVEL[lv % 2], FU), "u": (FU, FT, FX), "t": (FT, FX, FT)}[kind]
                            added = ride and kind != "x"
                            if added:
                                mm(o[:], c("ident"), old[:, t].rearrange("p h n -> p (h n)"), True, False)
                            for h in range(HEADS):
                                oh = o[:, h * P:(h + 1) * P]
                                if (kind, lv) == ("x", 0):
                                    ins = mm(oh, FT[:, t, h, :], c("ident"))
                                else:
                                    ins = mm(oh, lhs[:, t, h, :], rhs[:, t, h, :], not added, not added or h == HEADS - 1)
                            filled(ins, f"solve{d}", a, i)
                        if n + 1 == len(SOLVE) or SOLVE[n + 1][1] > lv:
                            fill(a, f"solved{lv}_{d}")
                    for t in range(NT):
                        after(pe, "u_out", a, (20,) * 4, 10 * d + 8 + t)
                    after(pe, "rhs_in", a, (2,) * 4, d)
                    after(pe, "rhs_v", a, (2,) * 4, d)
                    for t in range(NT):
                        o = empty(f"rhs{d}", a, t)
                        for h in range(HEADS):
                            ins = mm(o[:, h * P:(h + 1) * P], FU[:, t, h, :], FVB[:, t, h, :])
                        filled(ins, f"rhs{d}", a, t)
                    for t in range(NT):
                        o = empty(f"rhs{d}", a, 2 + t)
                        for h in range(HEADS):
                            ins = mm(o[:, h * P:(h + 1) * P], FKB[:, t, h, :], FU[:, t, h, :])
                        filled(ins, f"rhs{d}", a, 2 + t)
                    fill(a, f"righted{d}")
                    after(pe, "w_out", a, (2,) * 4, d)
                    sn = 3 if whole else 2
                    for s in range(4):
                        ch = 3 - s if d else s
                        t, half = ch // 2, ch % 2
                        lo = half * CHUNK
                        o = empty(f"scan{d}", a, sn * s)
                        mm(o[:], c("ident"), FY[:, t].rearrange("p h n -> p (h n)"), True, False)
                        after(pe, "state", a, (10,) * 4, 5 * d + s)
                        for h in range(HEADS):
                            ins = mm(o[:, h * P:(h + 1) * P], FW[:, t, h, :], S[:, d, h, :], False, h == HEADS - 1)
                        filled(ins, f"scan{d}", a, sn * s)
                        o = empty(f"scan{d}", a, sn * s + 1)
                        after(pe, "decayed_state", a, (8,) * 4, 4 * d + s)
                        mm(o[:], c("ident"), FX[:, 0].rearrange("p h n -> p (h n)"), True, False)
                        after(pe, "vnew", a, (8,) * 4, 4 * d + s)
                        for h in range(HEADS):
                            ins = mm(o[:, h * P:(h + 1) * P], FK[:, t, h, :], VN[:, half, h, :], False, h == HEADS - 1)
                        filled(ins, f"scan{d}", a, sn * s + 1)
                        if not whole:
                            continue
                        o = empty(f"scan{d}", a, sn * s + 2)
                        for h in range(HEADS):
                            oh = o[:, h * CHUNK:(h + 1) * CHUNK]
                            if d:
                                mm(oh, c("ident"), OSUM[:, h, ch * CHUNK:(ch + 1) * CHUNK], True, False)
                            mm(oh, S[:, d, h, :], FD[:, t, h, lo:lo + CHUNK], d == 0, False)
                            ins = mm(oh, VN[:, half, h, :], FQ[:, t, h, lo:lo + CHUNK], False, True)
                        filled(ins, f"scan{d}", a, sn * s + 2)
                        fill(a, f"stepped{s}_{d}")
                if whole:
                    after(pe, "sq_g", a, FULLP)
                    for j in range(2):
                        o = empty("gout", a, j)
                        filled(mm(o[:], c("ones"), F[:, j * 512:(j + 1) * 512]), "gout", a, j)
                    fill(a, "gout")
                after(pe, "sq_a", a)
                lo, n = (0, 5) if whole else (4, 1)
                for j in range(3 if whole else 1):
                    w = min(512, n * T - 512 * j)
                    o = empty("an", a, j)
                    filled(mm(o[:, 0:w], c("blk64"), F[:, 2048 + lo * T + j * 512:2048 + lo * T + j * 512 + w]), "an", a, j)
                if g == 1:
                    after(pe, "a_normed", a)
                    for j in range(3):
                        w = min(512, 5 * T - 512 * j)
                        o = empty("rope", a, j)
                        filled(mm(o[:, 0:w], c("rot"), PT[:, T_AQ * T + j * 512:T_AQ * T + j * 512 + w]), "rope", a, j)
                after(pe, "a_turned", a)
                o = empty("dup", a)
                for v in range(KVHEADS):
                    ins = mm(o[:, v * T:(v + 1) * T], c(f"dup{v}"), pt(T_AK))
                filled(ins, "dup", a)
                o = empty("vtok", a)
                for t in range(NT):
                    ins = pe.transpose(o[:, t * P:(t + 1) * P], PT[:, (T_AK + 1) * T + t * P:(T_AK + 1) * T + (t + 1) * P],
                                       c("ident"))
                filled(ins, "vtok", a)
                if not whole:
                    back(a, "back", a - 1)
                    continue
                after(pe, "kv_ready", a)
                k0, kt = (0, 4) if g else (2, 2)
                for n, (kind, i) in enumerate(ATT):
                    t, h = i // AHEADS, i % AHEADS
                    hp = HD * (h % 2)
                    o = empty("att", a, n) if kind != "p" else None
                    if kind == "s":
                        ins = mm(o[:, 0:kt * P], PT[hp:hp + HD, (T_AQ + h // 2) * T + t * P:(T_AQ + h // 2) * T + (t + 1) * P],
                                 KDUP[hp:hp + HD, h // 4, k0 * P:(k0 + kt) * P])
                    elif kind == "p":
                        after(pe, "probs", a, (16, 16, 0, 16), i)
                        o = empty("att", a, n)
                        for k in range(kt):
                            ins = pe.transpose(o[:, k * P:(k + 1) * P], F[:, (i % 2) * 512 + k * P:(i % 2) * 512 + (k + 1) * P],
                                               c("ident"))
                    else:
                        after(pe, "probs_t", a, (16, 16, 0, 16), i)
                        for k in range(kt):
                            ins = mm(o[hp:hp + HD, 0:P], VV[:, k0 + k, (h // 4) * HD:(h // 4 + 1) * HD],
                                     F[:, 1024 + (i % 2) * 512 + k * P:1024 + (i % 2) * 512 + (k + 1) * P],
                                     k == 0, k == kt - 1)
                    filled(ins, "att", a, n)
                    if kind == "o":
                        fill(a, f"att{i}")
                if a in EARLY_GATES:
                    after(pe, "early_out", a, (1, 0, 0, 1))
                if a == 0:
                    o = empty("modt2", a)
                    for k in range(32):
                        ins = mm(o[:, 2 * k:2 * k + 2], MROW[k // 16][0:2, (k % 16) * P:(k % 16 + 1) * P], cst[0:2, 0:2])
                    filled(ins, "modt2", a)
                after(pe, "att_out", a, FULLP)

                def merge(n, i, gate, branch):
                    weight_product(lambda k: U[:, k, :], KD, T)(i, *gate)
                    src = (T_OA, T_OB, T_OC)[n]
                    weight_product(lambda k: pt(src + k), 4, T)(i, *branch)
                if a in EARLY_GATES:
                    for n, src in enumerate((T_OA, T_OB, T_OC)):
                        chunks(pe, "merge", a, weight_product(lambda k: pt(src + k), 4, T), 4 * n, 4 * n + 4)
                else:
                    branch_chunks(pe, a, merge)
                after(pe, "mixed", a, FULLP)
                chunks(pe, "out", a, weight_product(lambda k: pt(T_MIX + k), KD, T))
                after(pe, "sq2", a, FULLP)
                sum_channels("rms2", a, c("ones"), lambda k: F[:, k * T:(k + 1) * T], KD)
                after(pe, "u2", a, FULLP)
                for j in range(4):
                    o = empty("u2t", a, j)
                    for k in range(4):
                        ins = pe.transpose(o[:, k * P:(k + 1) * P], U[:, (j % 2) * 4 + k, (j // 2) * P:(j // 2 + 1) * P],
                                           c("ident"))
                    filled(ins, "u2t", a, j)
                pe.wait_ge(sem("subkeys"), 16 * nth("subkeys", a, FULLP))
                for j in range(2):
                    o = empty("skt", a, j)
                    for k in range(4):
                        ins = pe.transpose(o[:, k * P:(k + 1) * P], SKRAW[:, 4 * j + k, :], c("ident"))
                    filled(ins, "skt", a, j)
                chunks(pe, "query", a, weight_product(lambda k: U[:, k, :], KD, T))
                after(pe, "query_out", a, FULLP)
                for j in range(8):
                    t, q, hb = j // 4, (j // 2) % 2, j % 2
                    o = empty("keys", a, j)
                    for h in range(4):
                        hh = 4 * hb + h
                        ins = mm(o[:, h * P:(h + 1) * P], PT[HD * q:HD * q + HD, (16 + hh) * T + t * P:(16 + hh) * T + (t + 1) * P],
                                 SKT[HD * q:HD * q + HD, hh, :])
                    filled(ins, "keys", a, j)
                if a == 1:
                    back(a, "back", 0)
            back(3, "back_last", 3)
            a = 3
            after(pe, "sq3", 0)
            sum_channels("fin", a, c("ones"), lambda k: F[:, k * T:(k + 1) * T], KD)
            after(pe, "u3", 0)
            for j in range(4):
                o = empty("out", a, j)
                for k in range(4):
                    ins = pe.transpose(o[:, k * P:(k + 1) * P], U[:, (j % 2) * 4 + k, (j // 2) * P:(j // 2 + 1) * P], c("ident"))
                filled(ins, "out", a, j)

        @block.scalar
        def _(act):
            steps = [0]

            def A(o, i, f=ACT.Copy, **k):
                return nc.scalar.activation(o, i, f, **k)

            def link(ins):
                steps[0] += 1
                ins.then_inc(sem("act_step"), 1)

            def settle():
                act.wait_ge(sem("act_step"), steps[0])

            def root(stage, a, i=0):
                n = before(ROOTS, stage, a, i)
                act.wait_ge(sem("var"), n + 1)

            def root_of(dst, src):
                link(A(dst, src, ACT.Ln))
                settle()
                A(dst, dst, ACT.Exp, scale=-0.5).then_inc(sem("root"), 1)

            def move(dst, w=512, first=0):
                def body(i, b, o):
                    act.wait_ge(sem(f"wdone{b}"), o + 2)
                    act.sem_inc(sem("act_hold"), 1)
                    A(dst(i, w), wbank[b][:, 0:w]).then_inc(sem(f"wbfree{b}"), 1)
                return body

            def moved(stage, a, hi=99):
                n = min(hi, dict(WEIGHTS)[stage][a])
                for i in range(max(0, n - 2), n):
                    cc = before(WEIGHTS, stage, a, i)
                    act.wait_ge(sem(f"wbfree{cc % 2}"), cc // 2 + 2)

            def serve(a, point):
                for t, kind, lo, hi in segments(*served(a, point)):
                    if kind == 0 and hi == BLOCKS:
                        src = min(a - 1, 3)
                        after(act, "dots", src, (2, 2, 0, 2), t)
                        mark(A(COEF[:], DOT[:], ACT.Gelu), "gelu")

            def fill(a, pause):
                if not filler(a, pause) or filler(a, pause)[2] == 0:
                    return
                stage, i, _ = filler(a, pause)
                c0 = before(WEIGHTS, stage, a, i)
                b = c0 % 2
                act.wait_ge(sem(f"wdone{b}"), c0 // 2 + 2)
                if stage == "gates":
                    A(GATES[:, i * 512:(i + 1) * 512], wbank[b][:]).then_inc(sem(f"wbfree{b}"), 1)
                else:
                    A(MROW[i // 8][0:2, (i % 8) * 256:(i % 8 + 1) * 256], wbank[b][0:2, 0:256]).then_inc(sem(f"wbfree{b}"), 1)

            for a, (l, g, whole) in enumerate(PASSES):
                if a == 0:
                    for j in range(8):
                        o = full(act, "x_in", a, j)
                        gi, t, hf = j // 4, (j // 2) % 2, j % 2
                        free(A(H[:, gi, 4 * hf:4 * hf + 4, t * P:(t + 1) * P], o[:].rearrange("p (k n) -> p k n", k=4)),
                             "x_in", a, j)
                    o = full(act, "cond", a)
                    link(A(CVEC[:, 16:24], o[:, 16:24]))
                    free(A(CVEC[:, 0:16], o[:, 0:16], ACT.Silu), "cond", a)
                    emptied(act, "cond", a)
                    settle()
                    tell(act, "x_read")
                    tell(act, "cond_ready")
                if a:
                    after(act, "pass_over", a - 1)
                if g == 0:
                    o = full(act, "vecs", a)
                    free(A(VEC[:], o[:, 0:NV]), "vecs", a)

                    def mod(i, b, o):
                        act.wait_ge(sem(f"wdone{b}"), o + 2)
                        act.sem_inc(sem("act_hold"), 1)
                        A(PT[0:2, bass.ds(i * 256, 256)], wbank[b][0:2, 0:256]).then_inc(sem(f"wbfree{b}"), 1)
                    chunks(act, "mod", a, mod, 0, 16)
                    serve(a, "mod")
                    chunks(act, "mod", a, mod, 16)
                    moved("mod", a)
                    tell(act, "mod_rows")
                if a == 0:
                    for j in range(2, 8):
                        emptied(act, "x_in", a, j)
                mark(A(F[:, 0:KD * T], H[:, g].rearrange("p k n -> p (k n)"), ACT.Square), "sq1")
                root("rms1", a)
                root_of(F[:, 2304:2560], F[:, 2048:2304])
                after(act, "scaled1", a)
                for k in range(KD):
                    ins = A(U[:, k, :], U[:, k, :], ACT.Identity, bias=MOD[:, l, k, g:g + 1])
                    mark(ins, "u1") if k == KD - 1 else link(ins)
                if whole:
                    chunks(act, "qkvz", a, move(lambda i, w: PT[:, bass.ds(i * 512, 512)]))
                else:
                    chunks(act, "qkvz", a, move(lambda i, w: PT[:, bass.ds(i * 512 + 4 * T, 512)]))
                moved("qkvz", a)
                tell(act, "qkv_out")
                o = full(act, "ab", a)
                free(A(AB[:].rearrange("p a b -> p (a b)"), o[:, 0:32]), "ab", a)
                emptied(act, "ab", a)
                mark(A(AB[:, :, 8:16], AB[:, :, 8:16], ACT.Sigmoid), "ab_out")
                if whole:
                    rest = move(lambda i, w: PT[:, bass.ds(i * 512 + T_BG * T, 512)])
                else:
                    rest = move(lambda i, w: PT[:, T_AK * T:T_AK * T + 512])
                chunks(act, "rest", a, rest, 0, EARLY // 2)
                serve(a, "proj")
                chunks(act, "rest", a, rest, EARLY // 2, EARLY)
                moved("rest", a, EARLY)
                tell(act, "rest_out")
                after(act, "ab_biased", a)
                link(A(TMPC[:, :, 0:8], AB[:, :, 0:8], ACT.Abs))
                settle()
                link(A(TMPC[:, :, 0:8], TMPC[:, :, 0:8], ACT.Exp, scale=-1.0))
                settle()
                link(A(TMPC[:, :, 0:8], TMPC[:, :, 0:8], ACT.Ln, bias=1.0))
                link(A(TMPC[:, :, 8:16], ADT[:, 0:1, :].to_broadcast([P, NT, 8]), ACT.Exp))
                settle()
                mark(A(AB[:, :, 0:8], AB[:, :, 0:8], ACT.Relu), "softplus")
                q0 = 0 if whole else 4
                after(act, "conv_a", a)
                link(A(QC[:, q0:12, :], QC[:, q0:12, :], ACT.Silu))
                settle()
                mark(A(f3(q0 * T, 8 - q0, T), QC[:, q0:8, :], ACT.Square), "sq_l2")
                o = full(act, "cum", a)
                free(A(GC[:].rearrange("p a b -> p (a b)"), o[:, 0:32]), "cum", a)
                emptied(act, "cum", a)
                tell(act, "cum_out")
                for j in range(4 if whole else 2):
                    root("l2", a, j)
                    root_of(F[:, 4096 + j * 512:4608 + j * 512], F[:, 2048 + j * 512:2560 + j * 512])
                chunks(act, "rest", a, rest, EARLY)
                moved("rest", a)
                serve(a, "l2")
                serve(a, "cols")
                for j in range(4):
                    o = full(act, "tok", a, j)
                    dst = (KTOK if j < 2 else VTOK)[:, j % 2]
                    ins = A(dst, o[:].rearrange("p (h n) -> p h n", h=HEADS))
                    free(ins, "tok", a, j)
                for j in range(4):
                    emptied(act, "tok", a, j)
                after(act, "cum_diff", a)
                mark(A(EGC[:], EGC[:], ACT.Exp), "cum_exp")
                for d in range(2):
                    for t in range(NT):
                        o = full(act, f"decay{d}", a, t)
                        o3 = o[:].rearrange("p (h n) -> p h n", h=HEADS)
                        ends = (CHUNK - 1, P) if d == 0 else (0, P - CHUNK + 1)
                        if d and t == 0:
                            after(act, "state", a, (10,) * 4, 4)
                        link(A(DEC[:, t], o3[:, :, ends[0]:ends[1]:CHUNK], ACT.Exp))
                        mark(A(FD[:, t], o3, ACT.Exp), "eg")
                    for t in range(NT):
                        after(act, "diffs", a, (4,) * 4, 2 * d + t)
                        link(A(FA[:, t], FA[:, t], ACT.Exp, scale=-1.0))
                        mark(A(FQ[:, t], FQ[:, t], ACT.Exp), "decays")
                    serve(a, f"prep{d}0")
                    fill(a, f"decayed{d}")
                    after(act, "columns", a)
                    for t in range(NT):
                        for h in range(HEADS):
                            k = 4 * d + h
                            link(A(FKB[:, t, h, :], KTOK[:, t, h, :], scale=BEG[:, t, k:k + 1]))
                            link(A(FK[:, t, h, :], KTOK[:, t, h, :], scale=EGC[:, t, 8 + k:9 + k]))
                    fill(a, f"weighed{d}")
                    for kind, lv in SOLVE:
                        if kind == "x":
                            for t in range(NT):
                                i = 2 * SOLVE.index(("x", lv)) + t
                                o = full(act, f"solve{d}", a, i)
                                ins = A((FX if lv else FU)[:, t], o[:].rearrange("p (h n) -> p h n", h=HEADS),
                                        scale=-1.0 if lv else 1.0)
                                free(ins, f"solve{d}", a, i)
                                emptied(act, f"solve{d}", a, i)
                                tell(act, "x_out")
                        elif a in SERVE:
                            for t in range(NT):
                                i = 2 * SOLVE.index((kind, lv)) + t
                                o = full(act, f"solve{d}", a, i)
                                free(A((FU if kind == "u" else FT)[:, t], o[:].rearrange("p (h n) -> p h n", h=HEADS)),
                                     f"solve{d}", a, i)
                                emptied(act, f"solve{d}", a, i)
                                tell(act, f"{kind}_out")
                        if kind == "x" and lv == 5:
                            for t in range(NT):
                                for h in range(HEADS):
                                    ins = A(FVB[:, t, h, :], VTOK[:, t, h, :], scale=GB[:, t, 8 + 4 * d + h:9 + 4 * d + h])
                                    link(ins)
                            settle()
                            tell(act, "rhs_v")
                        if (kind, lv) in (("x", 0), ("u", 5)) or kind == ("t" if a in SERVE else "x") and 0 < lv < 5:
                            serve(a, f"solve{d}{lv}")
                            fill(a, f"solved{lv}_{d}")
                    for t in range(NT):
                        o = full(act, f"rhs{d}", a, t)
                        free(A(FY[:, t], o[:].rearrange("p (h n) -> p h n", h=HEADS)), f"rhs{d}", a, t)
                    for t in range(NT):
                        o = full(act, f"rhs{d}", a, 2 + t)
                        free(A(FW[:, t], o[:].rearrange("p (h n) -> p h n", h=HEADS), scale=-1.0), f"rhs{d}", a, 2 + t)
                    for t in range(2 * NT):
                        emptied(act, f"rhs{d}", a, t)
                    tell(act, "w_out")
                    fill(a, f"righted{d}")
                    tell(act, "state")
                    sn = 3 if whole else 2
                    for s in range(4):
                        ch = 3 - s if d else s
                        t, half = ch // 2, ch % 2
                        hr = slice(half * CHUNK, (half + 1) * CHUNK)
                        for h in range(HEADS):
                            link(A(FX[:, 0, h, :], S[:, d, h, :], scale=DEC[:, t, h, half:half + 1]))
                        settle()
                        tell(act, "decayed_state")
                        o = full(act, f"scan{d}", a, sn * s)
                        free(A(VN[hr, half], o[hr, :].rearrange("p (h n) -> p h n", h=HEADS)), f"scan{d}", a, sn * s)
                        emptied(act, f"scan{d}", a, sn * s)
                        tell(act, "vnew")
                        o = full(act, f"scan{d}", a, sn * s + 1)
                        if whole:
                            full(act, f"scan{d}", a, sn * s + 2)
                        free(A(S[:, d], o[:].rearrange("p (h n) -> p h n", h=HEADS)), f"scan{d}", a, sn * s + 1)
                        emptied(act, f"scan{d}", a, sn * s + 1)
                        tell(act, "state")
                        if whole:
                            o = full(act, f"scan{d}", a, sn * s + 2)
                            free(A(OSUM[:, :, ch * CHUNK:(ch + 1) * CHUNK], o[:, 0:256].rearrange("p (h n) -> p h n", h=HEADS)),
                                 f"scan{d}", a, sn * s + 2)
                            emptied(act, f"scan{d}", a, sn * s + 2)
                        serve(a, f"scan{d}{s}")
                        fill(a, f"stepped{s}_{d}")
                if whole:
                    link(A(pt(T_Z, 4), pt(T_Z, 4), ACT.Silu))
                    settle()
                    mark(A(F[:, 0:1024], pt(T_OSUM, 4), ACT.Square), "sq_g")
                    for j in range(2):
                        root("gout", a, j)
                        root_of(F[:, 4096 + j * 512:4608 + j * 512], F[:, 2048 + j * 512:2560 + j * 512])
                    fill(a, "gout")
                    after(act, "branch_a", a, FULLP)
                lo, n = (0, 5) if whole else (4, 1)
                serve(a, "gout")
                mark(A(F[:, 2048 + lo * T:2048 + (lo + n) * T], PT[:, (T_AQ + lo) * T:(T_AQ + lo + n) * T], ACT.Square), "sq_a")
                for j in range(3 if whole else 1):
                    w = min(512, n * T - 512 * j)
                    root("an", a, j)
                    root_of(F[:, 6144 + j * 512:6144 + j * 512 + w], F[:, 4096 + j * 512:4096 + j * 512 + w])
                o = full(act, "dup", a)
                free(A(KDUP[:, :, (1 - g) * T:(2 - g) * T], o[:].rearrange("p (v n) -> p v n", v=2)), "dup", a)
                o = full(act, "vtok", a)
                free(A(VV[:, NT * (1 - g):NT * (2 - g), :], o[:, 0:T].rearrange("p (t n) -> p t n", t=NT)), "vtok", a)
                emptied(act, "dup", a)
                emptied(act, "vtok", a)
                tell(act, "kv_ready")
                serve(a, "turn")
                if not whole:
                    serve(a, "rest")
                    continue
                kt = 4 if g else 2
                for n, (kind, i) in enumerate(ATT):
                    if kind == "s":
                        after(act, "maxed", a, (16, 16, 0, 16), i)
                        o = full(act, "att", a, n)
                        free(A(F[:, (i % 2) * 512:(i % 2) * 512 + kt * P], o[:, 0:kt * P], ACT.Exp, scale=HD ** -0.5,
                               bias=SM[:, 0, i % 2:i % 2 + 1], accum_out=SM[:, 0, 2 + i % 2:3 + i % 2]), "att", a, n)
                    elif kind == "p":
                        o = full(act, "att", a, n)
                        free(A(F[:, 1024 + (i % 2) * 512:1024 + (i % 2) * 512 + kt * P], o[:, 0:kt * P]), "att", a, n)
                        emptied(act, "att", a, n)
                        tell(act, "probs_t")
                        serve(a, f"att{i}")
                        fill(a, f"att{i}")

                def merge(n, i, gate, branch):
                    b, o = gate
                    act.wait_ge(sem(f"wdone{b}"), o + 2)
                    act.wait_ge(sem("sgfree"), i + (nth("sgfree", a, (0, 12, 0, 0), 4 * n)))
                    act.sem_inc(sem("act_hold"), 1)
                    A(F[:, 0:512], wbank[b][:], ACT.Sigmoid).then_inc(sem(f"wbfree{b}"), 1)
                after(act, "att_out", a, FULLP)
                if a in EARLY_GATES:
                    moved("gates", a)
                    moved("mod2", a)
                    tell(act, "early_out")
                    for n in range(3):
                        mark(A(GATES[:, n * 2048:(n + 1) * 2048], GATES[:, n * 2048:(n + 1) * 2048], ACT.Sigmoid), "gates_out")
                else:
                    branch_chunks(act, a, merge)
                after(act, "h_mid", a, FULLP)
                mark(A(F[:, 0:KD * T], H[:, g].rearrange("p k n -> p (k n)"), ACT.Square), "sq2")
                root("rms2", a)
                root_of(F[:, 2304:2560], F[:, 2048:2304])
                after(act, "scaled2", a, FULLP)
                for k in range(KD):
                    ins = A(U[:, k, :], U[:, k, :], ACT.Identity, bias=MOD[:, l, 24 + k, g:g + 1])
                    mark(ins, "u2") if k == KD - 1 else link(ins)
                for j in range(4):
                    o = full(act, "u2t", a, j)
                    free(A(U2[:, j // 2, (j % 2) * 512:(j % 2) * 512 + 512], o[:]), "u2t", a, j)
                for j in range(2):
                    o = full(act, "skt", a, j)
                    free(A(SKT[:, 4 * j:4 * j + 4, :], o[:].rearrange("p (h n) -> p h n", h=4)), "skt", a, j)
                chunks(act, "query", a, move(lambda i, w: PT[:, bass.ds(i * 512 + 16 * T, 512)]))
                moved("query", a)
                for j in range(2):
                    emptied(act, "skt", a, j)
                for j in range(4):
                    emptied(act, "u2t", a, j)
                tell(act, "query_out")
                for t in range(NT):
                    after(act, "best", a, (2, 2, 0, 2), t)
                    mark(A(GATE[:, t, :], GATE[:, t, :], ACT.Exp), "gate_exp")
            serve(4, "")
            after(act, "h_done", 0)
            mark(A(F[:, 0:KD * T], H[:, 1].rearrange("p k n -> p (k n)"), ACT.Square), "sq3")
            root("fin", 3)
            root_of(F[:, 2304:2560], F[:, 2048:2304])
            for j in range(4):
                o = full(act, "out", 3, j)
                free(A(U2[:, j // 2, (j % 2) * 512:(j % 2) * 512 + 512], o[:]), "out", 3, j)
            for j in range(4):
                emptied(act, "out", 3, j)
            tell(act, "result")

        @block.vector
        def _(dve):
            steps = [0]
            v = nc.vector

            def post(ins):
                steps[0] += 1
                ins.then_inc(sem("dve_step"), 1)

            def settle():
                dve.wait_ge(sem("dve_step"), steps[0])

            def step(ins):
                post(ins)
                settle()

            def rsqrt(stage, a, i, w, scale, at, rt, tmp):
                o = full(dve, stage, a, i)
                free(v.tensor_scalar(F[:, at:at + w], o[:, 0:w], scale, EPS, ALU.mult, ALU.add), stage, a, i)
                emptied(dve, stage, a, i)
                dve.sem_inc(sem("var"), 1)
                dve.wait_ge(sem("root"), before(ROOTS, stage, a, i) + 1)
                x, y, z = F[:, at:at + w], F[:, rt:rt + w], F[:, tmp:tmp + w]
                step(v.scalar_tensor_tensor(out=z, in0=y, scalar=-0.5, in1=y, op0=ALU.mult, op1=ALU.mult))
                step(v.tensor_tensor(z, z, x, ALU.mult))
                step(v.scalar_tensor_tensor(out=y, in0=z, scalar=1.5, in1=y, op0=ALU.add, op1=ALU.mult))
                return y

            def conv(dst, src, w, n):
                for i in range(n):
                    post(v.tensor_scalar(dst(i), src(i), w(1, i), None, ALU.mult))
                settle()
                for i in range(n):
                    post(v.scalar_tensor_tensor(out=dst(i)[:, 1:T], in0=src(i)[:, 0:T - 1], scalar=w(0, i),
                                                in1=dst(i)[:, 1:T], op0=ALU.mult, op1=ALU.add))
                settle()
                for i in range(n):
                    post(v.scalar_tensor_tensor(out=dst(i)[:, 0:T - 1], in0=src(i)[:, 1:T], scalar=w(2, i),
                                                in1=dst(i)[:, 0:T - 1], op0=ALU.mult, op1=ALU.add))
                settle()

            def bc(ap, n):
                return ap.unsqueeze(len(ap.shape)).to_broadcast(list(ap.shape) + [n])

            step(v.memset(VN[:], 0.0))
            step(v.memset(SM[:], 0.0))
            for _ in range(2 * RING):
                dve.sem_inc(sem("rowfree"), 1)

            def rows(src, t, kind, blk):
                g0 = last_block(src, t, kind, 0)
                for b in range(RING):
                    dve.wait_ge(sem(f"row{b}"), blk * 16 + (g0 * 16 + 16))
                    col = bass.ds(blk * RING + b, 1)
                    if kind == 0:
                        v.scalar_tensor_tensor(out=ROW[:, b, :], in0=ROW[:, b, :], scalar=1.0, in1=U2[:, t, :], op0=ALU.mult,
                                               op1=ALU.mult, accum_out=DOT[:, col]).then_inc(sem("rowfree"), 1)
                    else:
                        v.scalar_tensor_tensor(out=ACC[:, t, :], in0=ROW[:, b, :], scalar=COEF[:, col], in1=ACC[:, t, :],
                                               op0=ALU.mult, op1=ALU.add).then_inc(sem("rowfree"), 1)
                        dve.wait_ge(sem("rowfree"), blk * RING + (g0 * RING + 2 * RING + b + 1))

            def open_segment(src, t, kind, lo):
                if kind and lo == 0:
                    after(dve, "gelu", src, (2, 2, 0, 2), t)
                    step(v.tensor_tensor(COEF[:], COEF[:], GATE[:, t, :], ALU.mult))
                    step(v.memset(ACC[:, t, :], 0.0))

            def close_segment(src, t, kind, hi):
                if kind == 0 and hi == BLOCKS:
                    dve.wait_ge(sem("rowfree"), (last_block(src, t, 0, BLOCKS) + 2) * RING)
                    tell(dve, "dots")

            def serve(a, point):
                src = a if point.startswith("own") else min(a - 1, 3)
                for t, kind, lo, hi in segments(*served(a, point)):
                    open_segment(src, t, kind, lo)
                    if hi - lo > 2:
                        with dve.Fori(lo, hi) as i:
                            rows(src, t, kind, i)
                    else:
                        for i in range(lo, hi):
                            rows(src, t, kind, i)
                    close_segment(src, t, kind, hi)

            def back(a, stage, src):
                tell(dve, "retrieved")
                l, g, _ = PASSES[src]
                for j in range(2 * NT):
                    o = full(dve, stage, a, j)
                    for k in range(4):
                        kk = 4 * (j % 2) + k
                        hh = H[:, g, kk, (j // 2) * P:(j // 2 + 1) * P]
                        ins = v.scalar_tensor_tensor(out=hh, in0=o[:, k * P:(k + 1) * P], scalar=MOD[:, l, 40 + kk, g:g + 1],
                                                     in1=hh, op0=ALU.mult, op1=ALU.add)
                        post(ins) if k < 3 else free(ins, stage, a, j)
                    emptied(dve, stage, a, j)

            def gains(l, n):
                vn, sc = ((V_N1, 8), (V_N2, 32))[n]
                step(v.tensor_scalar(A12[:, n], MOD[:, l, sc:sc + 8, :], 1.0, None, ALU.add))
                step(v.tensor_tensor(A12[:, n], A12[:, n], bc(VEC[:, vn:vn + 8], 2), ALU.mult))

            dve.sem_inc(sem("sgfree"), 1)
            for a, (l, g, whole) in enumerate(PASSES):
                if g == 0:
                    serve(a, "mod")
                    o = full(dve, "modt", a)
                    emptied(dve, "vecs", a)
                    n = 2 * dict(WEIGHTS)["mod"][a]
                    free(v.tensor_tensor(MOD[:, l, 0:n], o[:, 0:2 * n].rearrange("p (a b) -> p a b", b=2),
                                         bc(VEC[:, V_BMOD:V_BMOD + n], 2), ALU.add), "modt", a)
                    emptied(dve, "modt", a)
                    gains(l, 0)
                    if n == 48:
                        gains(l, 1)
                rs = rsqrt("rms1", a, 0, T, 1.0 / D, 2048, 2304, 2560)
                for k in range(KD):
                    ins = v.scalar_tensor_tensor(out=U[:, k, :], in0=H[:, g, k, :], scalar=A12[:, 0, k, g:g + 1],
                                                 in1=rs, op0=ALU.mult, op1=ALU.mult)
                    mark(ins, "scaled1") if k == KD - 1 else post(ins)
                serve(a, "proj")
                after(dve, "ab_out", a)
                mark(v.tensor_tensor(AB[:, :, 0:8], AB[:, :, 0:8], ADT[:, 1:2, :].to_broadcast([P, NT, 8]), ALU.add),
                     "ab_biased")
                q0 = 0 if whole else 4
                conv(lambda i: QC[:, q0 + i, :], lambda i: pt(T_QKV + q0 + i),
                     lambda j, i: VEC[:, V_CA + 12 * j + q0 + i:V_CA + 12 * j + q0 + i + 1], 12 - q0)
                tell(dve, "conv_a")
                serve(a, "gates")
                after(dve, "softplus", a)
                step(v.tensor_tensor(TMPC[:, :, 0:8], TMPC[:, :, 0:8], AB[:, :, 0:8], ALU.add))
                step(v.tensor_copy(GB[:, :, 8:16], AB[:, :, 8:16]))
                mark(v.scalar_tensor_tensor(out=GB[:, :, 0:8], in0=TMPC[:, :, 0:8], scalar=-1.0, in1=TMPC[:, :, 8:16],
                                            op0=ALU.mult, op1=ALU.mult), "gates_made")
                for j in range(4 if whole else 2):
                    jj = j if whole else j + 2
                    y = rsqrt("l2", a, j, 512, 1.0, 2048 + j * 512, 4096 + j * 512, 6144 + j * 512)
                    qk = QC[:, 2 * jj:2 * jj + 2, :].rearrange("p a b -> p (a b)")
                    ins = v.scalar_tensor_tensor(out=qk, in0=qk, scalar=P ** -0.5 if jj < 2 else 1.0, in1=y,
                                                 op0=ALU.mult, op1=ALU.mult)
                    mark(ins, "qk_normed") if jj == 3 else post(ins)
                if whole:
                    after(dve, "rest_out", a)
                    step(v.tensor_tensor(pt(T_CG, 4), pt(T_CG, 4), pt(T_XIN, 4), ALU.mult))
                    conv(lambda i: pt(T_XIN + i), lambda i: pt(T_CG + i),
                         lambda j, i: VEC[:, V_CB + 4 * j + i:V_CB + 4 * j + i + 1], 4)
                    step(v.tensor_tensor(pt(T_OB, 4), pt(T_BG, 4), pt(T_XIN, 4), ALU.mult))
                serve(a, "l2")
                after(dve, "cum_out", a)
                post(v.tensor_copy(EGC[:, :, 0:8], GC[:, :, 0:8]))
                mark(v.tensor_tensor(EGC[:, :, 8:16], GC[:, :, 8:16], GC[:, :, 0:8], ALU.subtract), "cum_diff")
                after(dve, "cum_exp", a)
                mark(v.tensor_tensor(BEG[:], EGC[:, :, 0:8], GB[:, :, 8:16], ALU.mult), "columns")
                after(dve, "columns", a)
                serve(a, "cols")
                for d in range(2):
                    if d:
                        after(dve, "state", a, (10,) * 4, 4)
                    if g == 0:
                        step(v.memset(S[:, d], 0.0))
                    for t in range(NT):
                        o = full(dve, f"decay{d}", a, t)
                        after(dve, "eg", a, (4,) * 4, 2 * d + t)
                        for h in range(HEADS):
                            col = GC[:, t, 4 * d + h:4 * d + h + 1]
                            post(v.tensor_scalar(FA[:, t, h, :], o[:, h * P:(h + 1) * P], col, 0.0, ALU.subtract, ALU.max))
                            ins = v.tensor_scalar(FQ[:, t, h, :], o[:, h * P:(h + 1) * P], col, 0.0, ALU.subtract, ALU.min)
                            if h < HEADS - 1:
                                post(ins)
                            else:
                                free(ins, f"decay{d}", a, t)
                        emptied(dve, f"decay{d}", a, t)
                        tell(dve, "diffs")
                    for t in range(NT):
                        if whole:
                            step(v.tensor_tensor(FD[:, t], FD[:, t], QC[:, 0:HEADS, t * P:(t + 1) * P], ALU.mult))
                    settle()
                    tell(dve, "rhs_in")
                    serve(a, f"prep{d}0")
                    for t in range(NT):
                        after(dve, "decays", a, (4,) * 4, 2 * d + t)
                        m = c(f"str{d}").unsqueeze(1).to_broadcast([P, HEADS, P])
                        step(v.tensor_tensor(FA[:, t], FA[:, t], m, ALU.mult))
                        o = full(dve, f"gram{d}", a, t)
                        for h in range(HEADS):
                            ins = v.scalar_tensor_tensor(out=FA[:, t, h, :], in0=o[:, h * P:(h + 1) * P],
                                                         scalar=GB[:, t, 8 + 4 * d + h:9 + 4 * d + h], in1=FA[:, t, h, :],
                                                         op0=ALU.mult, op1=ALU.mult)
                            post(ins) if h < HEADS - 1 else free(ins, f"gram{d}", a, t)
                        emptied(dve, f"gram{d}", a, t)
                    if whole:
                        for t in range(NT):
                            m = c(f"tri{d}").unsqueeze(1).to_broadcast([P, HEADS, P])
                            step(v.tensor_tensor(FQ[:, t], FQ[:, t], m, ALU.mult))
                            o = full(dve, f"qk{d}", a, t)
                            free(v.tensor_tensor(FQ[:, t], FQ[:, t], o[:].rearrange("p (h n) -> p h n", h=HEADS), ALU.mult),
                                 f"qk{d}", a, t)
                            emptied(dve, f"qk{d}", a, t)

                    def level(lv):
                        for t in range(NT):
                            ins = v.tensor_tensor(LEVEL[lv % 2][:, t], FA[:, t],
                                                  c(f"lv{lv}").unsqueeze(1).to_broadcast([P, HEADS, P]), ALU.mult)
                            mark(ins, "level") if lv else step(ins)
                        if lv == 0:
                            for t in range(NT):
                                mark(v.tensor_tensor(FT[:, t], c("ident").unsqueeze(1).to_broadcast([P, HEADS, P]),
                                                     LEVEL[0][:, t], ALU.subtract), "level")
                            after(dve, "level", a, (24,) * 4, 12 * d + 1)
                    for lv in range(3):
                        level(lv)
                    serve(a, f"solve{d}0")
                    for lv in range(1, 6):
                        if lv + 2 < 6:
                            after(dve, "x_out", a, (24,) * 4, 12 * d + 2 * lv + 1)
                            level(lv + 2)
                        if a in SERVE:
                            serve(a, f"solve{d}{lv}")
                            continue
                        for kind, dst in (("u", FU), ("t", FT)):
                            if (kind, lv) not in SOLVE:
                                continue
                            for t in range(NT):
                                i = 2 * SOLVE.index((kind, lv)) + t
                                o = full(dve, f"solve{d}", a, i)
                                free(v.tensor_tensor(dst[:, t], dst[:, t], o[:].rearrange("p (h n) -> p h n", h=HEADS),
                                                     ALU.add), f"solve{d}", a, i)
                                emptied(dve, f"solve{d}", a, i)
                                tell(dve, f"{kind}_out")
                    for s in range(4):
                        serve(a, f"scan{d}{s}")
                if whole:
                    for j in range(2):
                        y = rsqrt("gout", a, j, 512, 1.0 / P, 2048 + j * 512, 4096 + j * 512, 6144 + j * 512)
                        step(v.scalar_tensor_tensor(out=y, in0=y, scalar=VEC[:, V_GN:V_GN + 1], in1=pt(T_Z + 2 * j, 2),
                                                    op0=ALU.mult, op1=ALU.mult))
                        ins = v.tensor_tensor(pt(T_OA + 2 * j, 2), pt(T_OSUM + 2 * j, 2), y, ALU.mult)
                        mark(ins, "branch_a") if j else post(ins)
                serve(a, "gout")
                lo, n = (0, 5) if whole else (4, 1)
                for j in range(3 if whole else 1):
                    w = min(512, n * T - 512 * j)
                    y = rsqrt("an", a, j, w, 1.0 / HD, 4096 + j * 512, 6144 + j * 512, 8192 + j * 512)
                    at = (T_AQ + lo) * T + j * 512
                    col = V_KN if (not whole or j == 2) else V_QN
                    ins = v.scalar_tensor_tensor(out=PT[:, at:at + w], in0=PT[:, at:at + w], scalar=VEC[:, col:col + 1], in1=y,
                                                 op0=ALU.mult, op1=ALU.mult)
                    step(ins)
                if g:
                    tell(dve, "a_normed")
                    cos, sin = cst[:, C_COS:C_COS + T], cst[:, C_SIN:C_SIN + T]
                    for j in range(3):
                        w = min(512, 5 * T - 512 * j)
                        n2 = w // T
                        o = full(dve, "rope", a, j)
                        free(v.tensor_tensor(f3(4096 + j * 512, n2, T), o[:, 0:w].rearrange("p (a b) -> p a b", b=T),
                                             sin.unsqueeze(1).to_broadcast([P, n2, T]), ALU.mult), "rope", a, j)
                        emptied(dve, "rope", a, j)
                    for j in range(3):
                        n2 = min(2, 5 - 2 * j)
                        q = pt3(T_AQ + 2 * j, n2)
                        step(v.tensor_tensor(q, q, cos.unsqueeze(1).to_broadcast([P, n2, T]), ALU.mult))
                        step(v.tensor_tensor(q, q, f3(4096 + j * 512, n2, T), ALU.add))
                else:
                    tell(dve, "a_normed")
                tell(dve, "a_turned")
                serve(a, "turn")
                if not whole:
                    serve(a, "rest")
                    back(a, "back", a - 1)
                    tell(dve, "pass_over")
                    continue
                kt = 4 if g else 2

                def normalise(i):
                    n = ATT.index(("s", i))
                    emptied(dve, "att", a, n)
                    step(v.reciprocal(SM[:, 0, 2 + i % 2:3 + i % 2], SM[:, 0, 2 + i % 2:3 + i % 2]))
                    mark(v.tensor_scalar(F[:, (i % 2) * 512:(i % 2) * 512 + kt * P], F[:, (i % 2) * 512:(i % 2) * 512 + kt * P],
                                         SM[:, 0, 2 + i % 2:3 + i % 2], None, ALU.mult), "probs")
                for n, (kind, i) in enumerate(ATT):
                    t, h = i // AHEADS, i % AHEADS
                    if kind == "s":
                        o = full(dve, "att", a, n)
                        if i >= 2:
                            full(dve, "att", a, ATT.index(("p", i - 2)))
                        step(v.tensor_reduce(SM[:, 0, i % 2:i % 2 + 1], o[:, 0:kt * P], AX.X, ALU.max))
                        mark(v.tensor_scalar(SM[:, 0, i % 2:i % 2 + 1], SM[:, 0, i % 2:i % 2 + 1], -(HD ** -0.5), None, ALU.mult),
                             "maxed")
                        serve(a, f"att{i - 1}") if i else None
                        normalise(i)
                    elif kind == "o":
                        hp = HD * (h % 2)
                        o = full(dve, "att", a, n)
                        at = (T_OC + h // 2) * T + t * P
                        free(v.tensor_copy(PT[hp:hp + HD, at:at + P], o[hp:hp + HD, 0:P]), "att", a, n)
                        emptied(dve, "att", a, n)
                tell(dve, "att_out")

                def merge(n, i, gate, branch):
                    gb, go = gate
                    bb, bo = branch
                    dve.wait_ge(sem(f"wbfree{gb}"), go + 2)
                    dve.wait_ge(sem(f"wdone{bb}"), bo + 2)
                    if n == 0:
                        v.tensor_tensor(PT[:, bass.ds(i * 512 + T_MIX * T, 512)], F[:, 0:512], wbank[bb][:], ALU.mult).then_inc(
                            sem(f"wbfree{bb}"), 1)
                    else:
                        v.tensor_tensor(F[:, 512:1024], F[:, 0:512], wbank[bb][:], ALU.mult).then_inc(sem(f"wbfree{bb}"), 1)
                        dve.wait_ge(sem(f"wbfree{bb}"), bo + 2)
                        m = PT[:, bass.ds(i * 512 + T_MIX * T, 512)]
                        v.tensor_tensor(m, m, F[:, 512:1024], ALU.add).then_inc(sem("mixstep"), 1)
                        dve.wait_ge(sem("mixstep"), i + (1 + 8 * sum(FULLP[:a]) + 4 * (n - 1)))
                    dve.wait_ge(sem(f"wbfree{bb}"), bo + 2)
                    dve.sem_inc(sem("sgfree"), 1)
                    for t, kind, lo, hi in segments(*served(a, f"merge{n}")):
                        rows(a - 1, t, kind, i + lo)
                def early_merge(n, i, b, o):
                    dve.wait_ge(sem(f"wdone{b}"), o + 2)
                    gate = GATES[:, bass.ds(i * 512, 512)]
                    m = PT[:, bass.ds(i * 512 + (T_MIX * T - 4 * n * 512), 512)]
                    if n == 0:
                        v.tensor_tensor(m, gate, wbank[b][:], ALU.mult).then_inc(sem(f"wbfree{b}"), 1)
                    else:
                        v.tensor_tensor(F[:, 512:1024], gate, wbank[b][:], ALU.mult).then_inc(sem(f"wbfree{b}"), 1)
                        dve.wait_ge(sem(f"wbfree{b}"), o + 2)
                        v.tensor_tensor(m, m, F[:, 512:1024], ALU.add).then_inc(sem("mixstep"), 1)
                        dve.wait_ge(sem("mixstep"), i + (1 + 8 * sum(FULLP[:a]) - 4))
                    dve.wait_ge(sem(f"wbfree{b}"), o + 2)
                if a in EARLY_GATES:
                    if a == 0:
                        o = full(dve, "modt2", a)
                        free(v.tensor_tensor(MOD[:, l, 16:48], o[:, 0:64].rearrange("p (a b) -> p a b", b=2),
                                             bc(VEC[:, V_BMOD + 16:V_BMOD + 48], 2), ALU.add), "modt2", a)
                        emptied(dve, "modt2", a)
                        gains(l, 1)
                    for n in range(3):
                        after(dve, "gates_out", a, (3, 0, 0, 3), n)
                        chunks(dve, "merge", a, lambda i, b, o: early_merge(n, i, b, o), 4 * n, 4 * n + 4)
                else:
                    for t, kind, lo, hi in segments(*served(a, "merge0")):
                        open_segment(a - 1, t, kind, lo)
                    branch_chunks(dve, a, merge)
                tell(dve, "mixed")

                def residual(i, b, o):
                    dve.wait_ge(sem(f"wdone{b}"), o + 2)
                    h2 = H[:, g].rearrange("p k n -> p (k n)")
                    gcol = MOD[:, l, 16:24, :].rearrange("p k n -> p (k n)")
                    for j in range(2):
                        hh = h2[:, bass.ds(i * 512 + j * T, T)]
                        ins = v.scalar_tensor_tensor(out=hh, in0=wbank[b][:, j * T:(j + 1) * T],
                                                     scalar=gcol[:, bass.ds(i * 4 + 2 * j + g, 1)], in1=hh,
                                                     op0=ALU.mult, op1=ALU.add)
                        if j:
                            ins.then_inc(sem(f"wbfree{b}"), 1)
                serve(a, "out")
                chunks(dve, "out", a, residual)
                for i in (2, 3):
                    cc = before(WEIGHTS, "out", a, i)
                    dve.wait_ge(sem(f"wbfree{cc % 2}"), cc // 2 + 2)
                tell(dve, "h_mid")
                rs = rsqrt("rms2", a, 0, T, 1.0 / D, 2048, 2304, 2560)
                full(dve, "rms2", a)
                for k in range(KD):
                    ins = v.scalar_tensor_tensor(out=U[:, k, :], in0=H[:, g, k, :], scalar=A12[:, 1, k, g:g + 1],
                                                 in1=rs, op0=ALU.mult, op1=ALU.mult)
                    mark(ins, "scaled2") if k == KD - 1 else post(ins)
                serve(a, "query")
                after(dve, "query_out", a, FULLP)
                for t in range(NT):
                    sc = F[:, 0:2048].rearrange("p (r n) -> p r n", n=P)
                    s2 = F[:, 2048:4096].rearrange("p (r n) -> p r n", n=P)
                    for j in range(4):
                        o = full(dve, "keys", a, 4 * t + j)
                        free(v.tensor_copy(F[:, j * 512:(j + 1) * 512], o[:]), "keys", a, 4 * t + j)
                    for j in range(4):
                        emptied(dve, "keys", a, 4 * t + j)

                    def beside(i):
                        if t:
                            serve(a, f"own{i}")

                    def top16(vals, spare, best, at, n):
                        for r in range(n):
                            post(v.max(best[:, r, 0:8], vals[:, r, :]))
                        settle()
                        for r in range(n):
                            post(v.max_index(at[:, r, 0:8], best[:, r, 0:8], vals[:, r, :]))
                            post(v.match_replace(spare[:, r, :], best[:, r, 0:8], vals[:, r, :], NEG))
                        settle()
                        for r in range(n):
                            post(v.max(best[:, r, 8:16], spare[:, r, :]))
                        settle()
                        for r in range(n):
                            post(v.max_index(at[:, r, 8:16], best[:, r, 8:16], spare[:, r, :]))
                        settle()

                    beside(0)
                    top16(sc, s2, TOPV, TOPI, 16)
                    beside(1)
                    beside(2)
                    cand = F[:, 4096:6144].rearrange("p (h n) -> p h n", n=256)
                    cand2 = F[:, 6144:8192].rearrange("p (h n) -> p h n", n=256)
                    for h in range(PHEADS):
                        post(v.tensor_tensor(cand[:, h].rearrange("p (x y) -> p x y", x=TOPK), bc(TOPV[:, h, :], TOPK),
                                             TOPV[:, 8 + h, :].unsqueeze(1).to_broadcast([P, TOPK, TOPK]), ALU.add))
                    tif = F[:, 8192:8448].rearrange("p (r n) -> p r n", n=TOPK)
                    step(v.tensor_copy(tif, TOPI))
                    top16(cand, cand2, BV, BJ[:, 0], PHEADS)
                    beside(3)
                    beside(4)
                    step(v.tensor_scalar(BJ[:, 1], BJ[:, 0], 4, None, ALU.logical_shift_right))
                    step(v.tensor_scalar(BJ[:, 2], BJ[:, 0], 15, None, ALU.bitwise_and))
                    ab = F[:, 8448:8704].rearrange("p (q n) -> p q n", q=2)
                    step(v.tensor_copy(ab.rearrange("p q n -> p (q n)"), BJ[:, 1:3].rearrange("p q h n -> p (q h n)")))
                    iota = cst[:, C_IOTA:C_IOTA + TOPK].unsqueeze(1).to_broadcast([P, SLOTS, TOPK])
                    pick = F[:, 8704:8960].rearrange("p (q n) -> p q n", q=2)
                    for q in range(2):
                        hot = F[:, 0:2048].rearrange("p (s x) -> p s x", x=TOPK)
                        step(v.tensor_tensor(hot, bc(ab[:, q], TOPK), iota, ALU.is_equal))
                        for h in range(PHEADS):
                            hh = hot[:, h * TOPK:(h + 1) * TOPK, :]
                            post(v.tensor_tensor(hh, hh, tif[:, 8 * q + h, :].unsqueeze(1).to_broadcast([P, TOPK, TOPK]),
                                                 ALU.mult))
                        settle()
                        step(v.tensor_reduce(pick[:, q], hot, AX.X, ALU.add))
                        beside(5 + q)
                    step(v.tensor_scalar(pick[:, 0], pick[:, 0], float(NKEYS), float(l * EXPERTS), ALU.mult, ALU.add))
                    step(v.tensor_tensor(pick[:, 0], pick[:, 0], pick[:, 1], ALU.add))
                    mark(v.tensor_copy(IDX[:, t, :], pick[:, 0]), "chosen")
                    gt = GATE[:, t, :].rearrange("p (h n) -> p h n", h=PHEADS)
                    mark(v.tensor_tensor(gt, BV, BV[:, :, 0:1].to_broadcast([P, PHEADS, TOPK]), ALU.subtract), "best")
                    after(dve, "gate_exp", a, (2, 2, 0, 2), t)
                    step(v.tensor_reduce(PHS[:, 0], gt, AX.X, ALU.add))
                    step(v.reciprocal(PHS[:, 0], PHS[:, 0]))
                    step(v.tensor_tensor(gt, gt, bc(PHS[:, 0], TOPK), ALU.mult))
                    beside(7)
                if a == 1:
                    back(a, "back", 0)
                tell(dve, "pass_over")
            serve(4, "")
            back(3, "back_last", 3)
            tell(dve, "h_done")
            rs = rsqrt("fin", 3, 0, T, 1.0 / D, 2048, 2304, 2560)
            for k in range(KD):
                ins = v.scalar_tensor_tensor(out=U[:, k, :], in0=H[:, 1, k, :], scalar=CVEC[:, 16 + k:17 + k],
                                             in1=rs, op0=ALU.mult, op1=ALU.mult)
                mark(ins, "u3") if k == KD - 1 else post(ins)


_INS = ["x", "c", "ctx", "c_ctx", "w_mod", "b_mod", "norm1_w", "w_in", "conv_a_w", "a_log", "dt_bias", "gdn_norm_w",
        "conv_b_w", "q_norm_w", "k_norm_w", "w_branch", "w_out", "norm2_w", "w_query", "sub_keys", "expert_u",
        "expert_v", "final_norm_w"]


def kernel(**inputs):
    import concourse.bacc as bacc
    from concourse.bass_utils import run_bass_kernel_spmd

    nc = bacc.Bacc("TRN2", target_bir_lowering=False, num_devices=1)
    arrays = {f"in_{n}": np.ascontiguousarray(inputs[n]) for n in _INS}
    arrays["in_constants"] = constant_table()
    inp = {n[3:]: nc.dram_tensor(n, v.shape, mybir.dt.from_np(v.dtype), kind="ExternalInput").ap()
           for n, v in arrays.items()}
    out = nc.dram_tensor("out_0", (1, T, D), F32, kind="ExternalOutput").ap()
    build(nc, inp, out)
    r = run_bass_kernel_spmd(nc, [arrays], core_ids=[0])
    return r.results[0]["out_0"]
```
